# Optimizing a Trainium2 kernel written in Bass

```python
import jax, jax.numpy as jnp
from jax import lax
import numpy as np

D_MODEL = 1024
BATCH = 1
SEQ = 1024
DEPTH = 1

HEAD_DIM = 64
N_Q_HEADS = 8
N_KV_HEADS = 2
GROUP = N_Q_HEADS // N_KV_HEADS
WINDOW = 128
BLOCK = 128
ATTN_WIDTH = N_Q_HEADS * HEAD_DIM
KV_WIDTH = N_KV_HEADS * HEAD_DIM
CONV_WIDTH_CH = 512
CONV_TAPS = 3
MIX_WIDTH = ATTN_WIDTH + CONV_WIDTH_CH
IN_WIDTH = ATTN_WIDTH + 2 * KV_WIDTH + 3 * CONV_WIDTH_CH
D_FF = 2816
EPS = 1e-6
NEG_INF = -1e30

kernel_name = "hybrid_swa_sink_shortconv_convffn"

def rms_norm(x, w):
    xf = x.astype(jnp.float32)
    y = xf * lax.rsqrt(jnp.mean(xf * xf, axis=-1, keepdims=True) + EPS)
    return (y * w.astype(jnp.float32)).astype(x.dtype)

def causal_dwconv3(x, w):
    s = x.shape[1]
    xp = jnp.pad(x, ((0, 0), (CONV_TAPS - 1, 0), (0, 0)))
    y = xp[:, 0:s] * w[0]
    for i in range(1, CONV_TAPS):
        y = y + xp[:, i:i + s] * w[i]
    return y

def sliding_window_attention(q, k, v, sinks):
    bsz, s = q.shape[0], q.shape[1]
    nb = s // BLOCK
    qb = q.reshape(bsz, nb, BLOCK, N_KV_HEADS, GROUP, HEAD_DIM)
    pad = ((0, 0), (BLOCK, 0), (0, 0), (0, 0))
    kp = jnp.pad(k, pad).reshape(bsz, nb + 1, BLOCK, N_KV_HEADS, HEAD_DIM)
    vp = jnp.pad(v, pad).reshape(bsz, nb + 1, BLOCK, N_KV_HEADS, HEAD_DIM)
    kw = jnp.concatenate([kp[:, :-1], kp[:, 1:]], axis=2)
    vw = jnp.concatenate([vp[:, :-1], vp[:, 1:]], axis=2)
    scale = HEAD_DIM ** -0.5
    sc = jnp.einsum('bnqkgd,bnskd->bnkgqs', qb, kw).astype(jnp.float32) * scale
    qi = jnp.arange(BLOCK)[:, None]
    sj = jnp.arange(2 * BLOCK)[None, :]
    rel = qi + BLOCK - sj
    band = (rel >= 0) & (rel < WINDOW)
    kpos = jnp.arange(nb)[:, None] * BLOCK - BLOCK + jnp.arange(2 * BLOCK)[None, :]
    mask = band[None, :, :] & (kpos >= 0)[:, None, :]
    sc = jnp.where(mask[None, :, None, None, :, :], sc, jnp.float32(NEG_INF))
    sink = sinks.astype(jnp.float32).reshape(N_KV_HEADS, GROUP)[None, None, :, :, None, None]
    m = jnp.maximum(jnp.max(sc, axis=-1, keepdims=True), sink)
    p = jnp.exp(sc - m)
    denom = jnp.sum(p, axis=-1, keepdims=True) + jnp.exp(sink - m)
    p = (p / denom).astype(v.dtype)
    o = jnp.einsum('bnkgqs,bnskd->bnqkgd', p, vw)
    return o.reshape(bsz, s, ATTN_WIDTH)

def setup_inputs(seed: int = 0) -> dict:
    key = jax.random.key(seed)
    ks = jax.random.split(key, 16)
    f = jnp.float32
    L = DEPTH
    def gain(k, n):
        return jnp.ones((L, n), f) + 0.05 * jax.random.normal(k, (L, n), f)
    return {
        "x": jax.random.normal(ks[0], (BATCH, SEQ, D_MODEL), f),
        "attn_norm_w": gain(ks[1], D_MODEL),
        "w_in": jax.random.normal(ks[2], (L, D_MODEL, IN_WIDTH), f) * D_MODEL ** -0.5,
        "q_norm_w": gain(ks[3], HEAD_DIM),
        "k_norm_w": gain(ks[4], HEAD_DIM),
        "sinks": 0.5 * jax.random.normal(ks[5], (L, N_Q_HEADS), f),
        "conv_mix_w": jax.random.normal(ks[6], (L, CONV_TAPS, CONV_WIDTH_CH), f) * CONV_TAPS ** -0.5,
        "attn_out_norm_w": gain(ks[7], ATTN_WIDTH),
        "conv_out_norm_w": gain(ks[8], CONV_WIDTH_CH),
        "w_out": jax.random.normal(ks[9], (L, MIX_WIDTH, D_MODEL), f) * MIX_WIDTH ** -0.5,
        "ffn_norm_w": gain(ks[10], D_MODEL),
        "w_up": jax.random.normal(ks[11], (L, D_MODEL, 2 * D_FF), f) * D_MODEL ** -0.5,
        "ffn_conv_w": jax.random.normal(ks[12], (L, CONV_TAPS, 2 * D_FF), f) * CONV_TAPS ** -0.5,
        "w_down": jax.random.normal(ks[13], (L, D_FF, D_MODEL), f) * D_FF ** -0.5,
    }

def reference(x, attn_norm_w, w_in, q_norm_w, k_norm_w, sinks, conv_mix_w,
              attn_out_norm_w, conv_out_norm_w, w_out, ffn_norm_w, w_up,
              ffn_conv_w, w_down):
    bsz, s = x.shape[0], x.shape[1]
    splits = [ATTN_WIDTH,
              ATTN_WIDTH + KV_WIDTH,
              ATTN_WIDTH + 2 * KV_WIDTH,
              ATTN_WIDTH + 2 * KV_WIDTH + CONV_WIDTH_CH,
              ATTN_WIDTH + 2 * KV_WIDTH + 2 * CONV_WIDTH_CH]
    for l in range(DEPTH):
        h = rms_norm(x, attn_norm_w[l])
        proj = jnp.einsum('bsd,de->bse', h, w_in[l])
        q, k, v, bg, cg, u = jnp.split(proj, splits, axis=-1)
        q = rms_norm(q.reshape(bsz, s, N_Q_HEADS, HEAD_DIM), q_norm_w[l])
        k = rms_norm(k.reshape(bsz, s, N_KV_HEADS, HEAD_DIM), k_norm_w[l])
        v = v.reshape(bsz, s, N_KV_HEADS, HEAD_DIM)
        attn = sliding_window_attention(q, k, v, sinks[l])
        conv = bg * causal_dwconv3(cg * u, conv_mix_w[l])
        mix = jnp.concatenate([rms_norm(attn, attn_out_norm_w[l]),
                               rms_norm(conv, conv_out_norm_w[l])], axis=-1)
        x = x + jnp.einsum('bse,ed->bsd', mix, w_out[l])
        h = rms_norm(x, ffn_norm_w[l])
        up = causal_dwconv3(jnp.einsum('bsd,df->bsf', h, w_up[l]), ffn_conv_w[l])
        g, uu = jnp.split(up, [D_FF], axis=-1)
        x = x + jnp.einsum('bsf,fd->bsd', jax.nn.silu(g) * uu, w_down[l])
    return x


_drawn_inputs = setup_inputs


def setup_inputs(seed=0):
    import zlib

    import numpy as np

    out = dict(_drawn_inputs(seed))
    spreads = {}
    factors = {'sinks': 8.0}
    for name, (base, spread) in spreads.items():
        noise = np.random.default_rng([zlib.crc32(name.encode()), seed]).standard_normal(out[name].shape)
        drawn = base * np.exp(spread * noise) if base else spread * noise
        out[name] = __import__('jax').numpy.asarray(drawn.astype(out[name].dtype))
    for name, factor in factors.items():
        out[name] = (out[name] * factor).astype(out[name].dtype)
    return out
```

```python
import concourse.bass as bass
from concourse import mybir
from contextlib import ExitStack

P = 128
FP32 = mybir.dt.float32
FP32R = mybir.dt.float32r
BF16 = mybir.dt.bfloat16
ALU = mybir.AluOpType
ACT = mybir.ActivationFunctionType
AX = mybir.AxisListType
ds = bass.ds


def build_layer(nc, x, attn_norm_w, w_in, q_norm_w, k_norm_w, sinks, conv_mix_w, attn_out_norm_w,
                conv_out_norm_w, w_out, ffn_norm_w, w_up, ffn_conv_w, w_down, out):
    D = x.shape[2]
    SEQ = x.shape[1]
    HD = q_norm_w.shape[1]
    NQ = sinks.shape[1]
    CW = conv_mix_w.shape[2]
    AW = NQ * HD
    NKV = (w_in.shape[2] - AW - 3 * CW) // (2 * HD)
    GROUP = NQ // NKV
    QKV = AW + 2 * NKV * HD
    FF = w_down.shape[1]
    TAPS = conv_mix_w.shape[1]
    KT = D // P
    NT = SEQ // P
    HALF = 512
    NH = SEQ // HALF
    NC = CW // P
    NF = FF // P
    NG = NF // 2
    EPS = 1e-6
    NEG = -1e30
    assert TAPS == 3 and HD == 64 and NT == 8 and KT == 8 and NH == 2 and NF % 2 == 0
    assert AW == HALF and CW == HALF and D == 2 * HALF and NC == 4

    x_t = x[0].rearrange("(t p) d -> t p d", p=P)
    out_t = out[0].rearrange("(t p) d -> t p d", p=P)
    w_qkv = w_in[0].rearrange("(k p) e -> k p e", p=P)
    w_in_v = w_in[0].rearrange("(k p) e -> p k e", p=P)
    w_up_v = w_up[0].rearrange("(k p) e -> p k e", p=P)
    w_out_v = w_out[0].rearrange("(k p) e -> k p e", p=P)
    w_down_v = w_down[0].rearrange("(f p) e -> f p e", p=P)

    ctx = ExitStack()
    with ctx:
        def sem(name):
            return ctx.enter_context(nc.semaphore(name))

        base = (nc.sbuf_base + 31) // 32 * 32
        SBUF_END = nc.sbuf_usable_end
        top = [base]

        def place(name, shape, dt, at=None):
            size = 2 if dt == BF16 else 4
            for n in shape[1:]:
                size *= n
            size = (size + 31) // 32 * 32
            if at is None:
                at = top[0]
                top[0] += size
            return nc.alloc_sbuf_tensor_at(name, shape, dt, offset=at), at + size

        ident, _ = place("ident", [P, P], FP32)
        ones, _ = place("ones", [P, 1], FP32)
        coef, _ = place("coef", [P, 2 * P], FP32)
        neghalf, _ = place("neghalf", [P, 16], FP32)
        eps, _ = place("eps", [P, 16], FP32)
        x_ss, _ = place("x_ss", [P, 2], FP32)
        x_r, _ = place("x_r", [P, 2], FP32)
        h_ss, _ = place("h_ss", [P, 2], FP32)
        h_r, _ = place("h_r", [P, 2], FP32)
        attn_ss, _ = place("attn_ss", [P, NT], FP32)
        attn_r, _ = place("attn_r", [P, NT], FP32)
        conv_ss, _ = place("conv_ss", [P, NT], FP32)
        conv_r, _ = place("conv_r", [P, NT], FP32)
        junk, _ = place("junk", [P, D], BF16)
        gain, _ = place("gain", [P, D], FP32)
        STG = 3
        stage = [place(f"stage{i}", [P, D], FP32)[0] for i in range(STG)]
        hT_hi, _ = place("hT_hi", [P, KT, SEQ], FP32R)
        hT_lo, _ = place("hT_lo", [P, KT, SEQ], FP32R)
        shared = top[0]
        wq_hi, a = place("wq_hi", [P, KT, QKV], FP32R, shared)
        wq_lo, a = place("wq_lo", [P, KT, QKV], FP32R, a)
        hb_hi, hb_lo = [None] * 2, [None] * 2
        for i in range(2):
            hb_hi[i], a = place(f"hb_hi{i}", [P, KT, P], FP32R, a)
            hb_lo[i], a = place(f"hb_lo{i}", [P, KT, P], FP32R, a)
        wo_hi, b = place("wo_hi", [P, KT, D], FP32R, shared)
        wo_lo, b = place("wo_lo", [P, KT, D], FP32R, b)
        region_v = max(a, b)
        wu_hi, wu_lo = [None] * 4, [None] * 4
        a = shared
        for i in range(4):
            wu_hi[i], a = place(f"wu_hi{i}", [P, KT, P], FP32R, a)
            wu_lo[i], a = place(f"wu_lo{i}", [P, KT, P], FP32R, a)
        wd_hi, a = place("wd_hi", [P, 2, D], FP32R, a)
        wd_lo, a = place("wd_lo", [P, 2, D], FP32R, a)
        act_hi, a = place("act_hi", [P, 2, SEQ], FP32R, a)
        act_lo, a = place("act_lo", [P, 2, SEQ], FP32R, a)
        assert a <= region_v
        wc_hi, wc_lo = [None] * 3, [None] * 3
        wc_hi[0], a = place("wc_hi0", [P, KT, P], FP32R, region_v)
        wc_lo[0], a = place("wc_lo0", [P, KT, P], FP32R, a)
        xin, xin_at = [None] * 2, a
        xin[0], a = place("xin0", [P, D], FP32, a)
        xin[1], a = place("xin1", [P, D], FP32, a)
        prob, a = place("prob", [P, NQ, 2 * P], FP32, a)
        probT, a = place("probT", [P, 2, 2, 2, P], FP32, a)
        qk, a = place("qk", [P, NQ + NKV, HD], FP32, a)
        qs, a = place("qs", [P, NQ, 2, HD], FP32, a)
        ks, a = place("ks", [P, NKV, 2, 2, HD], FP32, a)
        qT, a = place("qT", [P, NQ, P], FP32R, a)
        kT, a = place("kT", [P, NKV, 2, 2, P], FP32R, a)
        v_new, a = place("v_new", [P, NKV * HD], FP32, a)
        v_win, a = place("v_win", [P, 2, NKV * HD], FP32, a)
        attn, a = place("attn", [P, AW], FP32, a)
        attnT, a = place("attnT", [P, AW // P, P], FP32, a)
        qk_gain, a = place("qk_gain", [P, 2, HD], FP32, a)
        mask, a = place("mask", [P, 3 * P], FP32, a)
        sink, a = place("sink", [P, NQ], FP32, a)
        qk_ss, a = place("qk_ss", [P, NQ + NKV], FP32, a)
        qk_r, a = place("qk_r", [P, NQ + NKV], FP32, a)
        mx, a = place("mx", [P, NQ], FP32, a)
        top_score, a = place("top_score", [P, NQ], FP32, a)
        negm, a = place("negm", [P, NQ], FP32, a)
        sd, a = place("sd", [P, NQ], FP32, a)
        es, a = place("es", [P, NQ], FP32, a)
        den, a = place("den", [P, NQ], FP32, a)
        dsum, a = place("dsum", [P, NQ], FP32, a)
        rden, a = place("rden", [P, NQ], FP32, a)
        rows, a = place("rows", [P, 2 * P], FP32, a)
        assert a <= SBUF_END
        wc_hi[1], a = place("wc_hi1", [P, KT, P], FP32R, xin_at)
        wc_lo[1], a = place("wc_lo1", [P, KT, P], FP32R, a)
        wc_hi[2], a = place("wc_hi2", [P, KT, P], FP32R, a)
        wc_lo[2], a = place("wc_lo2", [P, KT, P], FP32R, a)
        c_sb, a = place("c_sb", [P, SEQ], FP32, a)
        cu, a = place("cu", [P, TAPS - 1 + SEQ], FP32, a)
        y, a = place("y", [P, SEQ], FP32, a)
        ysq, a = place("ysq", [P, SEQ], FP32, a)
        X, d = place("X", [P, NT, D], FP32, region_v)
        mix_hi, mix_lo = [None] * 2, [None] * 2
        mix_hi[1], e = place("mix_hi1", [P, KT, P], FP32R, d)
        mix_lo[1], e = place("mix_lo1", [P, KT, P], FP32R, e)
        mixb, a = place("mixb", [P, KT, P], FP32, max(a, e))
        mix_hi[0], a = place("mix_hi0", [P, KT, P], FP32R, a)
        mix_lo[0], a = place("mix_lo0", [P, KT, P], FP32R, a)
        xn, a = place("xn", [P, D], FP32, a)
        assert a <= SBUF_END
        gated, e = place("gated", [P, 2, SEQ], FP32, d)
        z, e = place("z", [P, TAPS - 1 + SEQ], FP32, e)
        acc_g, e = place("acc_g", [P, SEQ], FP32, e)
        acc_u, e = place("acc_u", [P, SEQ], FP32, e)
        assert e <= SBUF_END

        mix_dram = nc.dram_tensor("mix_dram", [KT, P, SEQ], FP32, kind="Internal").ap()

        bank = [ctx.enter_context(nc.psum_tensor(f"bank{i}", [P, HALF], FP32)) for i in range(8)]
        Q = bank[0:2]
        TR = bank[2:4]
        A = bank[4:8]

        const_in = sem("const_in")
        gain_in = sem("gain_in")
        const_set = sem("const_set")
        stage_in = [sem(f"stage_in{i}") for i in range(STG)]
        stage_hi = sem("stage_hi")
        stage_lo = sem("stage_lo")
        x_in = [sem(f"x_in{i}") for i in range(2)]
        tr_filled = sem("tr_filled")
        coef_out = sem("coef_out")
        coef_set = sem("coef_set")
        x_sq = sem("x_sq")
        x_rms = sem("x_rms")
        x_normed = sem("x_normed")
        h_hi = sem("h_hi")
        h_lo = sem("h_lo")
        h_kept = sem("h_kept")
        qkv_done = sem("qkv_done")
        qk_sq = sem("qk_sq")
        v_read = sem("v_read")
        v_slot = sem("v_slot")
        qk_sum = sem("qk_sum")
        qk_rms = sem("qk_rms")
        qk_normed = sem("qk_normed")
        qk_hi = sem("qk_hi")
        qk_lo = sem("qk_lo")
        qkT_out = sem("qkT_out")
        scores_done = sem("scores_done")
        masked = sem("masked")
        scores_seen = sem("scores_seen")
        shift = sem("shift")
        exps = sem("exps")
        denom = sem("denom")
        probT_out = sem("probT_out")
        pv_done = sem("pv_done")
        attn_out = sem("attn_out")
        attn_sq = sem("attn_sq")
        attnT_out = sem("attnT_out")
        mix_stored = sem("mix_stored")
        attn_rms = sem("attn_rms")
        unit_done = sem("unit_done")
        c_out = sem("c_out")
        cu_pad = sem("cu_pad")
        cu_out = sem("cu_out")
        y_chain = sem("y_chain")
        ysq_out = sem("ysq_out")
        y_stored = sem("y_stored")
        css_done = sem("css_done")
        css_sum = sem("css_sum")
        conv_rms = sem("conv_rms")
        X_in = sem("X_in")
        mixb_in = sem("mixb_in")
        mix_hi_out = sem("mix_hi_out")
        mix_lo_out = sem("mix_lo_out")
        proj_done = sem("proj_done")
        X_added = sem("X_added")
        h_sq = sem("h_sq")
        h_rms = sem("h_rms")
        h_normed = sem("h_normed")
        h2_hi = sem("h2_hi")
        h2_lo = sem("h2_lo")
        up_done = sem("up_done")
        z_pad = sem("z_pad")
        z_out = sem("z_out")
        conv_chain = sem("conv_chain")
        silu_out = sem("silu_out")
        gated_out = sem("gated_out")
        act_hi_out = sem("act_hi_out")
        act_lo_out = sem("act_lo_out")
        down_filled = sem("down_filled")
        down_added = sem("down_added")
        out_stored = sem("out_stored")

        block = ctx.enter_context(nc.Block())

        class Fill:

            def __init__(self, t, c):
                self.n = 10 * t + c
                self.bank = TR[c % 2]

        LAST = NT - 1

        def is_(t, *values):
            return isinstance(t, int) and t in values

        def x_fill(t, i):
            return Fill(0, 4 * t + i) if is_(t, 0, 1) else Fill(t - 1, -1 + i)

        def qk_fill(t, i):
            return Fill(t, (6 if is_(t, 0) else 3 if is_(t, LAST) else 5) + i)

        def prob_fill(t, i):
            if is_(t, LAST):
                return Fill(t, 7 + i)
            return Fill(t + 1, (-1 if is_(t, LAST - 1) else 1) + i)

        def attn_fill(t):
            return Fill(t, 11) if is_(t, LAST) else Fill(t + 1, 6 if is_(t, LAST - 1) else 8)

        class HFill:

            def __init__(self, t, i):
                self.n = 10 * LAST + 12 + 2 * t + i
                self.bank = TR[i]

        class Load:

            def __init__(self, c, i=0, step=0):
                self.n = step * i + c
                self.buf = stage[c % STG]
                self.sem = stage_in[c % STG]
                self.uses = (step // STG) * i + c // STG

        WO_STEP = 3
        N_UNIT0 = KT
        N_C = N_UNIT0 + 3
        N_F0 = N_C + 3 * (NC - 1) + KT
        N_F = N_F0 + 4

        def qkv_load(k):
            return Load(k)

        def unit0_load(s):
            return Load(N_UNIT0 + s)

        def unit_load(j, s):
            return Load(N_C + s, j, 3 + WO_STEP)

        def wo_load(j, m):
            return Load(N_C + 3 + m, j, 3 + WO_STEP)

        def wo_tiles(j):
            return KT - 2 * WO_STEP if is_(j, 2) else WO_STEP

        def up0_load(s):
            return Load(N_F0 + s)

        def up_load(i, s):
            return Load(N_F + s, i, 6)

        def down_load(i, k):
            return Load(N_F + 4 + k - (4 if is_(i, NG - 1) else 0), i, 6)

        def staged(ld, like):
            src = ld.buf[:, 0:like.free_size()]
            return src if len(like.shape) == 2 else src.rearrange("p (a b) -> p a b", b=like.shape[2])

        def split_hi(act, ld, hi, scale=1.0):
            act.wait_ge(ld.sem, 16 * (ld.uses + 1))
            act.activation(hi, staged(ld, hi), ACT.Copy, scale=scale).then_inc(stage_hi, 1)

        def split_lo(dve, ld, hi, lo, scale=1.0):
            dve.wait_ge(ld.sem, 16 * (ld.uses + 1))
            dve.wait_ge(stage_hi, ld.n + 1)
            if isinstance(scale, float):
                dve.tensor_tensor(lo, staged(ld, hi), hi.bitcast(FP32), ALU.subtract).then_inc(stage_lo, 1)
            else:
                dve.scalar_tensor_tensor(lo, staged(ld, hi), scale, hi.bitcast(FP32), ALU.mult,
                                         ALU.subtract).then_inc(stage_lo, 1)

        def ffn_tap(tap, f):
            return ds(tap * 2 * NF + f, 1)

        MIX0 = TAPS * 2 * NF

        def mix_tap(tap, j):
            return ds(MIX0 + tap * NC + j, 1)

        OUT0 = MIX0 + TAPS * NC

        @block.sync
        def _(sp):
            def load_x(t):
                if t >= 2:
                    sp.wait_ge(tr_filled, x_fill(t - 2, 1).n + 1)
                sp.dma_start(xin[t % 2][:, :], x_t[t]).then_inc(x_in[t % 2], 16)

            def load(ld, dst, src):
                if not (isinstance(ld.n, int) and ld.n < STG):
                    sp.wait_ge(stage_lo, ld.n - STG + 1)
                sp.dma_start(dst, src).then_inc(ld.sem, 16)

            def load_unit(ld, view, col):
                load(ld, ld.buf[:, :].rearrange("p (k e) -> p k e", e=P), view[:, :, ds(col, P)])

            def load_row(ld, view, row):
                load(ld, ld.buf[:, :], view[ds(row, 1)].rearrange("a p e -> (a p) e"))

            def conv_col(s):
                return QKV + (1, 2, 0)[s] * CW

            def up_col(s):
                return (s % 2) * FF + (s // 2) * P

            load_x(0)
            for k in range(KT):
                ld = qkv_load(k)
                load(ld, ld.buf[:, 0:QKV], w_qkv[k, :, 0:QKV])
                if k == 2:
                    load_x(1)
            load_x(2)
            load_x(3)
            for t in range(NT):
                if t + 4 < NT:
                    load_x(t + 4)
                elif t + 4 == NT:
                    for s in range(3):
                        load_unit(unit0_load(s), w_in_v, conv_col(s))
                sp.wait_ge(attnT_out, t + 1)
                sp.dma_start(mix_dram[0:AW // P, :, ds(P * t, P)].rearrange("k p t -> p k t"),
                             attnT[:, :, :]).then_inc(mix_stored, 16)

            def store_y(j):
                sp.wait_ge(y_chain, 5 * j + 5)
                sp.dma_start(mix_dram[ds(AW // P + j, 1)].rearrange("a p t -> (a p) t"),
                             y[:, :]).then_inc(y_stored, 16)

            def load_conv_weights(j):
                for s in range(3):
                    load_unit(unit_load(j, s), w_in_v, conv_col(s) + P * (j + 1))
                for m in range(wo_tiles(j)):
                    load_row(wo_load(j, m), w_out_v, WO_STEP * j + m)

            with sp.Fori(0, 2) as j:
                load_conv_weights(j)
                store_y(j)
            load_conv_weights(2)
            store_y(2)
            for s in range(3):
                load_unit(up0_load(s), w_up_v, up_col(s))

            for t in range(NT):
                if t < 6:
                    sp.wait_ge(unit_done, 3 * (NC - 1) + t // 2 + 1)
                else:
                    sp.wait_ge(y_chain, 5 * NC)
                sp.dma_start(X[:, t, :], x_t[t]).then_inc(X_in, 16)
            store_y(NC - 1)
            sp.wait_ge(mix_stored, 16 * NT)
            sp.wait_ge(y_stored, 16 * NC)

            def load_mix(t):
                sp.dma_start(mixb[:, :, :],
                             mix_dram[:, :, ds(P * t, P)].rearrange("k p t -> p k t")).then_inc(mixb_in, 16)

            load_mix(0)
            with sp.Fori(1, NT) as t:
                sp.wait_ge(mix_lo_out, t)
                load_mix(t)
            load_unit(up0_load(3), w_up_v, up_col(3))

            def load_down(i):
                for k in range(2):
                    load_row(down_load(i, k), w_down_v, 2 * i + k)

            def load_up(i):
                for s in range(4):
                    load_unit(up_load(i, s), w_up_v, up_col(s) + 2 * P * (i + 1))

            load_up(0)
            with sp.Fori(1, NG - 1) as i:
                load_down(i - 1)
                load_up(i)
            load_down(NG - 2)
            load_down(NG - 1)
            with sp.Fori(0, NT) as t:
                sp.wait_ge(down_added, 2 * NT * (NG - 1) + 2 * t + 2)
                sp.dma_start(out_t[ds(t, 1)].rearrange("a p d -> (a p) d"),
                             X[:, ds(t, 1), :].rearrange("p a d -> p (a d)")).then_inc(out_stored, 16)
            sp.wait_ge(out_stored, 16 * NT)

        @block.gpsimd
        def _(pool):
            pool.memset(neghalf[:, :], -0.5).then_inc(const_set, 1)
            pool.memset(eps[:, :], EPS).then_inc(const_set, 1)
            pool.memset(ones[:, :], 1.0).then_inc(const_set, 1)
            pool.memset(ident[:, :], 0.0).then_inc(const_set, 1)
            pool.memset(mask[:, :], 0.0).then_inc(const_set, 1)
            pool.memset(rows[:, :], 0.0).then_inc(const_set, 1)
            pool.wait_ge(const_set, 6)
            pool.affine_select(out=ident[:, :], in_=ident[:, :], compare_op=ALU.not_equal, fill=1.0,
                               base=0, pattern=[[-1, P]], channel_multiplier=1).then_inc(const_set, 1)
            for s in (0, 2):
                pool.affine_select(out=mask[:, s * P:(s + 1) * P], in_=mask[:, s * P:(s + 1) * P],
                                   compare_op=ALU.is_ge, fill=NEG, base=0, pattern=[[-1, P]],
                                   channel_multiplier=1).then_inc(const_set, 1)
            pool.affine_select(out=mask[:, P:2 * P], in_=mask[:, P:2 * P], compare_op=ALU.is_gt, fill=NEG,
                               base=0, pattern=[[1, P]], channel_multiplier=-1).then_inc(const_set, 1)

            def power(dst, mean, width, done, before):
                pool.tensor_tensor(dst, mean, eps[:, 0:width], ALU.add).then_inc(done, 1)
                pool.wait_ge(done, before + 1)
                pool.tensor_tensor(dst, dst, neghalf[:, 0:width], ALU.pow).then_inc(done, 1)

            def x_power(t, par):
                pool.wait_ge(x_sq, t + 1)
                if not is_(t, 0, 1):
                    pool.wait_ge(x_normed, t - 1)
                power(x_r[:, par:par + 1], x_ss[:, par:par + 1], 1, x_rms, 2 * t)

            def h_power(t, par):
                pool.wait_ge(h_sq, t + 1)
                if not is_(t, 0, 1):
                    pool.wait_ge(h_normed, t - 1)
                power(h_r[:, par:par + 1], h_ss[:, par:par + 1], 1, h_rms, 2 * t)

            def qk_power(t):
                pool.wait_ge(qk_sum, t + 1)
                if not is_(t, 0):
                    pool.wait_ge(qk_normed, 4 * t - 2)
                power(qk_r[:, :], qk_ss[:, :], NQ + NKV, qk_rms, 2 * t)

            def keep_h(t, par):
                pool.wait_ge(h_lo, 2 * t + 2)
                pool.tensor_copy(hT_hi[:, :, ds(P * t, P)], hb_hi[par][:, :, :]).then_inc(h_kept, 1)
                pool.tensor_copy(hT_lo[:, :, ds(P * t, P)], hb_lo[par][:, :, :]).then_inc(h_kept, 1)

            def step(t, par):
                x_power(t + 1, 1 - par)
                qk_power(t)
                keep_h(t + 1, 1 - par)

            x_power(0, 0)
            keep_h(0, 0)
            step(0, 0)
            step(1, 1)
            step(2, 0)
            with pool.Fori(0, 2) as tt:
                step(2 * tt + 3, 1)
                step(2 * tt + 4, 0)
            qk_power(LAST)
            pool.wait_ge(attn_sq, NT)
            pool.tensor_scalar(attn_ss[:, :], attn_ss[:, :], 1.0 / AW, None, ALU.mult).then_inc(attn_rms, 1)
            pool.wait_ge(attn_rms, 1)
            power(attn_r[:, :], attn_ss[:, :], NT, attn_rms, 1)
            pool.wait_ge(css_sum, NC)
            pool.tensor_scalar(conv_ss[:, :], conv_ss[:, :], 1.0 / CW, None, ALU.mult).then_inc(conv_rms, 1)
            pool.wait_ge(conv_rms, 1)
            power(conv_r[:, :], conv_ss[:, :], NT, conv_rms, 1)
            h_power(0, 0)
            h_power(1, 1)
            with pool.Fori(1, NT // 2) as tt:
                h_power(2 * tt, 0)
                h_power(2 * tt + 1, 1)

        @block.scalar
        def _(act):
            act.dma_start(gain[:, :], attn_norm_w.to_broadcast([P, D])).then_inc(gain_in, 16)
            act.dma_start(qk_gain[:, 0, :], q_norm_w.to_broadcast([P, HD])).then_inc(const_in, 16)
            act.dma_start(qk_gain[:, 1, :], k_norm_w.to_broadcast([P, HD])).then_inc(const_in, 16)
            act.dma_start(sink[:, :], sinks.to_broadcast([P, NQ])).then_inc(const_in, 16)
            act.wait_ge(const_set, 6)
            fcw = ffn_conv_w[0].rearrange("t (f p) -> (t f) p", p=P)
            R = TAPS * 2 * NF - P
            act.dma_start(rows[:, 0:P], fcw[0:P, :]).then_inc(const_in, 16)
            act.dma_start(rows[0:R, P:2 * P], fcw[P:P + R, :]).then_inc(const_in, 16)
            act.dma_start(rows[R:R + TAPS * NC, P:2 * P],
                          conv_mix_w[0].rearrange("t (f p) -> (t f) p", p=P)).then_inc(const_in, 16)
            R += TAPS * NC
            act.dma_start(rows[R:R + 4, P:2 * P],
                          attn_out_norm_w[0].rearrange("(f p) -> f p", p=P)).then_inc(const_in, 16)
            act.dma_start(rows[R + 4:R + 8, P:2 * P],
                          conv_out_norm_w[0].rearrange("(f p) -> f p", p=P)).then_inc(const_in, 16)

            def square_sum(src, width, total, done, scale=1.0):
                act.activation(junk[:, 0:width], src, ACT.Square, scale=scale, accum_out=total).then_inc(done, 1)

            def x_square(t, par, uses):
                act.wait_ge(x_in[par], 16 * uses + 16)
                if not is_(t, 0):
                    act.wait_ge(x_sq, t)
                if not is_(t, 0, 1, 2):
                    act.wait_ge(attn_sq, t - 2)
                if not is_(t, 0, 1):
                    act.wait_ge(x_rms, 2 * t - 2)
                square_sum(xin[par][:, :], D, x_ss[:, par:par + 1], x_sq, float(D) ** -0.5)

            def h_split_hi(t, par):
                for i in range(2):
                    f = x_fill(t, i)
                    act.wait_ge(tr_filled, f.n + 1)
                    if not is_(t, 0, 1):
                        act.wait_ge(qkv_done, t - 1)
                        act.wait_ge(h_kept, 2 * t - 2)
                    act.activation(hb_hi[par][:, 4 * i:4 * i + 4, :],
                                   f.bank[:, :].rearrange("p (k t) -> p k t", t=P), ACT.Copy).then_inc(h_hi, 1)

            def qkv_read(t):
                act.wait_ge(qkv_done, t + 1)
                if not is_(t, 0):
                    act.wait_ge(qk_lo, 3 * t)
                    act.wait_ge(v_slot, t)
                act.activation(qk[:, NQ:, :], Q[1][:, 0:NKV * HD].rearrange("p (h d) -> p h d", d=HD),
                               ACT.Square, scale=float(HD) ** -0.5).then_inc(qk_sq, 1)
                act.activation(v_new[:, :], Q[1][:, NKV * HD:2 * NKV * HD], ACT.Copy).then_inc(v_read, 1)
                act.activation(qk[:, 0:NQ, :], Q[0][:, :].rearrange("p (h d) -> p h d", d=HD),
                               ACT.Square, scale=float(HD) ** -0.5).then_inc(qk_sq, 1)

            def qk_split_hi(t):
                act.wait_ge(qk_normed, 4 * t + 4)
                if not is_(t, 0):
                    act.wait_ge(tr_filled, qk_fill(t - 1, 2).n + 1)
                act.activation(qs[:, :, 0, :].bitcast(FP32R), qk[:, 0:NQ, :], ACT.Copy).then_inc(qk_hi, 1)
                for r in range(2):
                    act.activation(ks[:, :, 0, r, :].bitcast(FP32R), qk[:, NQ:, :], ACT.Copy).then_inc(qk_hi, 1)

            def qkT_copy(t, par):
                for i in range(3):
                    f = qk_fill(t, i)
                    act.wait_ge(tr_filled, f.n + 1)
                    if not is_(t, 0):
                        act.wait_ge(scores_done, 2 * t)
                    if i < 2:
                        act.activation(qT[:, 4 * i:4 * i + 4, :],
                                       f.bank[:, :].rearrange("p (h t) -> p h t", t=P), ACT.Copy).then_inc(qkT_out, 1)
                    else:
                        act.activation(kT[:, :, :, par, :],
                                       f.bank[:, :].rearrange("p (h s t) -> p h s t", h=NKV, t=P),
                                       ACT.Copy).then_inc(qkT_out, 1)

            def v_place(t, par):
                act.wait_ge(v_read, t + 1)
                if not is_(t, 0):
                    act.wait_ge(pv_done, 4 * t)
                act.activation(v_win[:, par, :], v_new[:, :], ACT.Copy).then_inc(v_slot, 1)

            def softmax_exp(t, keys):
                for g in range(2):
                    act.wait_ge(shift, 6 * t + 3 * g + 3)
                    if not is_(t, 0):
                        act.wait_ge(denom, 2 * t)
                    for h in range(4 * g, 4 * g + 4):
                        act.activation(prob[:, h, 0:keys], prob[:, h, 0:keys], ACT.Exp,
                                       bias=negm[:, h:h + 1], accum_out=den[:, h:h + 1])
                    act.activation(es[:, 4 * g:4 * g + 4], sd[:, 4 * g:4 * g + 4], ACT.Exp).then_inc(exps, 1)

            def attn_square(t, x_squared):
                act.wait_ge(attn_out, t + 1)
                act.wait_ge(x_sq, x_squared)
                if not is_(t, 0):
                    act.wait_ge(attn_sq, t)
                square_sum(attn[:, :], AW, attn_ss[:, ds(t, 1)], attn_sq)

            def attnT_copy(t):
                f = attn_fill(t)
                act.wait_ge(tr_filled, f.n + 1)
                if not is_(t, 0):
                    act.wait_ge(mix_stored, 16 * t)
                act.activation(attnT[:, :, :], f.bank[:, :].rearrange("p (k t) -> p k t", t=P),
                               ACT.Copy).then_inc(attnT_out, 1)

            def step(t, par, x_uses, keys):
                if not is_(t, LAST):
                    x_square(t + 1, 1 - par, x_uses)
                if keys:
                    softmax_exp(t - 1, keys)
                qkv_read(t)
                if not is_(t, LAST):
                    h_split_hi(t + 1, 1 - par)
                qk_split_hi(t)
                qkT_copy(t, par)
                if is_(t, LAST):
                    act.wait_ge(tr_filled, x_fill(LAST, 1).n + 1)
                    for s in range(2):
                        split_hi(act, unit0_load(s), wc_hi[s][:, :, :])
                v_place(t, par)
                if keys:
                    attn_square(t - 1, NT if is_(t, LAST) else t + 2)
                    attnT_copy(t - 1)

            x_square(0, 0, 0)
            h_split_hi(0, 0)
            for k in range(KT):
                split_hi(act, qkv_load(k), wq_hi[:, k, :])
            step(0, 0, 0, 0)
            step(1, 1, 1, P)
            step(2, 0, 1, 2 * P)
            with act.Fori(0, 2) as tt:
                step(2 * tt + 3, 1, tt + 2, 2 * P)
                step(2 * tt + 4, 0, tt + 2, 2 * P)
            step(LAST, 1, 0, 2 * P)
            softmax_exp(LAST, 2 * P)
            attn_square(LAST, NT)
            attnT_copy(LAST)
            split_hi(act, unit0_load(2), wc_hi[2][:, :, :])

            def conv_iteration(j, last):
                for hf in range(NH):
                    act.wait_ge(unit_done, 3 * j + 1)
                    if not is_(j, 0):
                        act.wait_ge(cu_out, NH * j)
                    act.activation(c_sb[:, hf * HALF:(hf + 1) * HALF], Q[hf][:, :], ACT.Copy).then_inc(c_out, 1)
                if not last:
                    for s in range(3):
                        act.wait_ge(unit_done, 3 * j + s + 1)
                        split_hi(act, unit_load(j, s), wc_hi[s][:, :, :])
                    for m in range(wo_tiles(j)):
                        k = WO_STEP * j + m
                        split_hi(act, wo_load(j, m), wo_hi[:, ds(k, 1), :].rearrange("p a e -> p (a e)"),
                                 coef[:, ds(OUT0 + k, 1)])
                act.wait_ge(y_chain, 5 * j + 5)
                if not is_(j, 0):
                    act.wait_ge(css_done, j)
                act.activation(ysq[:, :], y[:, :], ACT.Square).then_inc(ysq_out, 1)

            act.wait_ge(coef_out, 2)
            act.wait_ge(mix_stored, 16 * NT)
            for j in range(3):
                conv_iteration(j, False)
            act.wait_ge(x_normed, NT)
            act.dma_start(gain[:, :], ffn_norm_w.to_broadcast([P, D])).then_inc(gain_in, 16)
            conv_iteration(3, True)

            def mix_split_hi(t, par):
                act.wait_ge(mixb_in, 16 * t + 16)
                if is_(t, 1):
                    act.wait_ge(css_sum, NC)
                elif not is_(t, 0):
                    act.wait_ge(proj_done, 2 * t - 2)
                act.activation(mix_hi[par][:, :, :], mixb[:, :, :], ACT.Copy).then_inc(mix_hi_out, 1)

            def h_square(t, par):
                act.wait_ge(X_added, 4 * t + 4)
                act.wait_ge(attn_sq, NT)
                if not is_(t, 0):
                    act.wait_ge(h_sq, t)
                if not is_(t, 0, 1):
                    act.wait_ge(h_rms, 2 * t - 2)
                square_sum(X[:, ds(t, 1), :].rearrange("p a d -> p (a d)"), D, h_ss[:, par:par + 1], h_sq, float(D) ** -0.5)

            def h2_split_hi(t):
                for i in range(2):
                    f = HFill(t, i)
                    act.wait_ge(tr_filled, f.n + 1)
                    act.activation(hT_hi[:, 4 * i:4 * i + 4, ds(P * t, P)],
                                   f.bank[:, :].rearrange("p (k t) -> p k t", t=P), ACT.Copy).then_inc(h2_hi, 1)

            def d_step(t, par):
                if not is_(t, 0):
                    h_square(t - 1, 1 - par)
                if not is_(t, LAST):
                    mix_split_hi(t + 1, 1 - par)
                if not is_(t, 0):
                    h2_split_hi(t - 1)

            mix_split_hi(0, 0)
            d_step(0, 0)
            d_step(1, 1)
            d_step(2, 0)
            with act.Fori(0, 2) as tt:
                d_step(2 * tt + 3, 1)
                d_step(2 * tt + 4, 0)
            d_step(LAST, 1)
            h_square(LAST, 1)
            act.wait_ge(proj_done, 2 * NT)
            for s in range(2):
                split_hi(act, up0_load(s), wu_hi[s][:, :, :])
            h2_split_hi(LAST)
            for s in range(2, 4):
                split_hi(act, up0_load(s), wu_hi[s][:, :, :])

            def down_operands_hi(i):
                if is_(i, 0):
                    act.wait_ge(proj_done, 2 * NT)
                else:
                    act.wait_ge(down_filled, 2 * NT * i)
                for k in range(2):
                    act.wait_ge(gated_out, 2 * i + k + 1)
                    act.activation(act_hi[:, k, :], gated[:, k, :], ACT.Copy).then_inc(act_hi_out, 1)
                for k in range(2):
                    split_hi(act, down_load(i, k), wd_hi[:, k, :])

            def up_weights_hi(i, s):
                act.wait_ge(up_done, 4 * i + s + 1)
                split_hi(act, up_load(i, s), wu_hi[s][:, :, :])

            def ffn_iteration(i, first, last):
                for s in range(4):
                    act.wait_ge(up_done, 4 * i + s + 1)
                    if not (first and s == 0):
                        act.wait_ge(conv_chain, 12 * i + 3 * s)
                    for hf in range(NH):
                        act.activation(z[:, TAPS - 1 + hf * HALF:TAPS - 1 + (hf + 1) * HALF],
                                       (Q, A)[s % 2][hf][:, :], ACT.Copy).then_inc(z_out, 1)
                    if s == 0 and not first:
                        down_operands_hi(i - 1)
                    if s >= 1 and not last:
                        up_weights_hi(i, s - 1)
                    if s % 2 == 0:
                        act.wait_ge(conv_chain, 12 * i + 3 * s + 3)
                        act.activation(acc_g[:, :], acc_g[:, :], ACT.Silu).then_inc(silu_out, 1)
                if not last:
                    up_weights_hi(i, 3)

            act.wait_ge(z_pad, 1)
            ffn_iteration(0, True, False)
            ffn_iteration(1, False, False)
            with act.Fori(2, NG - 1) as i:
                ffn_iteration(i, False, False)
            ffn_iteration(NG - 1, False, True)
            down_operands_hi(NG - 1)

        @block.tensor
        def _(pe):
            def x_transpose(t, par):
                pe.wait_ge(x_normed, t + 1)
                for i in range(2):
                    f = x_fill(t, i)
                    if is_(t, 1):
                        pe.wait_ge(coef_out, i + 1)
                    elif not is_(t, 0):
                        pe.wait_ge(qkT_out, 3 * t - 3)
                        if not is_(t, 2):
                            pe.wait_ge(attnT_out, t - 2)
                    for k in range(4):
                        mm = pe.transpose(f.bank[:, k * P:(k + 1) * P],
                                          xin[par][:, (4 * i + k) * P:(4 * i + k + 1) * P], ident[:, :])
                    mm.then_inc(tr_filled, 1)

            def qkv(t, par, first=False):
                pe.wait_ge(h_lo, 2 * t + 2)
                if not first:
                    pe.wait_ge(qk_normed, 4 * t - 2)
                    pe.wait_ge(v_read, t)
                for k in range(KT):
                    if first:
                        pe.wait_ge(stage_lo, qkv_load(k).n + 1)
                    for h, w, st in ((hb_hi, wq_hi, k == 0), (hb_hi, wq_lo, False), (hb_lo, wq_hi, False)):
                        end = k == KT - 1 and h is hb_lo
                        pe.matmul(Q[0][:, :], h[par][:, k, :], w[:, k, 0:AW], start=st, stop=end)
                        mm = pe.matmul(Q[1][:, 0:QKV - AW], h[par][:, k, :], w[:, k, AW:QKV], start=st, stop=end)
                mm.then_inc(qkv_done, 1)

            def attention_output(t, slots):
                def turn(f4):
                    f = prob_fill(t, f4)
                    pe.wait_ge(exps, 2 * t + f4 // 2 + 1)
                    if f4 >= 2:
                        pe.wait_ge(probT_out, 4 * t + f4 - 1)
                    elif is_(t, LAST - 1, LAST):
                        pe.wait_ge(qkT_out, 3 * t + 3)
                        pe.wait_ge(attnT_out, t)
                    else:
                        pe.wait_ge(h_lo, 2 * t + 5 + f4)
                    for h in range(2):
                        for s in slots:
                            mm = pe.transpose(f.bank[:, (2 * h + s) * P:(2 * h + s + 1) * P],
                                              prob[:, 2 * f4 + h, s * P:(s + 1) * P], ident[:, :])
                    mm.then_inc(tr_filled, 1)

                def values(f4):
                    pe.wait_ge(probT_out, 4 * t + f4 + 1)
                    for h in range(2 * f4, 2 * f4 + 2):
                        kv = h // GROUP
                        for s in slots:
                            mm = pe.matmul(A[3][:, h * HD:(h + 1) * HD], probT[:, f4 % 2, h % 2, s, :],
                                           v_win[:, s, kv * HD:(kv + 1) * HD],
                                           start=s == slots[0], stop=s == slots[-1])
                    mm.then_inc(pv_done, 1)

                pe.wait_ge(v_slot, t + 1)
                turn(0)
                turn(1)
                values(0)
                turn(2)
                values(1)
                turn(3)
                values(2)
                values(3)

            def scores(t, slots):
                pe.wait_ge(qk_lo, 3 * t + 3)
                pe.wait_ge(qk_hi, 3 * t + 3)
                for i in range(3):
                    f = qk_fill(t, i)
                    if i == 2:
                        pe.wait_ge(qkT_out, 3 * t + 1)
                    elif is_(t, 0):
                        pe.wait_ge(h_lo, 3 + i)
                    else:
                        pe.wait_ge(probT_out, 4 * t - 1 + i)
                    for n in range(4):
                        src = qs[:, 4 * i + n, :, :] if i < 2 else ks[:, n // 2, n % 2, :, :]
                        mm = pe.transpose(f.bank[:, n * P:(n + 1) * P], src.rearrange("p a d -> p (a d)"), ident[:, :])
                    mm.then_inc(tr_filled, 1)
                pe.wait_ge(qkT_out, 3 * t + 3)
                for g in range(2):
                    if not is_(t, 0):
                        pe.wait_ge(masked, 2 * t - 1 + g)
                        if g == 1:
                            pe.wait_ge(attn_out, t)
                    for h in range(4 * g, 4 * g + 4):
                        n = len(slots) * P
                        for part in range(2):
                            mm = pe.matmul(A[h // 2][:, (h % 2) * 2 * P:(h % 2) * 2 * P + n], qT[:, h, :],
                                           kT[:, h // GROUP, part, 0:len(slots), :].rearrange("p s t -> p (s t)"),
                                           start=part == 0, stop=part == 1)
                    mm.then_inc(scores_done, 1)

            def attn_transpose(t):
                f = attn_fill(t)
                pe.wait_ge(attn_out, t + 1)
                if is_(t, LAST):
                    pe.wait_ge(probT_out, 4 * t + 3)
                else:
                    pe.wait_ge(qkT_out, 3 * t + 5)
                for k in range(AW // P):
                    mm = pe.transpose(f.bank[:, k * P:(k + 1) * P], attn[:, k * P:(k + 1) * P], ident[:, :])
                mm.then_inc(tr_filled, 1)

            def step(t, par, slots_before):
                qkv(t, par, first=is_(t, 0))
                if not is_(t, LAST):
                    x_transpose(t + 1, 1 - par)
                if slots_before:
                    attention_output(t - 1, slots_before)
                scores(t, (0,) if is_(t, 0) else (0, 1))
                if slots_before:
                    attn_transpose(t - 1)

            pe.wait_ge(const_set, 7)
            x_transpose(0, 0)
            pe.wait_ge(const_in, 8 * 16)
            for i in range(2):
                pe.wait_ge(h_lo, i + 1)
                pe.transpose(TR[i][:, 0:P], rows[:, i * P:(i + 1) * P], ident[:, :]).then_inc(tr_filled, 1)
            step(0, 0, ())
            step(1, 1, (0,))
            step(2, 0, (0, 1))
            with pe.Fori(0, 2) as tt:
                step(2 * tt + 3, 1, (0, 1))
                step(2 * tt + 4, 0, (0, 1))
            step(LAST, 1, (0, 1))

            def unit(banks, hi, lo):
                for k in range(KT):
                    for w, h, st in ((hi, hT_hi, k == 0), (hi, hT_lo, False), (lo, hT_hi, False)):
                        for hf in range(NH):
                            mm = pe.matmul(banks[hf][:, :], w[:, k, :], h[:, k, hf * HALF:(hf + 1) * HALF],
                                           start=st, stop=k == KT - 1 and w is lo)
                return mm

            def conv_unit(j, s, first):
                if first:
                    pe.wait_ge(stage_lo, unit0_load(s).n + 1)
                else:
                    pe.wait_ge(stage_lo, unit_load(j - 1, s).n + 1)
                    pe.wait_ge((c_out, cu_out, y_chain)[s], (NH, NH, 5)[s] * j)
                unit((Q, A[0:2], A[2:4])[s], wc_hi[s], wc_lo[s]).then_inc(unit_done, 1)

            def conv_sums(j):
                pe.wait_ge(ysq_out, j + 1)
                if is_(j, 0):
                    pe.wait_ge(probT_out, 4 * NT)
                else:
                    pe.wait_ge(css_sum, j)
                for t in range(NT):
                    mm = pe.matmul(TR[0][:, t:t + 1], ysq[:, t * P:(t + 1) * P], ones[:, :], start=True, stop=True)
                mm.then_inc(css_done, 1)

            pe.wait_ge(h_kept, 2 * NT)
            pe.wait_ge(qk_normed, 4 * NT - 2)
            pe.wait_ge(v_read, NT)
            conv_unit(0, 0, True)
            attention_output(LAST, (0, 1))
            attn_transpose(LAST)
            pe.wait_ge(masked, 2 * NT)
            conv_unit(0, 1, True)
            conv_unit(0, 2, True)

            def conv_iteration(j):
                conv_unit(j, 0, False)
                conv_sums(j - 1)
                conv_unit(j, 1, False)
                conv_unit(j, 2, False)

            conv_iteration(1)
            with pe.Fori(2, NC) as j:
                conv_iteration(j)

            def project(t, par, part):
                if not is_(t, 0):
                    pe.wait_ge(X_added, 4 * t - 2 + 2 * part)
                elif part == 0:
                    pe.wait_ge(cu_out, NH * NC)
                else:
                    pe.wait_ge(y_chain, 5 * NC)
                banks = A[2 * part:2 * part + 2]
                for k in range(4 * part, 4 * part + 4):
                    for m, w, st in ((mix_hi, wo_hi, k % 4 == 0), (mix_hi, wo_lo, False), (mix_lo, wo_hi, False)):
                        for n in range(2):
                            mm = pe.matmul(banks[n][:, :], m[par][:, k, :], w[:, k, n * HALF:(n + 1) * HALF],
                                           start=st, stop=k % 4 == 3 and m is mix_lo)
                mm.then_inc(proj_done, 1)

            def h_transpose(t):
                pe.wait_ge(h_normed, t + 1)
                for i in range(2):
                    f = HFill(t, i)
                    if is_(t, 0):
                        pe.wait_ge((css_sum, attnT_out)[i], (NC, NT)[i])
                    else:
                        pe.wait_ge(h2_lo, 2 * t - 1 + i)
                    for k in range(4):
                        mm = pe.transpose(f.bank[:, k * P:(k + 1) * P], xn[:, (4 * i + k) * P:(4 * i + k + 1) * P],
                                          ident[:, :])
                    mm.then_inc(tr_filled, 1)

            def d_step(t, par):
                pe.wait_ge(mix_lo_out, t + 1)
                project(t, par, 0)
                if is_(t, 0):
                    conv_sums(NC - 1)
                else:
                    h_transpose(t - 1)
                project(t, par, 1)

            pe.wait_ge(stage_lo, N_F0)
            d_step(0, 0)
            d_step(1, 1)
            d_step(2, 0)
            with pe.Fori(0, 2) as tt:
                d_step(2 * tt + 3, 1)
                d_step(2 * tt + 4, 0)
            d_step(LAST, 1)
            h_transpose(LAST)

            def up_units(i, first):
                for s in range(4):
                    if first:
                        pe.wait_ge(stage_lo, up0_load(s).n + 1)
                    else:
                        pe.wait_ge(stage_lo, up_load(i - 1, s).n + 1)
                    if not (first and s < 2):
                        pe.wait_ge(z_out, 8 * i + 2 * s - 2)
                    unit((Q, A[0:2])[s % 2], wu_hi[s], wu_lo[s]).then_inc(up_done, 1)

            def down(i):
                ring = (TR[0], TR[1], A[2], A[3])
                pe.wait_ge(act_lo_out, 2 * i + 2)
                pe.wait_ge(stage_lo, down_load(i, 1).n + 1)
                for g in range(2 * NT):
                    t, n = g // 2, g % 2
                    if not (is_(i, 0) and g < 4):
                        pe.wait_ge(down_added, 2 * NT * i + g - 3)
                    for k in range(2):
                        for a, w in ((act_hi, wd_hi), (act_hi, wd_lo), (act_lo, wd_hi)):
                            mm = pe.matmul(ring[g % 4][:, :], a[:, k, t * P:(t + 1) * P],
                                           w[:, k, n * HALF:(n + 1) * HALF],
                                           start=k == 0 and a is act_hi and w is wd_hi,
                                           stop=k == 1 and a is act_lo)
                    mm.then_inc(down_filled, 1)

            pe.wait_ge(h2_lo, 2 * NT)
            pe.wait_ge(X_added, 4 * NT)
            up_units(0, True)
            up_units(1, False)
            down(0)
            with pe.Fori(2, NG - 1) as i:
                up_units(i, False)
                down(i - 1)
            up_units(NG - 1, False)
            down(NG - 2)
            down(NG - 1)

        @block.vector
        def _(dve):
            def x_norm(t, par):
                dve.wait_ge(x_rms, 2 * t + 2)
                dve.scalar_tensor_tensor(xin[par][:, :], xin[par][:, :], x_r[:, par:par + 1], gain[:, :],
                                         ALU.mult, ALU.mult).then_inc(x_normed, 1)

            def h_split_lo(t, par):
                for i in range(2):
                    f = x_fill(t, i)
                    dve.wait_ge(h_hi, 2 * t + i + 1)
                    dve.tensor_tensor(hb_lo[par][:, 4 * i:4 * i + 4, :],
                                      f.bank[:, :].rearrange("p (k t) -> p k t", t=P),
                                      hb_hi[par][:, 4 * i:4 * i + 4, :].bitcast(FP32), ALU.subtract).then_inc(h_lo, 1)

            def head_sums(t):
                dve.wait_ge(qk_sq, 2 * t + 2)
                dve.tensor_reduce(qk_ss[:, :], qk[:, :, :], AX.X, ALU.add).then_inc(qk_sum, 1)

            def qk_norm(t):
                dve.wait_ge(qk_rms, 2 * t + 2)
                dve.wait_ge(v_read, t + 1)
                for n, (lo, hi, src) in enumerate(((0, NQ, Q[0][:, :]), (NQ, NQ + NKV, Q[1][:, 0:NKV * HD]))):
                    dve.tensor_tensor(qk[:, lo:hi, :], src.rearrange("p (h d) -> p h d", d=HD),
                                      qk_r[:, lo:hi].unsqueeze(2).to_broadcast([P, hi - lo, HD]),
                                      ALU.mult).then_inc(qk_normed, 1)
                for n, (lo, hi) in enumerate(((0, NQ), (NQ, NQ + NKV))):
                    dve.wait_ge(qk_normed, 4 * t + n + 1)
                    dve.tensor_tensor(qk[:, lo:hi, :], qk[:, lo:hi, :],
                                      qk_gain[:, n:n + 1, :].to_broadcast([P, hi - lo, HD]),
                                      ALU.mult).then_inc(qk_normed, 1)

            def qk_split_lo(t):
                dve.wait_ge(qk_hi, 3 * t + 1)
                dve.tensor_tensor(qs[:, :, 1, :].bitcast(FP32R), qk[:, 0:NQ, :], qs[:, :, 0, :],
                                  ALU.subtract).then_inc(qk_lo, 1)
                dve.wait_ge(qk_hi, 3 * t + 2)
                for r in range(2):
                    dve.tensor_tensor(ks[:, :, 1, r, :].bitcast(FP32R), qk[:, NQ:, :], ks[:, :, 0, 0, :],
                                      ALU.subtract).then_inc(qk_lo, 1)

            def probT_copy(t, i, slots):
                f = prob_fill(t, i)
                dve.wait_ge(tr_filled, f.n + 1)
                if not (is_(t, 0) and i < 2):
                    dve.wait_ge(pv_done, 4 * t + i - 1)
                src = f.bank[:, :].rearrange("p (h s t) -> p h s t", h=2, t=P)
                n = len(slots)
                dve.tensor_copy(probT[:, i % 2, :, 0:n, :], src[:, :, 0:n, :]).then_inc(probT_out, 1)

            def denominators(t):
                dve.wait_ge(exps, 2 * t + 2)
                dve.tensor_tensor(dsum[:, :], den[:, :], es[:, :], ALU.add).then_inc(denom, 1)
                dve.wait_ge(denom, 2 * t + 1)
                dve.reciprocal(rden[:, :], dsum[:, :]).then_inc(denom, 1)

            def attn_scale(t):
                dve.wait_ge(pv_done, 4 * t + 4)
                dve.wait_ge(denom, 2 * t + 2)
                if not is_(t, 0):
                    dve.wait_ge(tr_filled, attn_fill(t - 1).n + 1)
                    dve.wait_ge(attn_sq, t)
                dve.tensor_tensor(attn[:, :].rearrange("p (h d) -> p h d", d=HD),
                                  A[3][:, :].rearrange("p (h d) -> p h d", d=HD),
                                  rden[:, :].unsqueeze(2).to_broadcast([P, NQ, HD]), ALU.mult).then_inc(attn_out, 1)

            def mask_max(t, par, keys):
                window = mask[:, par * P:par * P + keys]
                for g in range(2):
                    dve.wait_ge(scores_done, 2 * t + g + 1)
                    if not is_(t, 0):
                        dve.wait_ge(exps, 2 * t)
                    dve.sem_inc(scores_seen, 1)
                    for h in range(4 * g, 4 * g + 4):
                        mm = dve.tensor_tensor_reduce(out=prob[:, h, 0:keys],
                                                      in0=A[h // 2][:, (h % 2) * 2 * P:(h % 2) * 2 * P + keys],
                                                      in1=window, scale=1.0, scalar=-3e38, op0=ALU.add, op1=ALU.max,
                                                      accum_out=mx[:, h:h + 1])
                    mm.then_inc(masked, 1)
                    cols = slice(4 * g, 4 * g + 4)
                    dve.wait_ge(masked, 2 * t + g + 1)
                    dve.tensor_tensor(top_score[:, cols], mx[:, cols], sink[:, cols], ALU.max).then_inc(shift, 1)
                    dve.wait_ge(shift, 6 * t + 3 * g + 1)
                    dve.tensor_scalar(negm[:, cols], top_score[:, cols], -1.0, None, ALU.mult).then_inc(shift, 1)
                    dve.tensor_tensor(sd[:, cols], sink[:, cols], top_score[:, cols], ALU.subtract).then_inc(shift, 1)

            def step(t, par, slots_before):
                if not is_(t, LAST):
                    x_norm(t + 1, 1 - par)
                if slots_before:
                    denominators(t - 1)
                head_sums(t)
                if not is_(t, LAST):
                    h_split_lo(t + 1, 1 - par)
                qk_norm(t)
                if slots_before:
                    probT_copy(t - 1, 0, slots_before)
                    probT_copy(t - 1, 1, slots_before)
                qk_split_lo(t)
                if slots_before:
                    probT_copy(t - 1, 2, slots_before)
                    probT_copy(t - 1, 3, slots_before)
                    attn_scale(t - 1)
                if is_(t, LAST):
                    for s in range(2):
                        split_lo(dve, unit0_load(s), wc_hi[s][:, :, :], wc_lo[s][:, :, :])
                mask_max(t, par, P if is_(t, 0) else 2 * P)

            dve.wait_ge(gain_in, 16)
            x_norm(0, 0)
            h_split_lo(0, 0)
            dve.wait_ge(const_in, 8 * 16)
            dve.tensor_scalar(qk_gain[:, 0, :], qk_gain[:, 0, :], float(HD) ** -0.5, None, ALU.mult).then_inc(coef_set, 1)
            for i in range(2):
                dve.wait_ge(tr_filled, 3 + i)
                dve.tensor_copy(coef[:, i * P:(i + 1) * P], TR[i][:, 0:P]).then_inc(coef_out, 1)
            for k in range(KT):
                split_lo(dve, qkv_load(k), wq_hi[:, k, :], wq_lo[:, k, :])
            dve.wait_ge(coef_set, 1)
            dve.wait_ge(const_set, 10)
            step(0, 0, ())
            step(1, 1, (0,))
            step(2, 0, (0, 1))
            with dve.Fori(0, 2) as tt:
                step(2 * tt + 3, 1, (0, 1))
                step(2 * tt + 4, 0, (0, 1))
            step(LAST, 1, (0, 1))
            denominators(LAST)
            for i in range(4):
                probT_copy(LAST, i, (0, 1))
            attn_scale(LAST)
            split_lo(dve, unit0_load(2), wc_hi[2][:, :, :], wc_lo[2][:, :, :])

            def causal_conv(acc, src, taps, chain, count, before=()):
                for sem_, value in before:
                    dve.wait_ge(sem_, value)
                dve.tensor_scalar(acc[:, :], src[:, 2:2 + SEQ], coef[:, taps[2]], None, ALU.mult).then_inc(chain, 1)
                for n in (1, 2):
                    dve.wait_ge(chain, count + n)
                    dve.scalar_tensor_tensor(acc[:, :], src[:, 2 - n:2 - n + SEQ], coef[:, taps[2 - n]], acc[:, :],
                                             ALU.mult, ALU.add).then_inc(chain, 1)

            def conv_iteration(j, last):
                if not last:
                    split_lo(dve, unit_load(j, 0), wc_hi[0][:, :, :], wc_lo[0][:, :, :])
                dve.wait_ge(unit_done, 3 * j + 2)
                if not is_(j, 0):
                    dve.wait_ge(y_chain, 5 * j)
                for hf in range(NH):
                    dve.wait_ge(c_out, NH * j + hf + 1)
                    dve.tensor_tensor(cu[:, TAPS - 1 + hf * HALF:TAPS - 1 + (hf + 1) * HALF], A[hf][:, :],
                                      c_sb[:, hf * HALF:(hf + 1) * HALF], ALU.mult).then_inc(cu_out, 1)
                dve.wait_ge(cu_out, NH * j + NH)
                before = () if is_(j, 0) else ((y_stored, 16 * j), (ysq_out, j))
                causal_conv(y, cu, [mix_tap(n, j) for n in range(TAPS)], y_chain, 5 * j, before)
                if not last:
                    split_lo(dve, unit_load(j, 1), wc_hi[1][:, :, :], wc_lo[1][:, :, :])
                dve.wait_ge(unit_done, 3 * j + 3)
                dve.wait_ge(y_chain, 5 * j + 3)
                for hf in range(NH):
                    half = slice(hf * HALF, (hf + 1) * HALF)
                    dve.tensor_tensor(y[:, half], A[2 + hf][:, :], y[:, half], ALU.mult).then_inc(y_chain, 1)
                if not last:
                    split_lo(dve, unit_load(j, 2), wc_hi[2][:, :, :], wc_lo[2][:, :, :])
                    for m in range(wo_tiles(j)):
                        k = WO_STEP * j + m
                        split_lo(dve, wo_load(j, m), wo_hi[:, ds(k, 1), :].rearrange("p a e -> p (a e)"),
                                 wo_lo[:, ds(k, 1), :].rearrange("p a e -> p (a e)"), coef[:, ds(OUT0 + k, 1)])

            def conv_sums(j):
                dve.wait_ge(css_done, j + 1)
                if is_(j, 0):
                    dve.tensor_copy(conv_ss[:, :], TR[0][:, 0:NT]).then_inc(css_sum, 1)
                else:
                    dve.wait_ge(css_sum, j)
                    dve.tensor_tensor(conv_ss[:, :], TR[0][:, 0:NT], conv_ss[:, :], ALU.add).then_inc(css_sum, 1)

            dve.wait_ge(mix_stored, 16 * NT)
            dve.memset(cu[:, 0:TAPS - 1], 0.0).then_inc(cu_pad, 1)
            dve.wait_ge(cu_pad, 1)
            conv_iteration(0, False)
            conv_sums(0)
            conv_iteration(1, False)
            conv_sums(1)
            conv_iteration(2, False)
            conv_sums(2)
            conv_iteration(3, True)

            def mix_split_lo(t, par):
                dve.wait_ge(mix_hi_out, t + 1)
                dve.tensor_tensor(mix_lo[par][:, :, :], mixb[:, :, :], mix_hi[par][:, :, :].bitcast(FP32),
                                  ALU.subtract).then_inc(mix_lo_out, 1)

            def add_part(t, part):
                dve.wait_ge(proj_done, 2 * t + part + 1)
                r = (attn_r, conv_r)[part]
                if part == 0:
                    dve.wait_ge(X_in, 16 * NT)
                    dve.wait_ge(attn_rms, 3)
                else:
                    dve.wait_ge(conv_rms, 3)
                    dve.wait_ge(X_added, 4 * t + 2)
                for n in range(2):
                    x_half = X[:, ds(t, 1), n * HALF:(n + 1) * HALF].rearrange("p a d -> p (a d)")
                    dve.scalar_tensor_tensor(x_half, A[2 * part + n][:, :], r[:, ds(t, 1)], x_half,
                                             ALU.mult, ALU.add).then_inc(X_added, 1)

            def h_norm(t, par):
                dve.wait_ge(h_rms, 2 * t + 2)
                if not is_(t, 0):
                    dve.wait_ge(tr_filled, HFill(t - 1, 1).n + 1)
                dve.scalar_tensor_tensor(xn[:, :], X[:, ds(t, 1), :].rearrange("p a d -> p (a d)"),
                                         h_r[:, par:par + 1], gain[:, :], ALU.mult, ALU.mult).then_inc(h_normed, 1)

            def h2_split_lo(t):
                for i in range(2):
                    f = HFill(t, i)
                    dve.wait_ge(h2_hi, 2 * t + i + 1)
                    dve.tensor_tensor(hT_lo[:, 4 * i:4 * i + 4, ds(P * t, P)],
                                      f.bank[:, :].rearrange("p (k t) -> p k t", t=P),
                                      hT_hi[:, 4 * i:4 * i + 4, ds(P * t, P)].bitcast(FP32),
                                      ALU.subtract).then_inc(h2_lo, 1)

            def d_step(t, par):
                h_norm(t - 1, 1 - par)
                if not is_(t, LAST):
                    mix_split_lo(t + 1, 1 - par)
                add_part(t, 0)
                h2_split_lo(t - 1)
                add_part(t, 1)

            mix_split_lo(0, 0)
            dve.wait_ge(gain_in, 32)
            conv_sums(NC - 1)
            mix_split_lo(1, 1)
            add_part(0, 0)
            add_part(0, 1)
            d_step(1, 1)
            d_step(2, 0)
            with dve.Fori(0, 2) as tt:
                d_step(2 * tt + 3, 1)
                d_step(2 * tt + 4, 0)
            d_step(LAST, 1)
            h_norm(LAST, 1)
            for s in range(2):
                split_lo(dve, up0_load(s), wu_hi[s][:, :, :], wu_lo[s][:, :, :])
            h2_split_lo(LAST)
            for s in range(2, 4):
                split_lo(dve, up0_load(s), wu_hi[s][:, :, :], wu_lo[s][:, :, :])

            def down_operands_lo(i):
                for k in range(2):
                    dve.wait_ge(act_hi_out, 2 * i + k + 1)
                    dve.tensor_tensor(act_lo[:, k, :], gated[:, k, :], act_hi[:, k, :].bitcast(FP32),
                                      ALU.subtract).then_inc(act_lo_out, 1)
                for k in range(2):
                    split_lo(dve, down_load(i, k), wd_hi[:, k, :], wd_lo[:, k, :])

            def up_weights_lo(i, s):
                split_lo(dve, up_load(i, s), wu_hi[s][:, :, :], wu_lo[s][:, :, :])

            def add_down(i, g):
                ring = (TR[0], TR[1], A[2], A[3])
                t, n = g // 2, g % 2
                x_half = X[:, t, n * HALF:(n + 1) * HALF]
                dve.wait_ge(down_filled, 2 * NT * i + g + 1)
                dve.tensor_tensor(x_half, ring[g % 4][:, :], x_half, ALU.add).then_inc(down_added, 1)

            def ffn_iteration(i, first, last):
                for s in range(4):
                    dve.wait_ge(z_out, 8 * i + 2 * s + 2)
                    before = () if first and s < 2 else ((gated_out, 2 * i + s // 2),)
                    f = 2 * i + s // 2 + (s % 2) * NF
                    causal_conv((acc_g, acc_u)[s % 2], z, [ffn_tap(n, f) for n in range(TAPS)], conv_chain,
                                12 * i + 3 * s, before)
                    if s == 0 and not first:
                        down_operands_lo(i - 1)
                    if s % 2 == 1:
                        k = s // 2
                        dve.wait_ge(silu_out, 2 * i + k + 1)
                        dve.wait_ge(conv_chain, 12 * i + 3 * s + 3)
                        if not first:
                            dve.wait_ge(act_lo_out, 2 * i)
                        dve.tensor_tensor(gated[:, k, :], acc_g[:, :], acc_u[:, :], ALU.mult).then_inc(gated_out, 1)
                    if s >= 1 and not last:
                        up_weights_lo(i, s - 1)
                for g in range(2 * NT if not first else 0):
                    add_down(i - 1, g)
                    if g == 3 and not last:
                        up_weights_lo(i, 3)
                if first:
                    up_weights_lo(i, 3)

            dve.wait_ge(tr_filled, HFill(LAST, 1).n + 1)
            dve.memset(z[:, 0:TAPS - 1], 0.0).then_inc(z_pad, 1)
            dve.wait_ge(z_pad, 1)
            ffn_iteration(0, True, False)
            ffn_iteration(1, False, False)
            with dve.Fori(2, NG - 1) as i:
                ffn_iteration(i, False, False)
            ffn_iteration(NG - 1, False, True)
            down_operands_lo(NG - 1)
            for g in range(2 * NT):
                add_down(NG - 1, g)


_INS = ["x", "attn_norm_w", "w_in", "q_norm_w", "k_norm_w", "sinks", "conv_mix_w", "attn_out_norm_w",
        "conv_out_norm_w", "w_out", "ffn_norm_w", "w_up", "ffn_conv_w", "w_down"]


def kernel(**inputs):
    import numpy as _np
    import concourse.bacc as _bacc
    from concourse import mybir as _mybir
    from concourse.bass_utils import run_bass_kernel_spmd as _run

    nc = _bacc.Bacc("TRN2", target_bir_lowering=False, num_devices=1)
    arrays, args = {}, []
    for name in _INS:
        a = _np.ascontiguousarray(inputs[name])
        arrays[f"in_{name}_dram"] = a
        args.append(nc.dram_tensor(f"in_{name}_dram", a.shape, _mybir.dt.from_np(a.dtype), kind="ExternalInput").ap())
    shape = tuple(inputs["x"].shape)
    args.append(nc.dram_tensor("out_0_dram", shape, _mybir.dt.float32, kind="ExternalOutput").ap())
    build_layer(nc, *args)
    r = _run(nc, [arrays], core_ids=[0])
    return r.results[0]["out_0_dram"]
```

```python
import concourse.bass as bass
from concourse import mybir
from contextlib import ExitStack

P = 128
FP32 = mybir.dt.float32
FP32R = mybir.dt.float32r
BF16 = mybir.dt.bfloat16
ALU = mybir.AluOpType
ACT = mybir.ActivationFunctionType
AX = mybir.AxisListType
ds = bass.ds


def build_layer(nc, x, attn_norm_w, w_in, q_norm_w, k_norm_w, sinks, conv_mix_w, attn_out_norm_w,
                conv_out_norm_w, w_out, ffn_norm_w, w_up, ffn_conv_w, w_down, out):
    D = x.shape[2]
    SEQ = x.shape[1]
    HD = q_norm_w.shape[1]
    NQ = sinks.shape[1]
    CW = conv_mix_w.shape[2]
    AW = NQ * HD
    NKV = (w_in.shape[2] - AW - 3 * CW) // (2 * HD)
    GROUP = NQ // NKV
    QKV = AW + 2 * NKV * HD
    FF = w_down.shape[1]
    TAPS = conv_mix_w.shape[1]
    KT = D // P
    NT = SEQ // P
    HALF = 512
    NH = SEQ // HALF
    NC = CW // P
    NF = FF // P
    NG = NF // 2
    EPS = 1e-6
    NEG = -1e30
    assert TAPS == 3 and HD == 64 and NT == 8 and KT == 8 and NH == 2 and NF % 2 == 0
    assert AW == HALF and CW == HALF and D == 2 * HALF and NC == 4

    x_t = x[0].rearrange("(t p) d -> t p d", p=P)
    out_t = out[0].rearrange("(t p) d -> t p d", p=P)
    w_qkv = w_in[0].rearrange("(k p) e -> k p e", p=P)
    w_in_v = w_in[0].rearrange("(k p) e -> p k e", p=P)
    w_up_v = w_up[0].rearrange("(k p) e -> p k e", p=P)
    w_out_v = w_out[0].rearrange("(k p) e -> k p e", p=P)
    w_down_v = w_down[0].rearrange("(f p) e -> f p e", p=P)

    ctx = ExitStack()
    with ctx:
        def sem(name):
            return ctx.enter_context(nc.semaphore(name))

        base = (nc.sbuf_base + 31) // 32 * 32
        SBUF_END = nc.sbuf_usable_end
        top = [base]

        def place(name, shape, dt, at=None):
            size = 2 if dt == BF16 else 4
            for n in shape[1:]:
                size *= n
            size = (size + 31) // 32 * 32
            if at is None:
                at = top[0]
                top[0] += size
            return nc.alloc_sbuf_tensor_at(name, shape, dt, offset=at), at + size

        ident, _ = place("ident", [P, P], FP32)
        ones, _ = place("ones", [P, 1], FP32)
        coef, _ = place("coef", [P, 2 * P], FP32)
        neghalf, _ = place("neghalf", [P, 16], FP32)
        eps, _ = place("eps", [P, 16], FP32)
        x_ss, _ = place("x_ss", [P, 2], FP32)
        x_r, _ = place("x_r", [P, 2], FP32)
        h_ss, _ = place("h_ss", [P, 2], FP32)
        h_r, _ = place("h_r", [P, 2], FP32)
        attn_ss, _ = place("attn_ss", [P, NT], FP32)
        attn_r, _ = place("attn_r", [P, NT], FP32)
        conv_ss, _ = place("conv_ss", [P, NT], FP32)
        conv_r, _ = place("conv_r", [P, NT], FP32)
        junk, _ = place("junk", [P, D], BF16)
        gain, _ = place("gain", [P, D], FP32)
        STG = 3
        stage = [place(f"stage{i}", [P, D], FP32)[0] for i in range(STG)]
        hT_hi, _ = place("hT_hi", [P, KT, SEQ], FP32R)
        hT_lo, _ = place("hT_lo", [P, KT, SEQ], FP32R)
        shared = top[0]
        wq_hi, a = place("wq_hi", [P, KT, QKV], FP32R, shared)
        wq_lo, a = place("wq_lo", [P, KT, QKV], FP32R, a)
        hb_hi, a = place("hb_hi", [P, KT, P], FP32R, a)
        hb_lo, a = place("hb_lo", [P, KT, P], FP32R, a)
        wo_hi, b = place("wo_hi", [P, KT, D], FP32R, shared)
        wo_lo, b = place("wo_lo", [P, KT, D], FP32R, b)
        region_v = max(a, b)
        wu_hi, wu_lo, wu_at = [None] * 4, [None] * 4, [None] * 4
        a = shared
        for i in range(4):
            wu_at[i] = a
            wu_hi[i], a = place(f"wu_hi{i}", [P, KT, P], FP32R, a)
            wu_lo[i], a = place(f"wu_lo{i}", [P, KT, P], FP32R, a)
        wd_hi, a = place("wd_hi", [P, 2, D], FP32R, a)
        wd_lo, a = place("wd_lo", [P, 2, D], FP32R, a)
        act_hi, a = place("act_hi", [P, 2, SEQ], FP32R, a)
        act_lo, a = place("act_lo", [P, 2, SEQ], FP32R, a)
        assert a <= region_v
        act_hi_last = [place(f"act_hi_last{k}", [P, SEQ], FP32R, wu_at[2 * k])[0] for k in range(2)]
        act_lo_last = [place(f"act_lo_last{k}", [P, SEQ], FP32R, wu_at[2 * k] + 4 * SEQ)[0] for k in range(2)]
        wd_hi_last = [place(f"wd_hi_last{k}", [P, D], FP32R, wu_at[2 * k + 1])[0] for k in range(2)]
        wd_lo_last = [place(f"wd_lo_last{k}", [P, D], FP32R, wu_at[2 * k + 1] + 4 * D)[0] for k in range(2)]
        wc_hi, wc_lo = [None] * 3, [None] * 3
        wc_hi[0], a = place("wc_hi0", [P, KT, P], FP32R, region_v)
        wc_lo[0], a = place("wc_lo0", [P, KT, P], FP32R, a)
        xin, xin_at = [None] * 2, a
        xin[0], a = place("xin0", [P, D], FP32, a)
        xin[1], a = place("xin1", [P, D], FP32, a)
        prob, a = place("prob", [P, NQ, 2 * P], FP32, a)
        probT, a = place("probT", [P, 4, GROUP * P], FP32, a)
        qk_sqr, a = place("qk_sqr", [P, NQ + NKV, HD], FP32, a)
        qn, a = place("qn", [P, GROUP + 1, P], FP32, a)
        qT_hi, a = place("qT_hi", [P, GROUP, P], FP32R, a)
        qT_lo, a = place("qT_lo", [P, GROUP, P], FP32R, a)
        kT_hi, a = place("kT_hi", [P, 2, P], FP32R, a)
        kT_lo, a = place("kT_lo", [P, 2, P], FP32R, a)
        v_new, a = place("v_new", [P, 2, NKV * HD], FP32, a)
        v_win, a = place("v_win", [P, 2, NKV * HD], FP32, a)
        attnT, a = place("attnT", [P, GROUP, P], FP32, a)
        attn_sqr, a = place("attn_sqr", [P, GROUP, P], FP32, a)
        qk_gain, a = place("qk_gain", [P, 2, HD], FP32, a)
        mask, a = place("mask", [P, 3 * P], FP32, a)
        sink, a = place("sink", [P, NQ], FP32, a)
        qk_ss, a = place("qk_ss", [P, NQ + NKV], FP32, a)
        qk_r, a = place("qk_r", [P, NQ + NKV], FP32, a)
        mx, a = place("mx", [P, NQ], FP32, a)
        top_score, a = place("top_score", [P, NQ], FP32, a)
        negm, a = place("negm", [P, NQ], FP32, a)
        sd, a = place("sd", [P, NQ], FP32, a)
        es, a = place("es", [P, NQ], FP32, a)
        den, a = place("den", [P, NQ], FP32, a)
        dsum, a = place("dsum", [P, NQ], FP32, a)
        rden, a = place("rden", [P, NQ], FP32, a)
        rows, a = place("rows", [P, 2 * P], FP32, a)
        assert a <= SBUF_END
        wc_hi[1], a = place("wc_hi1", [P, KT, P], FP32R, xin_at)
        wc_lo[1], a = place("wc_lo1", [P, KT, P], FP32R, a)
        wc_hi[2], a = place("wc_hi2", [P, KT, P], FP32R, a)
        wc_lo[2], a = place("wc_lo2", [P, KT, P], FP32R, a)
        c_sb, a = place("c_sb", [P, SEQ], FP32, a)
        cu, a = place("cu", [P, TAPS - 1 + SEQ], FP32, a)
        y, a = place("y", [P, SEQ], FP32, a)
        ysq, a = place("ysq", [P, SEQ], FP32, a)
        X, d = place("X", [P, NT, D], FP32, region_v)
        mix_hi, mix_lo = [None] * 2, [None] * 2
        mix_hi[1], e = place("mix_hi1", [P, KT, P], FP32R, d)
        mix_lo[1], e = place("mix_lo1", [P, KT, P], FP32R, e)
        mixb, a = place("mixb", [P, KT, P], FP32, max(a, e))
        mix_hi[0], a = place("mix_hi0", [P, KT, P], FP32R, a)
        mix_lo[0], a = place("mix_lo0", [P, KT, P], FP32R, a)
        xn, a = place("xn", [P, D], FP32, a)
        assert a <= SBUF_END
        gated, e = place("gated", [P, 2, SEQ], FP32, d)
        z, e = place("z", [P, TAPS - 1 + SEQ], FP32, e)
        acc_g, e = place("acc_g", [P, SEQ], FP32, e)
        acc_u, e = place("acc_u", [P, SEQ], FP32, e)
        assert e <= SBUF_END

        mix_dram = nc.dram_tensor("mix_dram", [KT, P, SEQ], FP32, kind="Internal").ap()

        bank = [ctx.enter_context(nc.psum_tensor(f"bank{i}", [P, HALF], FP32)) for i in range(8)]
        Q = bank[0:2]
        TR = bank[2:4]
        A = bank[4:8]

        const_in = sem("const_in")
        gain_in = sem("gain_in")
        const_set = sem("const_set")
        stage_in = [sem(f"stage_in{i}") for i in range(STG)]
        stage_hi = sem("stage_hi")
        stage_lo = sem("stage_lo")
        x_in = [sem(f"x_in{i}") for i in range(2)]
        x_turned = sem("x_turned")
        qk_turned = sem("qk_turned")
        prob_turned = sem("prob_turned")
        coef_turned = sem("coef_turned")
        h_turned = sem("h_turned")
        coef_out = sem("coef_out")
        coef_set = sem("coef_set")
        x_sq = sem("x_sq")
        x_rms = sem("x_rms")
        x_normed = sem("x_normed")
        h_hi = sem("h_hi")
        h_lo = sem("h_lo")
        h_kept = sem("h_kept")
        qkv_done = sem("qkv_done")
        qk_sq = sem("qk_sq")
        v_read = sem("v_read")
        v_slot = sem("v_slot")
        qk_sum = sem("qk_sum")
        qk_rms = sem("qk_rms")
        qk_normed = sem("qk_normed")
        qkT_hi_out = sem("qkT_hi_out")
        qkT_lo_out = sem("qkT_lo_out")
        scores_done = sem("scores_done")
        masked = sem("masked")
        scores_seen = sem("scores_seen")
        shift = sem("shift")
        exps = sem("exps")
        denom = sem("denom")
        prob_divided = sem("prob_divided")
        probT_out = sem("probT_out")
        pv_done = sem("pv_done")
        attn_sq = sem("attn_sq")
        attn_sums_done = sem("attn_sums_done")
        attn_sum_out = sem("attn_sum_out")
        attnT_out = sem("attnT_out")
        mix_stored = sem("mix_stored")
        attn_rms = sem("attn_rms")
        unit_done = sem("unit_done")
        c_out = sem("c_out")
        cu_pad = sem("cu_pad")
        cu_out = sem("cu_out")
        y_chain = sem("y_chain")
        ysq_out = sem("ysq_out")
        y_stored = sem("y_stored")
        css_done = sem("css_done")
        css_sum = sem("css_sum")
        conv_rms = sem("conv_rms")
        X_in = sem("X_in")
        X_late_in = sem("X_late_in")
        mixb_in = sem("mixb_in")
        mix_hi_out = sem("mix_hi_out")
        mix_lo_out = sem("mix_lo_out")
        proj_done = sem("proj_done")
        X_added = sem("X_added")
        h_sq = sem("h_sq")
        h_rms = sem("h_rms")
        h_normed = sem("h_normed")
        h2_hi = sem("h2_hi")
        h2_lo = sem("h2_lo")
        up_done = sem("up_done")
        z_pad = sem("z_pad")
        z_out = sem("z_out")
        conv_chain = sem("conv_chain")
        silu_out = sem("silu_out")
        gated_out = sem("gated_out")
        act_hi_out = sem("act_hi_out")
        act_lo_out = sem("act_lo_out")
        down_filled = sem("down_filled")
        down_added = sem("down_added")
        out_stored = sem("out_stored")

        block = ctx.enter_context(nc.Block())

        LAST = NT - 1

        def is_(t, *values):
            return isinstance(t, int) and t in values

        def from_(t, first):
            return not isinstance(t, int) or t >= first

        def prob_fill(b, f):
            return 4 * b + f - 1

        class Load:

            def __init__(self, c, i=0, step=0):
                self.n = step * i + c
                self.buf = stage[c % STG]
                self.sem = stage_in[c % STG]
                self.uses = (step // STG) * i + c // STG

        WO_STEP = 3
        N_UNIT0 = KT
        N_C = N_UNIT0 + 3
        N_F0 = N_C + 3 * (NC - 1) + KT
        N_F = N_F0 + 4

        def qkv_load(k):
            return Load(k)

        def unit0_load(s):
            return Load(N_UNIT0 + s)

        def unit_load(j, s):
            return Load(N_C + s, j, 3 + WO_STEP)

        def wo_load(j, m):
            return Load(N_C + 3 + m, j, 3 + WO_STEP)

        def wo_tiles(j):
            return KT - 2 * WO_STEP if is_(j, 2) else WO_STEP

        def up0_load(s):
            return Load(N_F0 + s)

        def up_load(i, s):
            return Load(N_F + s, i, 6)

        def down_load(i, k):
            return Load(N_F + 4 + k - (4 if is_(i, NG - 1) else 0), i, 6)

        def staged(ld, like):
            src = ld.buf[:, 0:like.free_size()]
            return src if len(like.shape) == 2 else src.rearrange("p (a b) -> p a b", b=like.shape[2])

        def split_hi(act, ld, hi, scale=1.0):
            act.wait_ge(ld.sem, 16 * (ld.uses + 1))
            act.activation(hi, staged(ld, hi), ACT.Copy, scale=scale).then_inc(stage_hi, 1)

        def split_lo(dve, ld, hi, lo, scale=1.0):
            dve.wait_ge(ld.sem, 16 * (ld.uses + 1))
            dve.wait_ge(stage_hi, ld.n + 1)
            if isinstance(scale, float):
                dve.tensor_tensor(lo, staged(ld, hi), hi.bitcast(FP32), ALU.subtract).then_inc(stage_lo, 1)
            else:
                dve.scalar_tensor_tensor(lo, staged(ld, hi), scale, hi.bitcast(FP32), ALU.mult,
                                         ALU.subtract).then_inc(stage_lo, 1)

        def down_operands(i):
            if is_(i, NG - 1):
                return tuple([t_[k][:, :] for k in range(2)]
                             for t_ in (act_hi_last, act_lo_last, wd_hi_last, wd_lo_last))
            return tuple([t_[:, k, :] for k in range(2)] for t_ in (act_hi, act_lo, wd_hi, wd_lo))

        def ffn_tap(tap, f):
            return ds(tap * 2 * NF + f, 1)

        MIX0 = TAPS * 2 * NF

        def mix_tap(tap, j):
            return ds(MIX0 + tap * NC + j, 1)

        OUT0 = MIX0 + TAPS * NC

        @block.sync
        def _(sp):
            def load_x(t):
                if t >= 2:
                    sp.wait_ge(x_turned, 2 * t - 2)
                sp.dma_start(xin[t % 2][:, :], x_t[t]).then_inc(x_in[t % 2], 16)

            def load(ld, dst, src):
                if not (isinstance(ld.n, int) and ld.n < STG):
                    sp.wait_ge(stage_lo, ld.n - STG + 1)
                sp.dma_start(dst, src).then_inc(ld.sem, 16)

            def load_unit(ld, view, col):
                load(ld, ld.buf[:, :].rearrange("p (k e) -> p k e", e=P), view[:, :, ds(col, P)])

            def load_row(ld, view, row):
                load(ld, ld.buf[:, :], view[ds(row, 1)].rearrange("a p e -> (a p) e"))

            def conv_col(s):
                return QKV + (1, 2, 0)[s] * CW

            def up_col(s):
                return (s % 2) * FF + (s // 2) * P

            load_x(0)
            for k in range(KT):
                ld = qkv_load(k)
                load(ld, ld.buf[:, 0:QKV], w_qkv[k, :, 0:QKV])
                if k == 2:
                    load_x(1)
            def keep_h():
                sp.wait_ge(h_lo, 2 * t + 2)
                sp.dma_start(hT_hi[:, :, ds(P * t, P)].bitcast(FP32),
                             hb_hi[:, :, :].bitcast(FP32)).then_inc(h_kept, 16)
                sp.dma_start(hT_lo[:, :, ds(P * t, P)].bitcast(FP32),
                             hb_lo[:, :, :].bitcast(FP32)).then_inc(h_kept, 16)

            mix_heads = mix_dram[0:AW // P].rearrange("k (a d) t -> d (k a) t", d=HD)

            def store_attn(b):
                sp.wait_ge(attnT_out, b + 1)
                for kv in range(NKV):
                    sp.dma_start(mix_heads[:, GROUP * kv:GROUP * (kv + 1), P * b:P * (b + 1)],
                                 attnT[HD * kv:HD * (kv + 1), :, :]).then_inc(mix_stored, 16)

            for t in range(NT):
                keep_h()
                if t + 2 < NT:
                    load_x(t + 2)
                if t == LAST - 2:
                    for s in range(3):
                        load_unit(unit0_load(s), w_in_v, conv_col(s))
                if t >= 3:
                    store_attn(t - 3)
            for b in range(LAST - 2, NT):
                store_attn(b)

            def store_y(j):
                sp.wait_ge(y_chain, 5 * j + 5)
                sp.dma_start(mix_dram[ds(AW // P + j, 1)].rearrange("a p t -> (a p) t"),
                             y[:, :]).then_inc(y_stored, 16)

            def load_conv_weights(j):
                for s in range(3):
                    load_unit(unit_load(j, s), w_in_v, conv_col(s) + P * (j + 1))
                for m in range(wo_tiles(j)):
                    load_row(wo_load(j, m), w_out_v, WO_STEP * j + m)

            with sp.Fori(0, 2) as j:
                load_conv_weights(j)
                store_y(j)
            load_conv_weights(2)
            store_y(2)
            for s in range(3):
                load_unit(up0_load(s), w_up_v, up_col(s))

            def load_mix(t, tiles):
                sp.dma_start(mixb[:, 0:tiles, :], mix_dram[0:tiles, :, ds(P * t, P)].rearrange(
                    "k p t -> p k t")).then_inc(mixb_in, 16)

            sp.wait_ge(mix_stored, 32 * NT)
            sp.wait_ge(y_stored, 16 * (NC - 1))
            load_mix(0, KT - 1)
            for t in range(6):
                sp.wait_ge(unit_done, 3 * (NC - 1) + t // 2 + 1)
                sp.dma_start(X[:, t, :], x_t[t]).then_inc(X_in, 16)
            store_y(NC - 1)
            for t in range(6, NT):
                sp.dma_start(X[:, t, :], x_t[t]).then_inc(X_late_in, 16)
            sp.wait_ge(y_stored, 16 * NC)
            with sp.Fori(1, NT) as t:
                sp.wait_ge(mix_lo_out, t + 1)
                load_mix(t, KT)
            load_unit(up0_load(3), w_up_v, up_col(3))

            def load_down(i):
                for k in range(2):
                    load_row(down_load(i, k), w_down_v, 2 * i + k)

            def load_up(i):
                for s in range(4):
                    load_unit(up_load(i, s), w_up_v, up_col(s) + 2 * P * (i + 1))

            load_up(0)
            with sp.Fori(1, NG - 1) as i:
                load_down(i - 1)
                load_up(i)
            load_down(NG - 2)
            load_down(NG - 1)
            with sp.Fori(0, NT) as t:
                sp.wait_ge(down_added, 2 * NT * (NG - 1) + 2 * t + 2)
                sp.dma_start(out_t[ds(t, 1)].rearrange("a p d -> (a p) d"),
                             X[:, ds(t, 1), :].rearrange("p a d -> p (a d)")).then_inc(out_stored, 16)
            sp.wait_ge(out_stored, 16 * NT)

        @block.gpsimd
        def _(pool):
            pool.memset(neghalf[:, :], -0.5).then_inc(const_set, 1)
            pool.memset(eps[:, :], EPS).then_inc(const_set, 1)
            pool.memset(ones[:, :], 1.0).then_inc(const_set, 1)
            pool.memset(ident[:, :], 0.0).then_inc(const_set, 1)
            pool.memset(mask[:, :], 0.0).then_inc(const_set, 1)
            pool.memset(rows[:, :], 0.0).then_inc(const_set, 1)
            pool.wait_ge(const_set, 6)
            pool.affine_select(out=ident[:, :], in_=ident[:, :], compare_op=ALU.not_equal, fill=1.0,
                               base=0, pattern=[[-1, P]], channel_multiplier=1).then_inc(const_set, 1)
            for s in (0, 2):
                pool.affine_select(out=mask[:, s * P:(s + 1) * P], in_=mask[:, s * P:(s + 1) * P],
                                   compare_op=ALU.is_ge, fill=NEG, base=0, pattern=[[-1, P]],
                                   channel_multiplier=1).then_inc(const_set, 1)
            pool.affine_select(out=mask[:, P:2 * P], in_=mask[:, P:2 * P], compare_op=ALU.is_gt, fill=NEG,
                               base=0, pattern=[[1, P]], channel_multiplier=-1).then_inc(const_set, 1)

            def power(dst, mean, width, done, before):
                pool.tensor_tensor(dst, mean, eps[:, 0:width], ALU.add).then_inc(done, 1)
                pool.wait_ge(done, before + 1)
                pool.tensor_tensor(dst, dst, neghalf[:, 0:width], ALU.pow).then_inc(done, 1)

            def x_power(t, par):
                pool.wait_ge(x_sq, t + 1)
                if not is_(t, 0, 1):
                    pool.wait_ge(x_normed, t - 1)
                power(x_r[:, par:par + 1], x_ss[:, par:par + 1], 1, x_rms, 2 * t)

            def h_power(t, par):
                pool.wait_ge(h_sq, t + 1)
                if not is_(t, 0, 1):
                    pool.wait_ge(h_normed, t - 1)
                power(h_r[:, par:par + 1], h_ss[:, par:par + 1], 1, h_rms, 2 * t)

            def qk_power(t):
                pool.wait_ge(qk_sum, t + 1)
                if not is_(t, 0):
                    pool.wait_ge(qk_normed, 4 * t - 2)
                power(qk_r[:, :], qk_ss[:, :], NQ + NKV, qk_rms, 2 * t)

            def step(t, par):
                x_power(t + 1, 1 - par)
                qk_power(t)

            x_power(0, 0)
            step(0, 0)
            step(1, 1)
            step(2, 0)
            with pool.Fori(0, 2) as tt:
                step(2 * tt + 3, 1)
                step(2 * tt + 4, 0)
            qk_power(LAST)
            pool.wait_ge(attn_sum_out, NT)
            pool.tensor_scalar(attn_ss[:, :], attn_ss[:, :], 1.0 / AW, None, ALU.mult).then_inc(attn_rms, 1)
            pool.wait_ge(attn_rms, 1)
            power(attn_r[:, :], attn_ss[:, :], NT, attn_rms, 1)
            pool.wait_ge(css_sum, NC)
            pool.tensor_scalar(conv_ss[:, :], conv_ss[:, :], 1.0 / CW, None, ALU.mult).then_inc(conv_rms, 1)
            pool.wait_ge(conv_rms, 1)
            power(conv_r[:, :], conv_ss[:, :], NT, conv_rms, 1)
            h_power(0, 0)
            h_power(1, 1)
            with pool.Fori(1, NT // 2) as tt:
                h_power(2 * tt, 0)
                h_power(2 * tt + 1, 1)

        @block.scalar
        def _(act):
            act.dma_start(gain[:, :], attn_norm_w.to_broadcast([P, D])).then_inc(gain_in, 16)
            act.dma_start(qk_gain[:, 0, :], q_norm_w.to_broadcast([P, HD])).then_inc(const_in, 16)
            act.dma_start(qk_gain[:, 1, :], k_norm_w.to_broadcast([P, HD])).then_inc(const_in, 16)
            act.dma_start(sink[:, :], sinks.to_broadcast([P, NQ])).then_inc(const_in, 16)
            act.wait_ge(const_set, 6)
            fcw = ffn_conv_w[0].rearrange("t (f p) -> (t f) p", p=P)
            R = TAPS * 2 * NF - P
            act.dma_start(rows[:, 0:P], fcw[0:P, :]).then_inc(const_in, 16)
            act.dma_start(rows[0:R, P:2 * P], fcw[P:P + R, :]).then_inc(const_in, 16)
            act.dma_start(rows[R:R + TAPS * NC, P:2 * P],
                          conv_mix_w[0].rearrange("t (f p) -> (t f) p", p=P)).then_inc(const_in, 16)
            R += TAPS * NC
            act.dma_start(rows[R:R + 4, P:2 * P],
                          attn_out_norm_w[0].rearrange("(f p) -> f p", p=P)).then_inc(const_in, 16)
            act.dma_start(rows[R + 4:R + 8, P:2 * P],
                          conv_out_norm_w[0].rearrange("(f p) -> f p", p=P)).then_inc(const_in, 16)

            def square_sum(src, width, total, done, scale=1.0):
                act.activation(junk[:, 0:width], src, ACT.Square, scale=scale, accum_out=total).then_inc(done, 1)

            def x_square(t, par, uses):
                act.wait_ge(x_in[par], 16 * uses + 16)
                if not is_(t, 0):
                    act.wait_ge(x_sq, t)
                if not is_(t, 0, 1):
                    act.wait_ge(x_rms, 2 * t - 2)
                square_sum(xin[par][:, :], D, x_ss[:, par:par + 1], x_sq, float(D) ** -0.5)

            def h_split_hi(t):
                for i in range(2):
                    act.wait_ge(x_turned, 2 * t + i + 1)
                    if not is_(t, 0):
                        act.wait_ge(qkv_done, t)
                        act.wait_ge(h_kept, 32 * t)
                    act.activation(hb_hi[:, 4 * i:4 * i + 4, :],
                                   TR[i][:, :].rearrange("p (k t) -> p k t", t=P), ACT.Copy).then_inc(h_hi, 1)

            def qkv_read(t, par):
                act.wait_ge(qkv_done, t + 1)
                if not is_(t, 0):
                    act.wait_ge(qk_sum, t)
                act.activation(qk_sqr[:, NQ:, :], Q[1][:, 0:NKV * HD].rearrange("p (h d) -> p h d", d=HD),
                               ACT.Square, scale=float(HD) ** -0.5).then_inc(qk_sq, 1)
                act.activation(qk_sqr[:, 0:NQ, :], Q[0][:, :].rearrange("p (h d) -> p h d", d=HD),
                               ACT.Square, scale=float(HD) ** -0.5).then_inc(qk_sq, 1)
                if from_(t, 2):
                    act.wait_ge(v_slot, t - 1)
                act.activation(v_new[:, par, :], Q[1][:, NKV * HD:2 * NKV * HD], ACT.Copy).then_inc(v_read, 1)

            def qkT_hi(t, par):
                for i, (dst, width) in enumerate(((qT_hi[:, :, :], AW), (kT_hi[:, par, :], P))):
                    act.wait_ge(qk_turned, 2 * t + i + 1)
                    if not is_(t, 0):
                        act.wait_ge(scores_done, 2 * t)
                    src = TR[i][:, 0:width]
                    act.activation(dst, src.rearrange("p (h t) -> p h t", t=P) if i == 0 else src,
                                   ACT.Copy).then_inc(qkT_hi_out, 1)

            def v_place(b, par):
                act.wait_ge(v_read, b + 1)
                if not is_(b, 0):
                    act.wait_ge(pv_done, 2 * b)
                act.activation(v_win[:, par, :], v_new[:, par, :], ACT.Copy).then_inc(v_slot, 1)

            def probT_copy(b, f):
                act.wait_ge(prob_turned, prob_fill(b, f))
                if not is_(b, 0):
                    act.wait_ge(pv_done, 2 * b)
                act.activation(probT[:, 2 * (f - 2) if is_(b, 0) else f, :], TR[f % 2][:, :],
                               ACT.Copy).then_inc(probT_out, 1)

            def softmax_exp(b, g, keys):
                act.wait_ge(shift, 6 * b + 3 * g + 3)
                if not is_(b, 0):
                    act.wait_ge(denom, 4 * b + 2 * g - 3)
                for h in range(4 * g, 4 * g + 4):
                    act.activation(prob[:, h, 0:keys], prob[:, h, 0:keys], ACT.Exp,
                                   bias=negm[:, h:h + 1], accum_out=den[:, h:h + 1])
                act.activation(es[:, 4 * g:4 * g + 4], sd[:, 4 * g:4 * g + 4], ACT.Exp).then_inc(exps, 1)

            def attn_read(b):
                act.wait_ge(pv_done, 2 * b + 2)
                if not is_(b, 0):
                    act.wait_ge(attn_sums_done, b)
                    act.wait_ge(mix_stored, 32 * b)
                src = A[0][:, :].rearrange("p (h t) -> p h t", t=P)
                act.activation(attn_sqr[:, :, :], src, ACT.Square).then_inc(attn_sq, 1)
                act.activation(attnT[:, :, :], src, ACT.Copy).then_inc(attnT_out, 1)

            def step(t, par, x_uses):
                if from_(t, 2):
                    v_place(t - 2, par)
                if not is_(t, LAST):
                    x_square(t + 1, 1 - par, x_uses)
                qkv_read(t, par)
                if from_(t, 2):
                    for f in range(2 if is_(t, 2) else 0, 4):
                        probT_copy(t - 2, f)
                if from_(t, 1):
                    softmax_exp(t - 1, 0, P if is_(t, 1) else 2 * P)
                if not is_(t, LAST):
                    h_split_hi(t + 1)
                if from_(t, 1):
                    softmax_exp(t - 1, 1, P if is_(t, 1) else 2 * P)
                if from_(t, 2):
                    attn_read(t - 2)
                qkT_hi(t, par)

            x_square(0, 0, 0)
            h_split_hi(0)
            for k in range(KT):
                split_hi(act, qkv_load(k), wq_hi[:, k, :])
            step(0, 0, 0)
            step(1, 1, 1)
            step(2, 0, 1)
            with act.Fori(0, 2) as tt:
                step(2 * tt + 3, 1, tt + 2)
                step(2 * tt + 4, 0, tt + 2)
            step(LAST, 1, 0)
            act.wait_ge(x_turned, 2 * NT)
            for s in range(2):
                split_hi(act, unit0_load(s), wc_hi[s][:, :, :])
            v_place(LAST - 1, 0)
            for f in range(4):
                probT_copy(LAST - 1, f)
            for g in range(2):
                softmax_exp(LAST, g, 2 * P)
            attn_read(LAST - 1)
            v_place(LAST, 1)
            for f in range(4):
                probT_copy(LAST, f)
            split_hi(act, unit0_load(2), wc_hi[2][:, :, :])
            attn_read(LAST)

            def conv_iteration(j, last):
                for hf in range(NH):
                    act.wait_ge(unit_done, 3 * j + 1)
                    if not is_(j, 0):
                        act.wait_ge(cu_out, NH * j)
                    act.activation(c_sb[:, hf * HALF:(hf + 1) * HALF], Q[hf][:, :], ACT.Copy).then_inc(c_out, 1)
                if not last:
                    for s in range(3):
                        act.wait_ge(unit_done, 3 * j + s + 1)
                        split_hi(act, unit_load(j, s), wc_hi[s][:, :, :])
                    for m in range(wo_tiles(j)):
                        k = WO_STEP * j + m
                        split_hi(act, wo_load(j, m), wo_hi[:, ds(k, 1), :].rearrange("p a e -> p (a e)"),
                                 coef[:, ds(OUT0 + k, 1)])
                else:
                    act.wait_ge(mixb_in, 16)
                    act.activation(mix_hi[0][:, 0:KT - 1, :], mixb[:, 0:KT - 1, :], ACT.Copy).then_inc(mix_hi_out, 1)
                act.wait_ge(y_chain, 5 * j + 5)
                if last:
                    act.activation(mix_hi[0][:, KT - 1, :], y[:, 0:P], ACT.Copy).then_inc(mix_hi_out, 1)
                if not is_(j, 0):
                    act.wait_ge(css_done, j)
                act.activation(ysq[:, :], y[:, :], ACT.Square).then_inc(ysq_out, 1)

            act.wait_ge(coef_out, 2)
            act.wait_ge(mix_stored, 32 * NT)
            for j in range(3):
                conv_iteration(j, False)
            act.wait_ge(x_normed, NT)
            act.dma_start(gain[:, :], ffn_norm_w.to_broadcast([P, D])).then_inc(gain_in, 16)
            conv_iteration(3, True)

            def mix_split_hi(t, par):
                act.wait_ge(mixb_in, 16 * t + 16)
                if is_(t, 1):
                    act.wait_ge(css_sum, NC)
                else:
                    act.wait_ge(proj_done, 2 * t - 2)
                act.activation(mix_hi[par][:, :, :], mixb[:, :, :], ACT.Copy).then_inc(mix_hi_out, 1)

            def h_square(t, par):
                act.wait_ge(X_added, 4 * t + 4)
                act.wait_ge(x_sq, NT)
                if not is_(t, 0):
                    act.wait_ge(h_sq, t)
                if not is_(t, 0, 1):
                    act.wait_ge(h_rms, 2 * t - 2)
                square_sum(X[:, ds(t, 1), :].rearrange("p a d -> p (a d)"), D, h_ss[:, par:par + 1], h_sq, float(D) ** -0.5)

            def h2_split_hi(t):
                for i in range(2):
                    act.wait_ge(h_turned, 2 * t + i + 1)
                    act.activation(hT_hi[:, 4 * i:4 * i + 4, ds(P * t, P)],
                                   TR[i][:, :].rearrange("p (k t) -> p k t", t=P), ACT.Copy).then_inc(h2_hi, 1)

            def d_step(t, par):
                if not is_(t, 0):
                    h_square(t - 1, 1 - par)
                if not is_(t, LAST):
                    mix_split_hi(t + 1, 1 - par)
                if not is_(t, 0):
                    h2_split_hi(t - 1)

            d_step(0, 0)
            d_step(1, 1)
            d_step(2, 0)
            with act.Fori(0, 2) as tt:
                d_step(2 * tt + 3, 1)
                d_step(2 * tt + 4, 0)
            d_step(LAST, 1)
            h_square(LAST, 1)
            act.wait_ge(proj_done, 2 * NT)
            for s in range(2):
                split_hi(act, up0_load(s), wu_hi[s][:, :, :])
            h2_split_hi(LAST)
            for s in range(2, 4):
                split_hi(act, up0_load(s), wu_hi[s][:, :, :])

            def down_operands_hi(i):
                if is_(i, 0):
                    act.wait_ge(proj_done, 2 * NT)
                elif is_(i, NG - 1):
                    act.wait_ge(up_done, 4 * NG)
                else:
                    act.wait_ge(down_filled, 2 * NT * i)
                a_hi, _, w_hi, _ = down_operands(i)
                for k in range(2):
                    act.wait_ge(gated_out, 2 * i + k + 1)
                    act.activation(a_hi[k], gated[:, k, :], ACT.Copy).then_inc(act_hi_out, 1)
                for k in range(2):
                    split_hi(act, down_load(i, k), w_hi[k])

            def up_weights_hi(i, s):
                act.wait_ge(up_done, 4 * i + s + 1)
                split_hi(act, up_load(i, s), wu_hi[s][:, :, :])

            def ffn_iteration(i, first, last):
                for s in range(4):
                    act.wait_ge(up_done, 4 * i + s + 1)
                    if not (first and s == 0):
                        act.wait_ge(conv_chain, 12 * i + 3 * s)
                    for hf in range(NH):
                        act.activation(z[:, TAPS - 1 + hf * HALF:TAPS - 1 + (hf + 1) * HALF],
                                       (Q, A)[s % 2][hf][:, :], ACT.Copy).then_inc(z_out, 1)
                    if s == 0 and not first:
                        down_operands_hi(i - 1)
                    if s >= 1 and not last:
                        up_weights_hi(i, s - 1)
                    if s % 2 == 0:
                        act.wait_ge(conv_chain, 12 * i + 3 * s + 3)
                        act.activation(acc_g[:, :], acc_g[:, :], ACT.Silu).then_inc(silu_out, 1)
                if not last:
                    up_weights_hi(i, 3)

            act.wait_ge(z_pad, 1)
            ffn_iteration(0, True, False)
            ffn_iteration(1, False, False)
            with act.Fori(2, NG - 1) as i:
                ffn_iteration(i, False, False)
            ffn_iteration(NG - 1, False, True)
            down_operands_hi(NG - 1)

        @block.tensor
        def _(pe):
            def x_transpose(t, par):
                pe.wait_ge(x_normed, t + 1)
                for i in range(2):
                    if is_(t, 1):
                        pe.wait_ge(coef_out, i + 1)
                    elif from_(t, 3):
                        pe.wait_ge(probT_out, prob_fill(t - 3, 2 + i))
                    for k in range(4):
                        mm = pe.transpose(TR[i][:, k * P:(k + 1) * P],
                                          xin[par][:, (4 * i + k) * P:(4 * i + k + 1) * P], ident[:, :])
                    mm.then_inc(x_turned, 1)

            def qkv(t, first=False):
                pe.wait_ge(h_lo, 2 * t + 2)
                if not first:
                    pe.wait_ge(qk_normed, 4 * t - 2)
                    pe.wait_ge(v_read, t)
                for k in range(KT):
                    if first:
                        pe.wait_ge(stage_lo, qkv_load(k).n + 1)
                    for h, w, st in ((hb_hi, wq_hi, k == 0), (hb_hi, wq_lo, False), (hb_lo, wq_hi, False)):
                        end = k == KT - 1 and h is hb_lo
                        pe.matmul(Q[0][:, :], h[:, k, :], w[:, k, 0:AW], start=st, stop=end)
                        mm = pe.matmul(Q[1][:, 0:QKV - AW], h[:, k, :], w[:, k, AW:QKV], start=st, stop=end)
                mm.then_inc(qkv_done, 1)

            def prob_transpose(b, kv):
                pe.wait_ge(prob_divided, 2 * b + kv + 1)
                for s in range(1 if is_(b, 0) else 2):
                    f = 2 + kv if is_(b, 0) else 2 * kv + s
                    if kv == 1 and not is_(b, 0):
                        pe.wait_ge(probT_out, prob_fill(b, s))
                    elif is_(b, LAST):
                        pe.wait_ge(probT_out, prob_fill(b - 1, 2 + s))
                    else:
                        pe.wait_ge(qkT_lo_out, 2 * b + 4)
                    for h in range(GROUP):
                        mm = pe.transpose(TR[f % 2][:, h * P:(h + 1) * P],
                                          prob[:, GROUP * kv + h, s * P:(s + 1) * P], ident[:, :])
                    mm.then_inc(prob_turned, 1)

            def attention_output(b):
                pe.wait_ge(v_slot, b + 1)
                if is_(b, LAST):
                    pe.wait_ge(attnT_out, b)
                else:
                    pe.wait_ge(masked, 2 * b + 3)
                for kv in range(NKV):
                    slots = (0,) if is_(b, 0) else (0, 1)
                    pe.wait_ge(probT_out, prob_fill(b, 2 + kv if is_(b, 0) else 2 * kv + 1))
                    for s in slots:
                        mm = pe.matmul(A[0][HD * kv:HD * (kv + 1), :], v_win[:, s, kv * HD:(kv + 1) * HD],
                                       probT[:, 2 * kv + s, :], start=s == slots[0], stop=s == slots[-1])
                    mm.then_inc(pv_done, 1)

            def attn_sums(b, out):
                pe.wait_ge(attn_sq, b + 1)
                if is_(b, LAST):
                    pe.wait_ge(probT_out, prob_fill(b, 3))
                else:
                    pe.wait_ge(masked, 2 * b + 4)
                for h in range(GROUP):
                    mm = pe.matmul(out, attn_sqr[:, h, :], ones[:, :], start=h == 0, stop=h == GROUP - 1)
                mm.then_inc(attn_sums_done, 1)

            def qk_transpose(t):
                pe.wait_ge(qk_normed, 4 * t + 4)
                for i, tiles in enumerate((range(GROUP), (GROUP,))):
                    if is_(t, LAST):
                        pe.wait_ge(probT_out, prob_fill(t - 2, 2 + i))
                    else:
                        pe.wait_ge(h_lo, 2 * t + 3 + i)
                    for n, tile in enumerate(tiles):
                        mm = pe.transpose(TR[i][:, n * P:(n + 1) * P], qn[:, tile, :], ident[:, :])
                    mm.then_inc(qk_turned, 1)

            def scores(b, kv):
                n = P if is_(b, 0) else 2 * P
                pe.wait_ge(qkT_lo_out, 2 * b + 2)
                if not is_(b, 0):
                    pe.wait_ge(masked, 2 * b - 1 + kv)
                if from_(b, 2):
                    pe.wait_ge((attnT_out, attn_sum_out)[kv], b - 1)
                rows_ = slice(HD * kv, HD * (kv + 1))
                for h in range(GROUP):
                    dst = A[2 * kv + h // 2][:, (h % 2) * 2 * P:(h % 2) * 2 * P + n]
                    for m, (q, k) in enumerate(((qT_hi, kT_hi), (qT_hi, kT_lo), (qT_lo, kT_hi))):
                        mm = pe.matmul(dst, q[rows_, h, :], k[rows_, 0:n // P, :].rearrange("p s t -> p (s t)"),
                                       start=m == 0, stop=m == 2)
                mm.then_inc(scores_done, 1)

            def step(t, par):
                qkv(t, first=is_(t, 0))
                if from_(t, 3):
                    attn_sums(t - 3, A[3][:, 0:1])
                if from_(t, 2):
                    prob_transpose(t - 2, 0)
                if from_(t, 1):
                    scores(t - 1, 0)
                if from_(t, 2):
                    prob_transpose(t - 2, 1)
                if from_(t, 1):
                    scores(t - 1, 1)
                if not is_(t, LAST):
                    x_transpose(t + 1, 1 - par)
                if from_(t, 2):
                    attention_output(t - 2)
                qk_transpose(t)

            pe.wait_ge(const_set, 7)
            x_transpose(0, 0)
            pe.wait_ge(const_in, 8 * 16)
            for i in range(2):
                pe.wait_ge(h_lo, i + 1)
                pe.transpose(TR[i][:, 0:P], rows[:, i * P:(i + 1) * P], ident[:, :]).then_inc(coef_turned, 1)
            step(0, 0)
            step(1, 1)
            step(2, 0)
            with pe.Fori(0, 2) as tt:
                step(2 * tt + 3, 1)
                step(2 * tt + 4, 0)
            step(LAST, 1)

            def unit(banks, hi, lo):
                for k in range(KT):
                    for w, h, st in ((hi, hT_hi, k == 0), (hi, hT_lo, False), (lo, hT_hi, False)):
                        for hf in range(NH):
                            mm = pe.matmul(banks[hf][:, :], w[:, k, :], h[:, k, hf * HALF:(hf + 1) * HALF],
                                           start=st, stop=k == KT - 1 and w is lo)
                return mm

            def conv_unit(j, s, first):
                if first:
                    pe.wait_ge(stage_lo, unit0_load(s).n + 1)
                else:
                    pe.wait_ge(stage_lo, unit_load(j - 1, s).n + 1)
                    if is_(j, 1) and s > 0:
                        pe.wait_ge((y_chain, cu_out)[s - 1], (5, NH)[s - 1])
                    else:
                        pe.wait_ge((c_out, cu_out, y_chain)[s], (NH, NH, 5)[s] * j)
                unit((Q, A[2:4], A[0:2])[s] if first else (Q, A[0:2], A[2:4])[s], wc_hi[s], wc_lo[s]).then_inc(unit_done, 1)

            def conv_sums(j):
                pe.wait_ge(ysq_out, j + 1)
                if is_(j, 0):
                    pe.wait_ge(probT_out, prob_fill(LAST, 2))
                else:
                    pe.wait_ge(css_sum, j)
                for t in range(NT):
                    mm = pe.matmul(TR[0][:, t:t + 1], ysq[:, t * P:(t + 1) * P], ones[:, :], start=True, stop=True)
                mm.then_inc(css_done, 1)

            pe.wait_ge(h_kept, 32 * NT)
            pe.wait_ge(qk_normed, 4 * NT - 2)
            pe.wait_ge(v_read, NT)
            conv_unit(0, 0, True)
            attn_sums(LAST - 2, A[3][:, 0:1])
            for kv in range(NKV):
                prob_transpose(LAST - 1, kv)
                scores(LAST, kv)
            attention_output(LAST - 1)
            pe.wait_ge(masked, 2 * NT)
            conv_unit(0, 1, True)
            attn_sums(LAST - 1, A[1][:, 0:1])
            for kv in range(NKV):
                prob_transpose(LAST, kv)
            attention_output(LAST)
            pe.wait_ge(attnT_out, NT)
            pe.wait_ge(attn_sum_out, LAST)
            conv_unit(0, 2, True)
            attn_sums(LAST, TR[1][:, 0:1])

            def conv_iteration(j):
                conv_unit(j, 0, False)
                conv_sums(j - 1)
                conv_unit(j, 1, False)
                conv_unit(j, 2, False)

            conv_iteration(1)
            with pe.Fori(2, NC) as j:
                conv_iteration(j)

            def project(t, par, part):
                if not is_(t, 0):
                    pe.wait_ge(X_added, 4 * t - 2 + 2 * part)
                elif part == 0:
                    pe.wait_ge(cu_out, NH * NC)
                else:
                    pe.wait_ge(y_chain, 5 * NC)
                banks = A[2 * part:2 * part + 2]
                for k in range(4 * part, 4 * part + 4):
                    for m, w, st in ((mix_hi, wo_hi, k % 4 == 0), (mix_hi, wo_lo, False), (mix_lo, wo_hi, False)):
                        for n in range(2):
                            mm = pe.matmul(banks[n][:, :], m[par][:, k, :], w[:, k, n * HALF:(n + 1) * HALF],
                                           start=st, stop=k % 4 == 3 and m is mix_lo)
                mm.then_inc(proj_done, 1)

            def h_transpose(t):
                pe.wait_ge(h_normed, t + 1)
                for i in range(2):
                    if is_(t, 0):
                        pe.wait_ge((css_sum, attn_sum_out)[i], (NC, NT)[i])
                    else:
                        pe.wait_ge(h2_lo, 2 * t - 1 + i)
                    for k in range(4):
                        mm = pe.transpose(TR[i][:, k * P:(k + 1) * P], xn[:, (4 * i + k) * P:(4 * i + k + 1) * P],
                                          ident[:, :])
                    mm.then_inc(h_turned, 1)

            def d_step(t, par):
                pe.wait_ge(mix_lo_out, 1 if is_(t, 0) else t + 2)
                project(t, par, 0)
                if is_(t, 0):
                    conv_sums(NC - 1)
                    pe.wait_ge(mix_lo_out, 2)
                else:
                    h_transpose(t - 1)
                project(t, par, 1)

            pe.wait_ge(stage_lo, N_F0)
            d_step(0, 0)
            d_step(1, 1)
            d_step(2, 0)
            with pe.Fori(0, 2) as tt:
                d_step(2 * tt + 3, 1)
                d_step(2 * tt + 4, 0)
            d_step(LAST, 1)
            h_transpose(LAST)

            def up_units(i, first):
                for s in range(4):
                    if first:
                        pe.wait_ge(stage_lo, up0_load(s).n + 1)
                    else:
                        pe.wait_ge(stage_lo, up_load(i - 1, s).n + 1)
                    if not (first and s < 2):
                        pe.wait_ge(z_out, 8 * i + 2 * s - 2)
                    unit((Q, A[0:2])[s % 2], wu_hi[s], wu_lo[s]).then_inc(up_done, 1)

            def down(i):
                ring = (TR[0], TR[1], A[2], A[3])
                a_hi, a_lo, w_hi, w_lo = down_operands(i)
                pe.wait_ge(act_lo_out, 2 * i + 2)
                pe.wait_ge(stage_lo, down_load(i, 1).n + 1)
                for g in range(2 * NT):
                    t, n = g // 2, g % 2
                    if not (is_(i, 0) and g < 4):
                        pe.wait_ge(down_added, 2 * NT * i + g - 3)
                    for k in range(2):
                        for m, (a, w) in enumerate(((a_hi, w_hi), (a_hi, w_lo), (a_lo, w_hi))):
                            mm = pe.matmul(ring[g % 4][:, :], a[k][:, t * P:(t + 1) * P],
                                           w[k][:, n * HALF:(n + 1) * HALF],
                                           start=k == 0 and m == 0, stop=k == 1 and m == 2)
                    mm.then_inc(down_filled, 1)

            pe.wait_ge(h2_lo, 2 * NT)
            pe.wait_ge(X_added, 4 * NT)
            up_units(0, True)
            up_units(1, False)
            down(0)
            with pe.Fori(2, NG - 1) as i:
                up_units(i, False)
                down(i - 1)
            up_units(NG - 1, False)
            down(NG - 2)
            down(NG - 1)

        @block.vector
        def _(dve):
            def x_norm(t, par):
                dve.wait_ge(x_rms, 2 * t + 2)
                dve.scalar_tensor_tensor(xin[par][:, :], xin[par][:, :], x_r[:, par:par + 1], gain[:, :],
                                         ALU.mult, ALU.mult).then_inc(x_normed, 1)

            def h_split_lo(t):
                for i in range(2):
                    dve.wait_ge(h_hi, 2 * t + i + 1)
                    dve.tensor_tensor(hb_lo[:, 4 * i:4 * i + 4, :],
                                      TR[i][:, :].rearrange("p (k t) -> p k t", t=P),
                                      hb_hi[:, 4 * i:4 * i + 4, :].bitcast(FP32), ALU.subtract).then_inc(h_lo, 1)

            def head_sums(t):
                dve.wait_ge(qk_sq, 2 * t + 2)
                dve.tensor_reduce(qk_ss[:, :], qk_sqr[:, :, :], AX.X, ALU.add).then_inc(qk_sum, 1)

            qn_heads = (qn[:, 0:GROUP, :].rearrange("p i (g d) -> p g i d", d=HD),
                        qn[:, GROUP, :].rearrange("p (g d) -> p g d", d=HD))

            def qk_norm(t):
                dve.wait_ge(qk_rms, 2 * t + 2)
                dve.wait_ge(qk_sq, 2 * t + 2)
                dve.wait_ge(v_read, t + 1)
                if not is_(t, 0):
                    dve.wait_ge(qk_turned, 2 * t)
                q_r = qk_r[:, 0:NQ].rearrange("p (g i) -> p g i", i=GROUP)
                dve.tensor_tensor(qn_heads[0], Q[0][:, :].rearrange("p (g i d) -> p g i d", i=GROUP, d=HD),
                                  q_r.unsqueeze(3).to_broadcast([P, NKV, GROUP, HD]), ALU.mult).then_inc(qk_normed, 1)
                dve.tensor_tensor(qn_heads[1], Q[1][:, 0:NKV * HD].rearrange("p (h d) -> p h d", d=HD),
                                  qk_r[:, NQ:].unsqueeze(2).to_broadcast([P, NKV, HD]), ALU.mult).then_inc(qk_normed, 1)
                for n, (lo, hi) in enumerate(((0, GROUP), (GROUP, GROUP + 1))):
                    dve.wait_ge(qk_normed, 4 * t + n + 1)
                    tile = qn[:, lo:hi, :].rearrange("p i (g d) -> p (i g) d", d=HD)
                    dve.tensor_tensor(tile, tile, qk_gain[:, n:n + 1, :].to_broadcast([P, 2 * (hi - lo), HD]),
                                      ALU.mult).then_inc(qk_normed, 1)

            def qkT_lo(t, par):
                for i, (lo, hi, width) in enumerate(((qT_lo[:, :, :], qT_hi[:, :, :], AW),
                                                     (kT_lo[:, par, :], kT_hi[:, par, :], P))):
                    dve.wait_ge(qkT_hi_out, 2 * t + i + 1)
                    src = TR[i][:, 0:width]
                    dve.tensor_tensor(lo, src.rearrange("p (h t) -> p h t", t=P) if i == 0 else src,
                                      hi.bitcast(FP32), ALU.subtract).then_inc(qkT_lo_out, 1)

            def prob_divide(b, g, keys):
                cols = slice(4 * g, 4 * g + 4)
                dve.wait_ge(exps, 2 * b + g + 1)
                dve.tensor_tensor(dsum[:, cols], den[:, cols], es[:, cols], ALU.add).then_inc(denom, 1)
                dve.wait_ge(denom, 4 * b + 2 * g + 1)
                dve.reciprocal(rden[:, cols], dsum[:, cols]).then_inc(denom, 1)
                dve.wait_ge(denom, 4 * b + 2 * g + 2)
                dve.tensor_tensor(prob[:, cols, 0:keys], prob[:, cols, 0:keys],
                                  rden[:, cols].unsqueeze(2).to_broadcast([P, GROUP, keys]),
                                  ALU.mult).then_inc(prob_divided, 1)

            def copy_attn_sums(b, src):
                dve.wait_ge(attn_sums_done, b + 1)
                dve.tensor_copy(attn_ss[:, ds(b, 1)], src).then_inc(attn_sum_out, 1)

            def mask_max(b, g, par, keys):
                window = mask[:, par * P:par * P + keys]
                cols = slice(4 * g, 4 * g + 4)
                dve.wait_ge(scores_done, 2 * b + g + 1)
                if not is_(b, 0):
                    dve.wait_ge(exps, 2 * b + g - 1)
                dve.sem_inc(scores_seen, 1)
                for h in range(4 * g, 4 * g + 4):
                    mm = dve.tensor_tensor_reduce(out=prob[:, h, 0:keys],
                                                  in0=A[h // 2][:, (h % 2) * 2 * P:(h % 2) * 2 * P + keys],
                                                  in1=window, scale=1.0, scalar=-3e38, op0=ALU.add, op1=ALU.max,
                                                  accum_out=mx[:, h:h + 1])
                mm.then_inc(masked, 1)
                dve.wait_ge(masked, 2 * b + g + 1)
                dve.tensor_tensor(top_score[:, cols], mx[:, cols], sink[:, cols], ALU.max).then_inc(shift, 1)
                dve.wait_ge(shift, 6 * b + 3 * g + 1)
                dve.tensor_scalar(negm[:, cols], top_score[:, cols], -1.0, None, ALU.mult).then_inc(shift, 1)
                dve.tensor_tensor(sd[:, cols], sink[:, cols], top_score[:, cols], ALU.subtract).then_inc(shift, 1)

            def step(t, par):
                if from_(t, 2):
                    for g in range(2):
                        prob_divide(t - 2, g, P if is_(t, 2) else 2 * P)
                if not is_(t, LAST):
                    x_norm(t + 1, 1 - par)
                if from_(t, 3):
                    copy_attn_sums(t - 3, A[3][:, 0:1])
                head_sums(t)
                keys = P if is_(t, 1) else 2 * P
                if from_(t, 1):
                    mask_max(t - 1, 0, 1 - par, keys)
                qk_norm(t)
                if from_(t, 1):
                    mask_max(t - 1, 1, 1 - par, keys)
                if not is_(t, LAST):
                    h_split_lo(t + 1)
                qkT_lo(t, par)

            dve.wait_ge(gain_in, 16)
            x_norm(0, 0)
            h_split_lo(0)
            dve.wait_ge(const_in, 8 * 16)
            dve.tensor_scalar(qk_gain[:, 0, :], qk_gain[:, 0, :], float(HD) ** -0.5, None, ALU.mult).then_inc(coef_set, 1)
            for i in range(2):
                dve.wait_ge(coef_turned, i + 1)
                dve.tensor_copy(coef[:, i * P:(i + 1) * P], TR[i][:, 0:P]).then_inc(coef_out, 1)
            for k in range(KT):
                split_lo(dve, qkv_load(k), wq_hi[:, k, :], wq_lo[:, k, :])
            dve.wait_ge(coef_set, 1)
            dve.wait_ge(const_set, 10)
            step(0, 0)
            step(1, 1)
            step(2, 0)
            with dve.Fori(0, 2) as tt:
                step(2 * tt + 3, 1)
                step(2 * tt + 4, 0)
            step(LAST, 1)
            for s in range(2):
                split_lo(dve, unit0_load(s), wc_hi[s][:, :, :], wc_lo[s][:, :, :])
            for g in range(2):
                prob_divide(LAST - 1, g, 2 * P)
            copy_attn_sums(LAST - 2, A[3][:, 0:1])
            for g in range(2):
                mask_max(LAST, g, 1, 2 * P)
            for g in range(2):
                prob_divide(LAST, g, 2 * P)
            copy_attn_sums(LAST - 1, A[1][:, 0:1])
            split_lo(dve, unit0_load(2), wc_hi[2][:, :, :], wc_lo[2][:, :, :])

            def causal_conv(acc, src, taps, chain, count, before=(), between=None):
                for sem_, value in before:
                    dve.wait_ge(sem_, value)
                dve.tensor_scalar(acc[:, :], src[:, 2:2 + SEQ], coef[:, taps[2]], None, ALU.mult).then_inc(chain, 1)
                for n in (1, 2):
                    if between:
                        between(n - 1)
                    dve.wait_ge(chain, count + n)
                    dve.scalar_tensor_tensor(acc[:, :], src[:, 2 - n:2 - n + SEQ], coef[:, taps[2 - n]], acc[:, :],
                                             ALU.mult, ALU.add).then_inc(chain, 1)

            def conv_iteration(j, last):
                if not last:
                    split_lo(dve, unit_load(j, 0), wc_hi[0][:, :, :], wc_lo[0][:, :, :])
                u_banks, b_banks = (A[2:4], A[0:2]) if is_(j, 0) else (A[0:2], A[2:4])
                dve.wait_ge(unit_done, 3 * j + 2)
                if not is_(j, 0):
                    dve.wait_ge(y_chain, 5 * j)
                for hf in range(NH):
                    dve.wait_ge(c_out, NH * j + hf + 1)
                    dve.tensor_tensor(cu[:, TAPS - 1 + hf * HALF:TAPS - 1 + (hf + 1) * HALF], u_banks[hf][:, :],
                                      c_sb[:, hf * HALF:(hf + 1) * HALF], ALU.mult).then_inc(cu_out, 1)
                dve.wait_ge(cu_out, NH * j + NH)
                before = () if is_(j, 0) else ((y_stored, 16 * j), (ysq_out, j))
                causal_conv(y, cu, [mix_tap(n, j) for n in range(TAPS)], y_chain, 5 * j, before)
                if not last:
                    split_lo(dve, unit_load(j, 1), wc_hi[1][:, :, :], wc_lo[1][:, :, :])
                else:
                    dve.wait_ge(mix_hi_out, 1)
                    dve.tensor_tensor(mix_lo[0][:, 0:KT - 1, :], mixb[:, 0:KT - 1, :],
                                      mix_hi[0][:, 0:KT - 1, :].bitcast(FP32), ALU.subtract).then_inc(mix_lo_out, 1)
                dve.wait_ge(unit_done, 3 * j + 3)
                dve.wait_ge(y_chain, 5 * j + 3)
                for hf in range(NH):
                    half = slice(hf * HALF, (hf + 1) * HALF)
                    dve.tensor_tensor(y[:, half], b_banks[hf][:, :], y[:, half], ALU.mult).then_inc(y_chain, 1)
                if not last:
                    split_lo(dve, unit_load(j, 2), wc_hi[2][:, :, :], wc_lo[2][:, :, :])
                    for m in range(wo_tiles(j)):
                        k = WO_STEP * j + m
                        split_lo(dve, wo_load(j, m), wo_hi[:, ds(k, 1), :].rearrange("p a e -> p (a e)"),
                                 wo_lo[:, ds(k, 1), :].rearrange("p a e -> p (a e)"), coef[:, ds(OUT0 + k, 1)])

            def conv_sums(j):
                dve.wait_ge(css_done, j + 1)
                if is_(j, 0):
                    dve.tensor_copy(conv_ss[:, :], TR[0][:, 0:NT]).then_inc(css_sum, 1)
                else:
                    dve.wait_ge(css_sum, j)
                    dve.tensor_tensor(conv_ss[:, :], TR[0][:, 0:NT], conv_ss[:, :], ALU.add).then_inc(css_sum, 1)

            dve.wait_ge(mix_stored, 32 * NT)
            dve.memset(cu[:, 0:TAPS - 1], 0.0).then_inc(cu_pad, 1)
            dve.wait_ge(cu_pad, 1)
            conv_iteration(0, False)
            copy_attn_sums(LAST, TR[1][:, 0:1])
            conv_sums(0)
            conv_iteration(1, False)
            conv_sums(1)
            conv_iteration(2, False)
            conv_sums(2)
            conv_iteration(3, True)

            def mix_split_lo(t, par):
                dve.wait_ge(mix_hi_out, t + 2)
                dve.tensor_tensor(mix_lo[par][:, :, :], mixb[:, :, :], mix_hi[par][:, :, :].bitcast(FP32),
                                  ALU.subtract).then_inc(mix_lo_out, 1)

            def add_part(t, part):
                dve.wait_ge(proj_done, 2 * t + part + 1)
                r = (attn_r, conv_r)[part]
                if part == 0:
                    dve.wait_ge(X_in, 16 * 6)
                    if not is_(t, 0):
                        dve.wait_ge(X_late_in, 16 * 2)
                    dve.wait_ge(attn_rms, 3)
                else:
                    dve.wait_ge(conv_rms, 3)
                    dve.wait_ge(X_added, 4 * t + 2)
                for n in range(2):
                    x_half = X[:, ds(t, 1), n * HALF:(n + 1) * HALF].rearrange("p a d -> p (a d)")
                    dve.scalar_tensor_tensor(x_half, A[2 * part + n][:, :], r[:, ds(t, 1)], x_half,
                                             ALU.mult, ALU.add).then_inc(X_added, 1)

            def h_norm(t, par):
                dve.wait_ge(h_rms, 2 * t + 2)
                if not is_(t, 0):
                    dve.wait_ge(h_turned, 2 * t)
                dve.scalar_tensor_tensor(xn[:, :], X[:, ds(t, 1), :].rearrange("p a d -> p (a d)"),
                                         h_r[:, par:par + 1], gain[:, :], ALU.mult, ALU.mult).then_inc(h_normed, 1)

            def h2_split_lo(t):
                for i in range(2):
                    dve.wait_ge(h2_hi, 2 * t + i + 1)
                    dve.tensor_tensor(hT_lo[:, 4 * i:4 * i + 4, ds(P * t, P)],
                                      TR[i][:, :].rearrange("p (k t) -> p k t", t=P),
                                      hT_hi[:, 4 * i:4 * i + 4, ds(P * t, P)].bitcast(FP32),
                                      ALU.subtract).then_inc(h2_lo, 1)

            def d_step(t, par):
                h_norm(t - 1, 1 - par)
                if not is_(t, LAST):
                    mix_split_lo(t + 1, 1 - par)
                add_part(t, 0)
                h2_split_lo(t - 1)
                add_part(t, 1)

            dve.wait_ge(mix_hi_out, 2)
            dve.tensor_tensor(mix_lo[0][:, KT - 1, :], y[:, 0:P], mix_hi[0][:, KT - 1, :].bitcast(FP32),
                              ALU.subtract).then_inc(mix_lo_out, 1)
            dve.wait_ge(gain_in, 32)
            conv_sums(NC - 1)
            mix_split_lo(1, 1)
            add_part(0, 0)
            add_part(0, 1)
            d_step(1, 1)
            d_step(2, 0)
            with dve.Fori(0, 2) as tt:
                d_step(2 * tt + 3, 1)
                d_step(2 * tt + 4, 0)
            d_step(LAST, 1)
            h_norm(LAST, 1)
            for s in range(2):
                split_lo(dve, up0_load(s), wu_hi[s][:, :, :], wu_lo[s][:, :, :])
            h2_split_lo(LAST)
            for s in range(2, 4):
                split_lo(dve, up0_load(s), wu_hi[s][:, :, :], wu_lo[s][:, :, :])

            def act_split_lo(i, k):
                a_hi, a_lo, _, _ = down_operands(i)
                dve.wait_ge(act_hi_out, 2 * i + k + 1)
                dve.tensor_tensor(a_lo[k], gated[:, k, :], a_hi[k].bitcast(FP32), ALU.subtract).then_inc(act_lo_out, 1)

            def down_weights_lo(i, k):
                _, _, w_hi, w_lo = down_operands(i)
                split_lo(dve, down_load(i, k), w_hi[k], w_lo[k])

            def up_weights_lo(i, s):
                split_lo(dve, up_load(i, s), wu_hi[s][:, :, :], wu_lo[s][:, :, :])

            def add_down(i, g):
                ring = (TR[0], TR[1], A[2], A[3])
                t, n = g // 2, g % 2
                x_half = X[:, t, n * HALF:(n + 1) * HALF]
                dve.wait_ge(down_filled, 2 * NT * i + g + 1)
                dve.tensor_tensor(x_half, ring[g % 4][:, :], x_half, ALU.add).then_inc(down_added, 1)

            def convolve(i, s, first, between=None):
                dve.wait_ge(z_out, 8 * i + 2 * s + 2)
                before = () if first and s < 2 else ((gated_out, 2 * i + s // 2),)
                f = 2 * i + s // 2 + (s % 2) * NF
                causal_conv((acc_g, acc_u)[s % 2], z, [ffn_tap(n, f) for n in range(TAPS)], conv_chain,
                            12 * i + 3 * s, before, between)

            def gate(i, k, first):
                dve.wait_ge(silu_out, 2 * i + k + 1)
                dve.wait_ge(conv_chain, 12 * i + 6 * k + 6)
                if not first:
                    dve.wait_ge(act_lo_out, 2 * i)
                dve.tensor_tensor(gated[:, k, :], acc_g[:, :], acc_u[:, :], ALU.mult).then_inc(gated_out, 1)

            def ffn_iteration(i, first, last):
                def add(g):
                    if not first:
                        add_down(i - 1, g)

                convolve(i, 0, first)
                if not first:
                    for k in range(2):
                        act_split_lo(i - 1, k)
                    for k in range(2):
                        down_weights_lo(i - 1, k)
                convolve(i, 1, first)
                gate(i, 0, first)
                if not last:
                    up_weights_lo(i, 0)
                convolve(i, 2, first)
                if not last:
                    up_weights_lo(i, 1)
                convolve(i, 3, first, between=add)
                add(2)
                gate(i, 1, first)
                add(3)
                if last:
                    act_split_lo(i, 0)
                else:
                    up_weights_lo(i, 2)
                add(4)
                add(5)
                if last:
                    act_split_lo(i, 1)
                else:
                    up_weights_lo(i, 3)
                for g in range(6, 2 * NT):
                    add(g)
                    if last and g in (7, 9):
                        down_weights_lo(i, (g - 7) // 2)

            dve.wait_ge(h_turned, 2 * NT)
            dve.memset(z[:, 0:TAPS - 1], 0.0).then_inc(z_pad, 1)
            dve.wait_ge(z_pad, 1)
            ffn_iteration(0, True, False)
            ffn_iteration(1, False, False)
            with dve.Fori(2, NG - 1) as i:
                ffn_iteration(i, False, False)
            ffn_iteration(NG - 1, False, True)
            for g in range(2 * NT):
                add_down(NG - 1, g)


_INS = ["x", "attn_norm_w", "w_in", "q_norm_w", "k_norm_w", "sinks", "conv_mix_w", "attn_out_norm_w",
        "conv_out_norm_w", "w_out", "ffn_norm_w", "w_up", "ffn_conv_w", "w_down"]


def kernel(**inputs):
    import numpy as _np
    import concourse.bacc as _bacc
    from concourse import mybir as _mybir
    from concourse.bass_utils import run_bass_kernel_spmd as _run

    nc = _bacc.Bacc("TRN2", target_bir_lowering=False, num_devices=1)
    arrays, args = {}, []
    for name in _INS:
        a = _np.ascontiguousarray(inputs[name])
        arrays[f"in_{name}_dram"] = a
        args.append(nc.dram_tensor(f"in_{name}_dram", a.shape, _mybir.dt.from_np(a.dtype), kind="ExternalInput").ap())
    shape = tuple(inputs["x"].shape)
    args.append(nc.dram_tensor("out_0_dram", shape, _mybir.dt.float32, kind="ExternalOutput").ap())
    build_layer(nc, *args)
    r = _run(nc, [arrays], core_ids=[0])
    return r.results[0]["out_0_dram"]
```

```python
import concourse.bass as bass
from concourse import mybir
from contextlib import ExitStack

P = 128
FP32 = mybir.dt.float32
FP32R = mybir.dt.float32r
BF16 = mybir.dt.bfloat16
ALU = mybir.AluOpType
ACT = mybir.ActivationFunctionType
AX = mybir.AxisListType
ds = bass.ds


def build_layer(nc, x, attn_norm_w, w_in, q_norm_w, k_norm_w, sinks, conv_mix_w, attn_out_norm_w,
                conv_out_norm_w, w_out, ffn_norm_w, w_up, ffn_conv_w, w_down, out):
    D = x.shape[2]
    SEQ = x.shape[1]
    HD = q_norm_w.shape[1]
    NQ = sinks.shape[1]
    CW = conv_mix_w.shape[2]
    AW = NQ * HD
    NKV = (w_in.shape[2] - AW - 3 * CW) // (2 * HD)
    GROUP = NQ // NKV
    QKV = AW + 2 * NKV * HD
    FF = w_down.shape[1]
    TAPS = conv_mix_w.shape[1]
    KT = D // P
    NT = SEQ // P
    HALF = 512
    NH = SEQ // HALF
    NC = CW // P
    NF = FF // P
    NG = NF // 2
    EPS = 1e-6
    NEG = -1e30
    assert TAPS == 3 and HD == 64 and NT == 8 and KT == 8 and NH == 2 and NF % 2 == 0
    assert AW == HALF and CW == HALF and D == 2 * HALF and NC == 4

    x_t = x[0].rearrange("(t p) d -> t p d", p=P)
    out_t = out[0].rearrange("(t p) d -> t p d", p=P)
    w_in_v = w_in[0].rearrange("(k p) e -> p k e", p=P)
    w_up_v = w_up[0].rearrange("(k p) e -> p k e", p=P)
    w_out_v = w_out[0].rearrange("(k p) e -> k p e", p=P)
    w_down_v = w_down[0].rearrange("(f p) e -> f p e", p=P)

    ctx = ExitStack()
    with ctx:
        def sem(name):
            return ctx.enter_context(nc.semaphore(name))

        base = (nc.sbuf_base + 31) // 32 * 32
        SBUF_END = nc.sbuf_usable_end
        top = [base]

        def place(name, shape, dt, at=None):
            size = 2 if dt == BF16 else 4
            for n in shape[1:]:
                size *= n
            size = (size + 31) // 32 * 32
            if at is None:
                at = top[0]
                top[0] += size
            return nc.alloc_sbuf_tensor_at(name, shape, dt, offset=at), at + size

        ident, _ = place("ident", [P, P], FP32)
        ones, _ = place("ones", [P, 1], FP32)
        coef, _ = place("coef", [P, 2 * P], FP32)
        neghalf, _ = place("neghalf", [P, 16], FP32)
        eps, _ = place("eps", [P, 16], FP32)
        x_ss, _ = place("x_ss", [P, 2], FP32)
        x_r, _ = place("x_r", [P, 2], FP32)
        h_ss, _ = place("h_ss", [P, 2], FP32)
        h_r, _ = place("h_r", [P, 2], FP32)
        attn_ss, _ = place("attn_ss", [P, NT], FP32)
        attn_r, _ = place("attn_r", [P, NT], FP32)
        conv_ss, _ = place("conv_ss", [P, NT], FP32)
        conv_r, _ = place("conv_r", [P, NT], FP32)
        junk, _ = place("junk", [P, D], BF16)
        gain, _ = place("gain", [P, D], FP32)
        STG = 3
        stage = [place(f"stage{i}", [P, D], FP32)[0] for i in range(STG)]
        hT_hi, _ = place("hT_hi", [P, KT, SEQ], FP32R)
        hT_lo_at = top[0]
        hT_lo, _ = place("hT_lo", [P, KT, SEQ], FP32R)
        wq_raw, _ = place("wq_raw", [P, KT, QKV], FP32, hT_lo_at)
        shared = top[0]
        wq_hi, a = place("wq_hi", [P, KT, QKV], FP32R, shared)
        wq_lo, a = place("wq_lo", [P, KT, QKV], FP32R, a)
        hb_hi, hb_lo = [None] * 2, [None] * 2
        for i in range(2):
            hb_hi[i], a = place(f"hb_hi{i}", [P, KT, P], FP32R, a)
            hb_lo[i], a = place(f"hb_lo{i}", [P, KT, P], FP32R, a)
        wo_hi, b = place("wo_hi", [P, KT, D], FP32R, shared)
        wo_lo, b = place("wo_lo", [P, KT, D], FP32R, b)
        region_v = max(a, b)
        wu_hi, wu_lo, wu_at = [None] * 4, [None] * 4, [None] * 4
        a = shared
        for i in range(4):
            wu_at[i] = a
            wu_hi[i], a = place(f"wu_hi{i}", [P, KT, P], FP32R, a)
            wu_lo[i], a = place(f"wu_lo{i}", [P, KT, P], FP32R, a)
        wd_hi, a = place("wd_hi", [P, 2, D], FP32R, a)
        wd_lo, a = place("wd_lo", [P, 2, D], FP32R, a)
        act_hi, a = place("act_hi", [P, 2, SEQ], FP32R, a)
        act_lo, a = place("act_lo", [P, 2, SEQ], FP32R, a)
        assert a <= region_v
        act_hi_last = [place(f"act_hi_last{k}", [P, SEQ], FP32R, wu_at[2 * k])[0] for k in range(2)]
        act_lo_last = [place(f"act_lo_last{k}", [P, SEQ], FP32R, wu_at[2 * k] + 4 * SEQ)[0] for k in range(2)]
        wd_hi_last = [place(f"wd_hi_last{k}", [P, D], FP32R, wu_at[2 * k + 1])[0] for k in range(2)]
        wd_lo_last = [place(f"wd_lo_last{k}", [P, D], FP32R, wu_at[2 * k + 1] + 4 * D)[0] for k in range(2)]
        b0_hi, a = place("b0_hi", [P, KT, P], FP32R, shared + 6 * 4 * D)
        b0_lo, a = place("b0_lo", [P, KT, P], FP32R, a)
        wc_hi, wc_lo = [None] * 3, [None] * 3
        wc_hi[0], a = place("wc_hi0", [P, KT, P], FP32R, region_v)
        wc_lo[0], a = place("wc_lo0", [P, KT, P], FP32R, a)
        xin, xin_at = [None] * 2, a
        xin[0], a = place("xin0", [P, D], FP32, a)
        xin[1], a = place("xin1", [P, D], FP32, a)
        prob, a = place("prob", [P, NQ, 2 * P], FP32, a)
        probT, a = place("probT", [P, 4, GROUP * P], FP32, a)
        qk_sqr, a = place("qk_sqr", [P, NQ + NKV, HD], FP32, a)
        qn, a = place("qn", [P, GROUP + 1, P], FP32, a)
        qT_hi, a = place("qT_hi", [P, GROUP, P], FP32R, a)
        qT_lo, a = place("qT_lo", [P, GROUP, P], FP32R, a)
        kT_hi, a = place("kT_hi", [P, 2, P], FP32R, a)
        kT_lo, a = place("kT_lo", [P, 2, P], FP32R, a)
        v_new, a = place("v_new", [P, 2, NKV * HD], FP32, a)
        v_win, a = place("v_win", [P, 2, NKV * HD], FP32, a)
        attnT, a = place("attnT", [P, GROUP, P], FP32, a)
        attn_sqr, a = place("attn_sqr", [P, GROUP, P], FP32, a)
        attn_sqf, a = place("attn_sqf", [P, P], FP32, a)
        qk_gain, a = place("qk_gain", [P, 2, HD], FP32, a)
        mask, a = place("mask", [P, 3 * P], FP32, a)
        sink, a = place("sink", [P, NQ], FP32, a)
        qk_ss, a = place("qk_ss", [P, NQ + NKV], FP32, a)
        qk_r, a = place("qk_r", [P, NQ + NKV], FP32, a)
        mx, a = place("mx", [P, NQ], FP32, a)
        top_score, a = place("top_score", [P, NQ], FP32, a)
        negm, a = place("negm", [P, NQ], FP32, a)
        sd, a = place("sd", [P, NQ], FP32, a)
        es, a = place("es", [P, NQ], FP32, a)
        den, a = place("den", [P, NQ], FP32, a)
        dsum, a = place("dsum", [P, NQ], FP32, a)
        rden, a = place("rden", [P, NQ], FP32, a)
        rows, a = place("rows", [P, 2 * P], FP32, a)
        assert a <= SBUF_END
        wc_hi[1], a = place("wc_hi1", [P, KT, P], FP32R, xin_at)
        wc_lo[1], a = place("wc_lo1", [P, KT, P], FP32R, a)
        wc_hi[2], a = place("wc_hi2", [P, KT, P], FP32R, a)
        wc_lo[2], a = place("wc_lo2", [P, KT, P], FP32R, a)
        c_sb, a = place("c_sb", [P, SEQ], FP32, a)
        cu, a = place("cu", [P, TAPS - 1 + SEQ], FP32, a)
        y, a = place("y", [P, SEQ], FP32, a)
        ysq, a = place("ysq", [P, SEQ], FP32, a)
        ysum_at = a
        ysum, a = place("ysum", [P, SEQ], FP32, a)
        X, d = place("X", [P, NT, D], FP32, region_v)
        mix_hi, mix_lo = [None] * 2, [None] * 2
        mix_hi[1], e = place("mix_hi1", [P, KT, P], FP32R, d)
        mix_lo[1], e = place("mix_lo1", [P, KT, P], FP32R, e)
        mixb, a = place("mixb", [P, KT, P], FP32, max(a, e))
        mix_hi[0], a = place("mix_hi0", [P, KT, P], FP32R, a)
        mix_lo[0], a = place("mix_lo0", [P, KT, P], FP32R, a)
        assert a <= SBUF_END and ysum_at >= e
        xn, _ = place("xn", [P, D], FP32, ysum_at)
        gated, e = place("gated", [P, 2, SEQ], FP32, d)
        z, e = place("z", [P, TAPS - 1 + SEQ], FP32, e)
        acc_g, e = place("acc_g", [P, SEQ], FP32, e)
        acc_u, e = place("acc_u", [P, SEQ], FP32, e)
        assert e <= SBUF_END

        mix_dram = nc.dram_tensor("mix_dram", [KT, P, SEQ], FP32, kind="Internal").ap()

        bank = [ctx.enter_context(nc.psum_tensor(f"bank{i}", [P, HALF], FP32)) for i in range(8)]
        Q = bank[0:2]
        TR = bank[2:4]
        A = bank[4:8]

        const_in = sem("const_in")
        gain_in = sem("gain_in")
        const_set = sem("const_set")
        act_ready = sem("act_ready")
        warmed_up = sem("warmed_up")
        wq_in = [sem(f"wq_in{i}") for i in range(KT // 2)]
        wq_hi_out = sem("wq_hi_out")
        wq_lo_out = sem("wq_lo_out")
        stage_in = [sem(f"stage_in{i}") for i in range(STG)]
        stage_hi = sem("stage_hi")
        stage_lo = sem("stage_lo")
        x_in = [sem(f"x_in{i}") for i in range(2)]
        x_turned = sem("x_turned")
        qk_turned = sem("qk_turned")
        prob_turned = sem("prob_turned")
        coef_turned = sem("coef_turned")
        h_turned = sem("h_turned")
        coef_out = sem("coef_out")
        coef_set = sem("coef_set")
        x_sq = sem("x_sq")
        x_rms = sem("x_rms")
        x_normed = sem("x_normed")
        h_hi = sem("h_hi")
        h_lo = sem("h_lo")
        h_kept = sem("h_kept")
        qkv_done = sem("qkv_done")
        qk_sq = sem("qk_sq")
        v_read = sem("v_read")
        v_slot = sem("v_slot")
        qk_sum = sem("qk_sum")
        qk_rms = sem("qk_rms")
        qk_normed = sem("qk_normed")
        qkT_hi_out = sem("qkT_hi_out")
        qkT_lo_out = sem("qkT_lo_out")
        scores_done = sem("scores_done")
        masked = sem("masked")
        scores_seen = sem("scores_seen")
        shift = sem("shift")
        exps = sem("exps")
        denom = sem("denom")
        prob_divided = sem("prob_divided")
        probT_out = sem("probT_out")
        pv_done = sem("pv_done")
        attn_sq = sem("attn_sq")
        attn_folded = sem("attn_folded")
        attn_sums_done = sem("attn_sums_done")
        attn_sum_out = sem("attn_sum_out")
        attnT_out = sem("attnT_out")
        mix_stored = sem("mix_stored")
        attn_rms = sem("attn_rms")
        unit_done = sem("unit_done")
        c_out = sem("c_out")
        cu_pad = sem("cu_pad")
        cu_out = sem("cu_out")
        y_chain = sem("y_chain")
        ysq_out = sem("ysq_out")
        y_stored = sem("y_stored")
        ysum_out = sem("ysum_out")
        css_done = sem("css_done")
        css_sum = sem("css_sum")
        conv_rms = sem("conv_rms")
        X_in = sem("X_in")
        X_late_in = sem("X_late_in")
        mixb_in = sem("mixb_in")
        mix_hi_out = sem("mix_hi_out")
        mix_lo_out = sem("mix_lo_out")
        proj_done = sem("proj_done")
        X_added = sem("X_added")
        h_sq = sem("h_sq")
        h_rms = sem("h_rms")
        h_normed = sem("h_normed")
        h2_hi = sem("h2_hi")
        h2_lo = sem("h2_lo")
        up_done = sem("up_done")
        z_pad = sem("z_pad")
        z_out = sem("z_out")
        conv_chain = sem("conv_chain")
        silu_out = sem("silu_out")
        gated_out = sem("gated_out")
        act_hi_out = sem("act_hi_out")
        act_lo_out = sem("act_lo_out")
        down_filled = sem("down_filled")
        down_added = sem("down_added")
        out_stored = sem("out_stored")

        block = ctx.enter_context(nc.Block())

        LAST = NT - 1
        WARM_UP = 24

        def is_(t, *values):
            return isinstance(t, int) and t in values

        def from_(t, first):
            return not isinstance(t, int) or t >= first

        def qkv_banks(t):
            return A[2:4] if is_(t, 0) else Q

        def qk_banks(t):
            return A[0:2] if is_(t, 0) else TR

        def output_bank(b):
            return TR[0] if is_(b, LAST) else A[0]

        def prob_fill(b, f):
            return 4 * b + f - 1

        class Load:

            def __init__(self, c, i=0, step=0):
                self.n = step * i + c
                self.buf = stage[c % STG]
                self.sem = stage_in[c % STG]
                self.uses = (step // STG) * i + c // STG

        WO_STEP = 3
        N_UNIT0 = 0
        N_C = N_UNIT0 + 3
        N_F0 = N_C + 3 * (NC - 1) + KT
        N_F = N_F0 + 4

        def unit0_load(s):
            return Load(N_UNIT0 + s)

        def unit_load(j, s):
            return Load(N_C + s, j, 3 + WO_STEP)

        def wo_load(j, m):
            return Load(N_C + 3 + m, j, 3 + WO_STEP)

        def wo_tiles(j):
            return KT - 2 * WO_STEP if is_(j, 2) else WO_STEP

        def up0_load(s):
            return Load(N_F0 + s)

        def up_load(i, s):
            return Load(N_F + s, i, 6)

        def down_load(i, k):
            return Load(N_F + 4 + k - (4 if is_(i, NG - 1) else 0), i, 6)

        def staged(ld, like):
            src = ld.buf[:, 0:like.free_size()]
            return src if len(like.shape) == 2 else src.rearrange("p (a b) -> p a b", b=like.shape[2])

        def split_hi(act, ld, hi, scale=1.0):
            act.wait_ge(ld.sem, 16 * (ld.uses + 1))
            act.activation(hi, staged(ld, hi), ACT.Copy, scale=scale).then_inc(stage_hi, 1)

        def split_lo(dve, ld, hi, lo, scale=1.0):
            dve.wait_ge(ld.sem, 16 * (ld.uses + 1))
            dve.wait_ge(stage_hi, ld.n + 1)
            if isinstance(scale, float):
                dve.tensor_tensor(lo, staged(ld, hi), hi.bitcast(FP32), ALU.subtract).then_inc(stage_lo, 1)
            else:
                dve.scalar_tensor_tensor(lo, staged(ld, hi), scale, hi.bitcast(FP32), ALU.mult,
                                         ALU.subtract).then_inc(stage_lo, 1)

        def down_operands(i):
            if is_(i, NG - 1):
                return tuple([t_[k][:, :] for k in range(2)]
                             for t_ in (act_hi_last, act_lo_last, wd_hi_last, wd_lo_last))
            return tuple([t_[:, k, :] for k in range(2)] for t_ in (act_hi, act_lo, wd_hi, wd_lo))

        def ffn_tap(tap, f):
            return ds(tap * 2 * NF + f, 1)

        MIX0 = TAPS * 2 * NF

        def mix_tap(tap, j):
            return ds(MIX0 + tap * NC + j, 1)

        OUT0 = MIX0 + TAPS * NC

        @block.sync
        def _(sp):
            def load_x(t):
                if t >= 2:
                    sp.wait_ge(x_turned, 2 * t - 2)
                sp.dma_start(xin[t % 2][:, :], x_t[t]).then_inc(x_in[t % 2], 16)

            def load(ld, dst, src):
                if not (isinstance(ld.n, int) and ld.n < STG):
                    sp.wait_ge(stage_lo, ld.n - STG + 1)
                sp.dma_start(dst, src).then_inc(ld.sem, 16)

            def load_unit(ld, view, col):
                load(ld, ld.buf[:, :].rearrange("p (k e) -> p k e", e=P), view[:, :, ds(col, P)])

            def load_row(ld, view, row):
                load(ld, ld.buf[:, :], view[ds(row, 1)].rearrange("a p e -> (a p) e"))

            def conv_col(s):
                return QKV + (1, 2, 0)[s] * CW

            def up_col(s):
                return (s % 2) * FF + (s // 2) * P

            load_x(0)
            for k in range(0, KT, 2):
                sp.dma_start(wq_raw[:, k:k + 2, :], w_in_v[:, k:k + 2, 0:QKV]).then_inc(wq_in[k // 2], 16)
            load_x(1)
            sp.dma_start(qk_gain[:, 0, :], q_norm_w.to_broadcast([P, HD])).then_inc(const_in, 16)
            sp.dma_start(qk_gain[:, 1, :], k_norm_w.to_broadcast([P, HD])).then_inc(const_in, 16)
            sp.dma_start(sink[:, :], sinks.to_broadcast([P, NQ])).then_inc(const_in, 16)
            sp.wait_ge(const_set, 6)
            fcw = ffn_conv_w[0].rearrange("t (f p) -> (t f) p", p=P)
            R = TAPS * 2 * NF - P
            sp.dma_start(rows[:, 0:P], fcw[0:P, :]).then_inc(const_in, 16)
            sp.dma_start(rows[0:R, P:2 * P], fcw[P:P + R, :]).then_inc(const_in, 16)
            sp.dma_start(rows[R:R + TAPS * NC, P:2 * P],
                         conv_mix_w[0].rearrange("t (f p) -> (t f) p", p=P)).then_inc(const_in, 16)
            R += TAPS * NC
            sp.dma_start(rows[R:R + 4, P:2 * P],
                         attn_out_norm_w[0].rearrange("(f p) -> f p", p=P)).then_inc(const_in, 16)
            sp.dma_start(rows[R + 4:R + 8, P:2 * P],
                         conv_out_norm_w[0].rearrange("(f p) -> f p", p=P)).then_inc(const_in, 16)
            for s in range(3):
                load_unit(unit0_load(s), w_in_v, conv_col(s))
            sp.wait_ge(wq_lo_out, KT)

            def keep_h(t):
                sp.wait_ge(h_lo, 2 * t + 2)
                sp.dma_start(hT_hi[:, :, ds(P * t, P)].bitcast(FP32),
                             hb_hi[t % 2][:, :, :].bitcast(FP32)).then_inc(h_kept, 16)
                sp.dma_start(hT_lo[:, :, ds(P * t, P)].bitcast(FP32),
                             hb_lo[t % 2][:, :, :].bitcast(FP32)).then_inc(h_kept, 16)

            mix_heads = mix_dram[0:AW // P].rearrange("k (a d) t -> d (k a) t", d=HD)

            def store_attn(b):
                sp.wait_ge(attnT_out, b + 1)
                for kv in range(NKV):
                    sp.dma_start(mix_heads[:, GROUP * kv:GROUP * (kv + 1), P * b:P * (b + 1)],
                                 attnT[HD * kv:HD * (kv + 1), :, :]).then_inc(mix_stored, 16)

            for t in range(NT):
                keep_h(t)
                if t + 2 < NT:
                    load_x(t + 2)
                if t >= 3:
                    store_attn(t - 3)
            for b in range(LAST - 2, NT):
                store_attn(b)

            def store_y(j):
                sp.wait_ge(y_chain, 5 * j + 5)
                sp.dma_start(mix_dram[ds(AW // P + j, 1)].rearrange("a p t -> (a p) t"),
                             y[:, :]).then_inc(y_stored, 16)

            def load_conv_weights(j):
                for s in range(3):
                    load_unit(unit_load(j, s), w_in_v, conv_col(s) + P * (j + 1))
                for m in range(wo_tiles(j)):
                    load_row(wo_load(j, m), w_out_v, WO_STEP * j + m)

            with sp.Fori(0, 2) as j:
                load_conv_weights(j)
                store_y(j)
            load_conv_weights(2)
            store_y(2)
            for s in range(3):
                load_unit(up0_load(s), w_up_v, up_col(s))

            def load_mix(t, tiles):
                sp.dma_start(mixb[:, 0:tiles, :], mix_dram[0:tiles, :, ds(P * t, P)].rearrange(
                    "k p t -> p k t")).then_inc(mixb_in, 16)

            sp.wait_ge(mix_stored, 32 * NT)
            sp.wait_ge(y_stored, 16 * (NC - 1))
            load_mix(0, KT - 1)
            for t in range(4):
                sp.wait_ge(unit_done, 3 * (NC - 1) + t // 2 + 1)
                sp.dma_start(X[:, t, :], x_t[t]).then_inc(X_in, 16)
            store_y(NC - 1)
            for t in range(4, NT):
                if t == 6:
                    sp.wait_ge(y_stored, 16 * NC)
                    sp.wait_ge(mix_lo_out, 2)
                    load_mix(1, KT)
                sp.dma_start(X[:, t, :], x_t[t]).then_inc(X_late_in, 16)
            with sp.Fori(2, NT) as t:
                sp.wait_ge(mix_lo_out, t + 1)
                load_mix(t, KT)
            load_unit(up0_load(3), w_up_v, up_col(3))

            def load_down(i):
                for k in range(2):
                    load_row(down_load(i, k), w_down_v, 2 * i + k)

            def load_up(i):
                for s in range(4):
                    load_unit(up_load(i, s), w_up_v, up_col(s) + 2 * P * (i + 1))

            load_up(0)
            with sp.Fori(1, NG - 1) as i:
                load_down(i - 1)
                load_up(i)
            load_down(NG - 2)
            load_down(NG - 1)
            with sp.Fori(0, LAST) as t:
                sp.wait_ge(down_added, 2 * NT * (NG - 1) + 2 * t + 2)
                sp.dma_start(out_t[ds(t, 1)].rearrange("a p d -> (a p) d"),
                             X[:, ds(t, 1), :].rearrange("p a d -> p (a d)")).then_inc(out_stored, 16)
            for n in range(2):
                half = slice(n * HALF, (n + 1) * HALF)
                sp.wait_ge(down_added, 2 * NT * NG - 1 + n)
                sp.dma_start(out_t[LAST, :, half], X[:, LAST, half]).then_inc(out_stored, 16)
            sp.wait_ge(out_stored, 16 * (NT + 1))

        @block.gpsimd
        def _(pool):
            pool.memset(neghalf[:, :], -0.5).then_inc(const_set, 1)
            pool.memset(eps[:, :], EPS).then_inc(const_set, 1)
            pool.memset(ones[:, :], 1.0).then_inc(const_set, 1)
            pool.memset(ident[:, :], 0.0).then_inc(const_set, 1)
            pool.memset(mask[:, :], 0.0).then_inc(const_set, 1)
            pool.memset(rows[:, :], 0.0).then_inc(const_set, 1)
            pool.wait_ge(const_set, 6)
            pool.affine_select(out=ident[:, :], in_=ident[:, :], compare_op=ALU.not_equal, fill=1.0,
                               base=0, pattern=[[-1, P]], channel_multiplier=1).then_inc(const_set, 1)
            for s in (0, 2):
                pool.affine_select(out=mask[:, s * P:(s + 1) * P], in_=mask[:, s * P:(s + 1) * P],
                                   compare_op=ALU.is_ge, fill=NEG, base=0, pattern=[[-1, P]],
                                   channel_multiplier=1).then_inc(const_set, 1)
            pool.affine_select(out=mask[:, P:2 * P], in_=mask[:, P:2 * P], compare_op=ALU.is_gt, fill=NEG,
                               base=0, pattern=[[1, P]], channel_multiplier=-1).then_inc(const_set, 1)

            def power(dst, mean, width, done, before):
                pool.tensor_tensor(dst, mean, eps[:, 0:width], ALU.add).then_inc(done, 1)
                pool.wait_ge(done, before + 1)
                pool.tensor_tensor(dst, dst, neghalf[:, 0:width], ALU.pow).then_inc(done, 1)

            def x_power(t, par):
                pool.wait_ge(x_sq, t + 1)
                if not is_(t, 0, 1):
                    pool.wait_ge(x_normed, t - 1)
                power(x_r[:, par:par + 1], x_ss[:, par:par + 1], 1, x_rms, 2 * t)

            def h_power(t, par):
                pool.wait_ge(h_sq, t + 1)
                if not is_(t, 0, 1):
                    pool.wait_ge(h_normed, t - 1)
                power(h_r[:, par:par + 1], h_ss[:, par:par + 1], 1, h_rms, 2 * t)

            def qk_power(t):
                pool.wait_ge(qk_sum, t + 1)
                if not is_(t, 0):
                    pool.wait_ge(qk_normed, 4 * t - 2)
                power(qk_r[:, :], qk_ss[:, :], NQ + NKV, qk_rms, 2 * t)

            def step(t, par):
                x_power(t + 1, 1 - par)
                qk_power(t)

            x_power(0, 0)
            step(0, 0)
            step(1, 1)
            step(2, 0)
            with pool.Fori(0, 2) as tt:
                step(2 * tt + 3, 1)
                step(2 * tt + 4, 0)
            qk_power(LAST)
            pool.wait_ge(attn_sum_out, NT)
            pool.tensor_scalar(attn_ss[:, :], attn_ss[:, :], 1.0 / AW, None, ALU.mult).then_inc(attn_rms, 1)
            pool.wait_ge(attn_rms, 1)
            power(attn_r[:, :], attn_ss[:, :], NT, attn_rms, 1)
            pool.wait_ge(css_sum, 1)
            pool.tensor_scalar(conv_ss[:, :], conv_ss[:, :], 1.0 / CW, None, ALU.mult).then_inc(conv_rms, 1)
            pool.wait_ge(conv_rms, 1)
            power(conv_r[:, :], conv_ss[:, :], NT, conv_rms, 1)
            h_power(0, 0)
            h_power(1, 1)
            with pool.Fori(1, NT // 2) as tt:
                h_power(2 * tt, 0)
                h_power(2 * tt + 1, 1)

        @block.scalar
        def _(act):
            act.dma_start(gain[:, :], attn_norm_w.to_broadcast([P, D])).then_inc(gain_in, 16)
            act.wait_ge(const_set, 2)
            act.activation(junk[:, 0:1], eps[:, 0:1], ACT.Exp).then_inc(act_ready, 1)

            def square_sum(src, width, total, done, scale=1.0):
                act.activation(junk[:, 0:width], src, ACT.Square, scale=scale, accum_out=total).then_inc(done, 1)

            def x_square(t, par, uses):
                act.wait_ge(x_in[par], 16 * uses + 16)
                if is_(t, 0):
                    act.wait_ge(act_ready, 1)
                else:
                    act.wait_ge(x_sq, t)
                if not is_(t, 0, 1):
                    act.wait_ge(x_rms, 2 * t - 2)
                square_sum(xin[par][:, :], D, x_ss[:, par:par + 1], x_sq, float(D) ** -0.5)

            def h_split_hi(t, par):
                for i in range(2):
                    act.wait_ge(x_turned, 2 * t + i + 1)
                    if from_(t, 2):
                        act.wait_ge(qkv_done, t - 1)
                        act.wait_ge(h_kept, 32 * (t - 1))
                    act.activation(hb_hi[par][:, 4 * i:4 * i + 4, :],
                                   TR[i][:, :].rearrange("p (k t) -> p k t", t=P), ACT.Copy).then_inc(h_hi, 1)

            def qkv_read(t, par):
                act.wait_ge(qkv_done, t + 1)
                if not is_(t, 0):
                    act.wait_ge(qk_sum, t)
                q_bank, kv_bank = qkv_banks(t)
                act.activation(qk_sqr[:, NQ:, :], kv_bank[:, 0:NKV * HD].rearrange("p (h d) -> p h d", d=HD),
                               ACT.Square, scale=float(HD) ** -0.5).then_inc(qk_sq, 1)
                act.activation(qk_sqr[:, 0:NQ, :], q_bank[:, :].rearrange("p (h d) -> p h d", d=HD),
                               ACT.Square, scale=float(HD) ** -0.5).then_inc(qk_sq, 1)
                if from_(t, 2):
                    act.wait_ge(v_slot, t - 1)
                act.activation(v_new[:, par, :], kv_bank[:, NKV * HD:2 * NKV * HD], ACT.Copy).then_inc(v_read, 1)

            def qkT_hi(t, par):
                for i, (dst, width) in enumerate(((qT_hi[:, :, :], AW), (kT_hi[:, par, :], P))):
                    act.wait_ge(qk_turned, 2 * t + i + 1)
                    if not is_(t, 0):
                        act.wait_ge(scores_done, 2 * t)
                    src = qk_banks(t)[i][:, 0:width]
                    act.activation(dst, src.rearrange("p (h t) -> p h t", t=P) if i == 0 else src,
                                   ACT.Copy).then_inc(qkT_hi_out, 1)

            def v_place(b, par):
                act.wait_ge(v_read, b + 1)
                if not is_(b, 0):
                    act.wait_ge(pv_done, 2 * b)
                act.activation(v_win[:, par, :], v_new[:, par, :], ACT.Copy).then_inc(v_slot, 1)

            def probT_copy(b, f):
                act.wait_ge(prob_turned, prob_fill(b, f))
                if not is_(b, 0):
                    act.wait_ge(pv_done, 2 * b)
                act.activation(probT[:, 2 * (f - 2) if is_(b, 0) else f, :], TR[f % 2][:, :],
                               ACT.Copy).then_inc(probT_out, 1)

            def softmax_exp(b, g, keys):
                act.wait_ge(shift, 6 * b + 3 * g + 3)
                if not is_(b, 0):
                    act.wait_ge(denom, 4 * b + 2 * g - 3)
                for h in range(4 * g, 4 * g + 4):
                    act.activation(prob[:, h, 0:keys], prob[:, h, 0:keys], ACT.Exp,
                                   bias=negm[:, h:h + 1], accum_out=den[:, h:h + 1])
                act.activation(es[:, 4 * g:4 * g + 4], sd[:, 4 * g:4 * g + 4], ACT.Exp).then_inc(exps, 1)

            def attn_read(b):
                act.wait_ge(pv_done, 2 * b + 2)
                if not is_(b, 0):
                    act.wait_ge(attn_folded, b)
                    act.wait_ge(mix_stored, 32 * b)
                src = output_bank(b)[:, :].rearrange("p (h t) -> p h t", t=P)
                act.activation(attn_sqr[:, :, :], src, ACT.Square).then_inc(attn_sq, 1)
                act.activation(attnT[:, :, :], src, ACT.Copy).then_inc(attnT_out, 1)

            def step(t, par, x_uses):
                v_place(t - 2, par)
                if is_(t, LAST):
                    act.wait_ge(x_turned, 2 * NT)
                    split_hi(act, unit0_load(0), wc_hi[0][:, :, :])
                else:
                    x_square(t + 1, 1 - par, x_uses)
                qkv_read(t, par)
                for f in range(2 if is_(t, 2) else 0, 4):
                    probT_copy(t - 2, f)
                if is_(t, LAST):
                    split_hi(act, unit0_load(1), wc_hi[1][:, :, :])
                else:
                    h_split_hi(t + 1, 1 - par)
                for g in range(2):
                    softmax_exp(t - 1, g, 2 * P)
                attn_read(t - 2)
                qkT_hi(t, par)

            x_square(0, 0, 0)
            h_split_hi(0, 0)
            for k in range(KT):
                act.wait_ge(wq_in[k // 2], 16)
                act.activation(wq_hi[:, k, :], wq_raw[:, k, :], ACT.Copy).then_inc(wq_hi_out, 1)
            x_square(1, 1, 0)
            h_split_hi(1, 1)
            qkv_read(0, 0)
            x_square(2, 0, 1)
            qkv_read(1, 1)
            qkT_hi(0, 0)
            h_split_hi(2, 0)
            for g in range(2):
                softmax_exp(0, g, P)
            qkT_hi(1, 1)
            step(2, 0, 1)
            with act.Fori(0, 2) as tt:
                step(2 * tt + 3, 1, tt + 2)
                step(2 * tt + 4, 0, tt + 2)
            step(LAST, 1, 0)
            act.wait_ge(qkv_done, NT)
            split_hi(act, unit0_load(2), b0_hi[:, :, :])
            v_place(LAST - 1, 0)
            for f in range(4):
                probT_copy(LAST - 1, f)
            for g in range(2):
                softmax_exp(LAST, g, 2 * P)
            attn_read(LAST - 1)
            v_place(LAST, 1)
            for f in range(4):
                probT_copy(LAST, f)
            attn_read(LAST)

            def conv_iteration(j, last):
                for hf in range(NH):
                    act.wait_ge(unit_done, 3 * j + 1)
                    if not is_(j, 0):
                        act.wait_ge(cu_out, NH * j)
                    act.activation(c_sb[:, hf * HALF:(hf + 1) * HALF], Q[hf][:, :], ACT.Copy).then_inc(c_out, 1)
                if not last:
                    for s in range(3):
                        act.wait_ge(unit_done, 3 * j + s + 1)
                        split_hi(act, unit_load(j, s), wc_hi[s][:, :, :])
                    for m in range(wo_tiles(j)):
                        k = WO_STEP * j + m
                        split_hi(act, wo_load(j, m), wo_hi[:, ds(k, 1), :].rearrange("p a e -> p (a e)"),
                                 coef[:, ds(OUT0 + k, 1)])
                else:
                    act.wait_ge(mixb_in, 16)
                    act.activation(mix_hi[0][:, 0:KT - 1, :], mixb[:, 0:KT - 1, :], ACT.Copy).then_inc(mix_hi_out, 1)
                act.wait_ge(y_chain, 5 * j + 5)
                if last:
                    act.activation(mix_hi[0][:, KT - 1, :], y[:, 0:P], ACT.Copy).then_inc(mix_hi_out, 1)
                if from_(j, 2):
                    act.wait_ge(ysum_out, j - 1)
                act.activation((ysum if is_(j, 0) else ysq)[:, :], y[:, :], ACT.Square).then_inc(ysq_out, 1)

            act.wait_ge(coef_out, 2)
            act.wait_ge(mix_stored, 32 * NT)
            for j in range(3):
                conv_iteration(j, False)
            act.wait_ge(x_normed, NT)
            act.dma_start(gain[:, :], ffn_norm_w.to_broadcast([P, D])).then_inc(gain_in, 16)
            conv_iteration(3, True)

            def mix_split_hi(t, par):
                act.wait_ge(mixb_in, 16 * t + 16)
                if is_(t, 1):
                    act.wait_ge(ysum_out, NC - 1)
                else:
                    act.wait_ge(proj_done, 2 * t - 2)
                act.activation(mix_hi[par][:, :, :], mixb[:, :, :], ACT.Copy).then_inc(mix_hi_out, 1)

            def h_square(t, par):
                act.wait_ge(X_added, 4 * t + 4)
                act.wait_ge(x_sq, NT)
                if not is_(t, 0):
                    act.wait_ge(h_sq, t)
                if not is_(t, 0, 1):
                    act.wait_ge(h_rms, 2 * t - 2)
                square_sum(X[:, ds(t, 1), :].rearrange("p a d -> p (a d)"), D, h_ss[:, par:par + 1], h_sq, float(D) ** -0.5)

            def h2_split_hi(t):
                for i in range(2):
                    act.wait_ge(h_turned, 2 * t + i + 1)
                    act.activation(hT_hi[:, 4 * i:4 * i + 4, ds(P * t, P)],
                                   TR[i][:, :].rearrange("p (k t) -> p k t", t=P), ACT.Copy).then_inc(h2_hi, 1)

            def d_step(t, par):
                if not is_(t, 0):
                    h_square(t - 1, 1 - par)
                if not is_(t, LAST):
                    mix_split_hi(t + 1, 1 - par)
                if not is_(t, 0):
                    h2_split_hi(t - 1)

            d_step(0, 0)
            d_step(1, 1)
            d_step(2, 0)
            with act.Fori(0, 2) as tt:
                d_step(2 * tt + 3, 1)
                d_step(2 * tt + 4, 0)
            d_step(LAST, 1)
            act.wait_ge(proj_done, 2 * NT - 1)
            for s in range(2):
                split_hi(act, up0_load(s), wu_hi[s][:, :, :])
            h_square(LAST, 1)
            h2_split_hi(LAST)
            act.wait_ge(proj_done, 2 * NT)
            for s in range(2, 4):
                split_hi(act, up0_load(s), wu_hi[s][:, :, :])

            def down_operands_hi(i):
                if is_(i, 0):
                    act.wait_ge(proj_done, 2 * NT)
                elif is_(i, NG - 1):
                    act.wait_ge(up_done, 4 * NG)
                else:
                    act.wait_ge(down_filled, 2 * NT * i)
                a_hi, _, w_hi, _ = down_operands(i)
                for k in range(2):
                    act.wait_ge(gated_out, 2 * i + k + 1)
                    act.activation(a_hi[k], gated[:, k, :], ACT.Copy).then_inc(act_hi_out, 1)
                for k in range(2):
                    split_hi(act, down_load(i, k), w_hi[k])

            def up_weights_hi(i, s):
                act.wait_ge(up_done, 4 * i + s + 1)
                split_hi(act, up_load(i, s), wu_hi[s][:, :, :])

            def ffn_iteration(i, first, last):
                for s in range(4):
                    act.wait_ge(up_done, 4 * i + s + 1)
                    if not (first and s == 0):
                        act.wait_ge(conv_chain, 12 * i + 3 * s)
                    for hf in range(NH):
                        act.activation(z[:, TAPS - 1 + hf * HALF:TAPS - 1 + (hf + 1) * HALF],
                                       (Q, A)[s % 2][hf][:, :], ACT.Copy).then_inc(z_out, 1)
                    if s == 0 and not first:
                        down_operands_hi(i - 1)
                    if s >= 1 and not last:
                        up_weights_hi(i, s - 1)
                    if s % 2 == 0:
                        act.wait_ge(conv_chain, 12 * i + 3 * s + 3)
                        act.activation(acc_g[:, :], acc_g[:, :], ACT.Silu).then_inc(silu_out, 1)
                if not last:
                    up_weights_hi(i, 3)

            act.wait_ge(z_pad, 1)
            ffn_iteration(0, True, False)
            ffn_iteration(1, False, False)
            with act.Fori(2, NG - 1) as i:
                ffn_iteration(i, False, False)
            ffn_iteration(NG - 1, False, True)
            down_operands_hi(NG - 1)

        @block.tensor
        def _(pe):
            def keep_warm():
                for _ in range(WARM_UP):
                    mm = pe.transpose(A[0][:, 0:P], ident[:, :], ident[:, :])
                mm.then_inc(warmed_up, 1)

            def x_transpose(t, par):
                pe.wait_ge(x_normed, t + 1)
                for i in range(2):
                    if is_(t, 1, 2):
                        pe.wait_ge(h_lo, 2 * t - 1 + i)
                    elif from_(t, 3):
                        pe.wait_ge(probT_out, prob_fill(t - 3, 2 + i))
                    for k in range(4):
                        mm = pe.transpose(TR[i][:, k * P:(k + 1) * P],
                                          xin[par][:, (4 * i + k) * P:(4 * i + k + 1) * P], ident[:, :])
                    mm.then_inc(x_turned, 1)

            def qkv(t, par):
                q_bank, kv_bank = qkv_banks(t)
                pe.wait_ge(h_lo, 2 * t + 2)
                if from_(t, 2):
                    pe.wait_ge(qk_normed, 4 * t - 2)
                    pe.wait_ge(v_read, t)
                for k in range(KT):
                    if is_(t, 0):
                        pe.wait_ge(wq_lo_out, k + 1)
                    for h, w, st in ((hb_hi, wq_hi, k == 0), (hb_hi, wq_lo, False), (hb_lo, wq_hi, False)):
                        end = k == KT - 1 and h is hb_lo
                        pe.matmul(q_bank[:, :], h[par][:, k, :], w[:, k, 0:AW], start=st, stop=end)
                        mm = pe.matmul(kv_bank[:, 0:QKV - AW], h[par][:, k, :], w[:, k, AW:QKV], start=st, stop=end)
                mm.then_inc(qkv_done, 1)

            def prob_transpose(b, kv):
                pe.wait_ge(prob_divided, 2 * b + kv + 1)
                for s in range(1 if is_(b, 0) else 2):
                    f = 2 + kv if is_(b, 0) else 2 * kv + s
                    if kv == 1 and not is_(b, 0):
                        pe.wait_ge(probT_out, prob_fill(b, s))
                    elif is_(b, LAST):
                        pe.wait_ge(probT_out, prob_fill(b - 1, 2 + s))
                    else:
                        pe.wait_ge(qkT_lo_out, 2 * b + 4)
                    for h in range(GROUP):
                        mm = pe.transpose(TR[f % 2][:, h * P:(h + 1) * P],
                                          prob[:, GROUP * kv + h, s * P:(s + 1) * P], ident[:, :])
                    mm.then_inc(prob_turned, 1)

            def attention_output(b):
                pe.wait_ge(v_slot, b + 1)
                if is_(b, LAST):
                    pe.wait_ge(probT_out, prob_fill(b, 2))
                else:
                    pe.wait_ge(masked, 2 * b + 3)
                for kv in range(NKV):
                    slots = (0,) if is_(b, 0) else (0, 1)
                    pe.wait_ge(probT_out, prob_fill(b, 2 + kv if is_(b, 0) else 2 * kv + 1))
                    for s in slots:
                        mm = pe.matmul(output_bank(b)[HD * kv:HD * (kv + 1), :], v_win[:, s, kv * HD:(kv + 1) * HD],
                                       probT[:, 2 * kv + s, :], start=s == slots[0], stop=s == slots[-1])
                    mm.then_inc(pv_done, 1)

            def attn_sums(b, out):
                pe.wait_ge(attn_folded, b + 1)
                if is_(b, LAST):
                    pe.wait_ge(probT_out, prob_fill(b, 3))
                else:
                    pe.wait_ge(masked, 2 * b + 4)
                pe.matmul(out, attn_sqf[:, :], ones[:, :], start=True, stop=True).then_inc(attn_sums_done, 1)

            def qk_transpose(t):
                pe.wait_ge(qk_normed, 4 * t + 4)
                for i, tiles in enumerate((range(GROUP), (GROUP,))):
                    if is_(t, 0):
                        pe.wait_ge(coef_out, i + 1)
                    elif is_(t, LAST):
                        pe.wait_ge(probT_out, prob_fill(t - 2, 2 + i))
                    else:
                        pe.wait_ge(h_lo, 2 * t + 3 + i)
                    for n, tile in enumerate(tiles):
                        mm = pe.transpose(qk_banks(t)[i][:, n * P:(n + 1) * P], qn[:, tile, :], ident[:, :])
                    mm.then_inc(qk_turned, 1)

            def scores(b, kv):
                n = P if is_(b, 0) else 2 * P
                pe.wait_ge(qkT_lo_out, 2 * b + 2)
                if not is_(b, 0):
                    pe.wait_ge(masked, 2 * b - 1 + kv)
                elif kv == 1:
                    pe.wait_ge(qk_normed, 2)
                    pe.wait_ge(v_read, 1)
                if from_(b, 2):
                    pe.wait_ge((attnT_out, attn_sum_out)[kv], b - 1)
                rows_ = slice(HD * kv, HD * (kv + 1))
                for h in range(GROUP):
                    dst = A[2 * kv + h // 2][:, (h % 2) * 2 * P:(h % 2) * 2 * P + n]
                    for m, (q, k) in enumerate(((qT_hi, kT_hi), (qT_hi, kT_lo), (qT_lo, kT_hi))):
                        mm = pe.matmul(dst, q[rows_, h, :], k[rows_, 0:n // P, :].rearrange("p s t -> p (s t)"),
                                       start=m == 0, stop=m == 2)
                mm.then_inc(scores_done, 1)

            def step(t, par):
                qkv(t, par)
                if from_(t, 3):
                    attn_sums(t - 3, A[3][:, 0:1])
                for kv in range(NKV):
                    prob_transpose(t - 2, kv)
                    scores(t - 1, kv)
                if not is_(t, LAST):
                    x_transpose(t + 1, 1 - par)
                attention_output(t - 2)
                qk_transpose(t)

            pe.wait_ge(const_set, 7)
            keep_warm()
            x_transpose(0, 0)
            keep_warm()
            qkv(0, 0)
            x_transpose(1, 1)
            pe.wait_ge(const_in, 8 * 16)
            for i in range(2):
                pe.transpose(A[i][:, 0:P], rows[:, i * P:(i + 1) * P], ident[:, :]).then_inc(coef_turned, 1)
            qkv(1, 1)
            qk_transpose(0)
            x_transpose(2, 0)
            for kv in range(NKV):
                scores(0, kv)
            qk_transpose(1)
            step(2, 0)
            with pe.Fori(0, 2) as tt:
                step(2 * tt + 3, 1)
                step(2 * tt + 4, 0)
            step(LAST, 1)

            def unit(banks, hi, lo, halves=range(NH)):
                for k in range(KT):
                    for w, h, st in ((hi, hT_hi, k == 0), (hi, hT_lo, False), (lo, hT_hi, False)):
                        for hf in halves:
                            mm = pe.matmul(banks[hf][:, :], w[:, k, :], h[:, k, hf * HALF:(hf + 1) * HALF],
                                           start=st, stop=k == KT - 1 and w is lo)
                return mm

            def conv_unit(j, s, first):
                if first:
                    pe.wait_ge(stage_lo, unit0_load(s).n + 1)
                else:
                    pe.wait_ge(stage_lo, unit_load(j - 1, s).n + 1)
                    if is_(j, 1) and s > 0:
                        pe.wait_ge((y_chain, cu_out)[s - 1], (5, NH)[s - 1])
                    else:
                        pe.wait_ge((c_out, cu_out, y_chain)[s], (NH, NH, 5)[s] * j)
                hi, lo = (b0_hi, b0_lo) if first and s == 2 else (wc_hi[s], wc_lo[s])
                unit((Q, A[2:4], A[0:2])[s] if first else (Q, A[0:2], A[2:4])[s], hi, lo).then_inc(unit_done, 1)

            def conv_sums():
                pe.wait_ge(ysum_out, NC - 1)
                pe.wait_ge(attnT_out, NT)
                for t in range(NT):
                    mm = pe.matmul(TR[0][:, t:t + 1], ysum[:, t * P:(t + 1) * P], ones[:, :], start=True, stop=True)
                mm.then_inc(css_done, 1)

            pe.wait_ge(h_kept, 32 * NT)
            pe.wait_ge(qk_normed, 4 * NT - 2)
            pe.wait_ge(v_read, NT)
            conv_unit(0, 0, True)
            attn_sums(LAST - 2, A[3][:, 0:1])
            for kv in range(NKV):
                prob_transpose(LAST - 1, kv)
                scores(LAST, kv)
            attention_output(LAST - 1)
            pe.wait_ge(masked, 2 * NT)
            conv_unit(0, 1, True)
            attn_sums(LAST - 1, A[1][:, 0:1])
            for kv in range(NKV):
                prob_transpose(LAST, kv)
            attention_output(LAST)
            pe.wait_ge(attnT_out, LAST)
            pe.wait_ge(attn_sum_out, LAST)
            conv_unit(0, 2, True)
            attn_sums(LAST, TR[1][:, 0:1])

            def conv_iteration(j):
                for s in range(3):
                    conv_unit(j, s, False)

            conv_iteration(1)
            with pe.Fori(2, NC) as j:
                conv_iteration(j)

            def project(t, par, part):
                if not is_(t, 0):
                    pe.wait_ge(X_added, 4 * t - 2 + 2 * part)
                elif part == 0:
                    pe.wait_ge(cu_out, NH * NC)
                else:
                    pe.wait_ge(y_chain, 5 * NC)
                banks = A[2 * part:2 * part + 2]
                for k in range(4 * part, 4 * part + 4):
                    for m, w, st in ((mix_hi, wo_hi, k % 4 == 0), (mix_hi, wo_lo, False), (mix_lo, wo_hi, False)):
                        for n in range(2):
                            mm = pe.matmul(banks[n][:, :], m[par][:, k, :], w[:, k, n * HALF:(n + 1) * HALF],
                                           start=st, stop=k % 4 == 3 and m is mix_lo)
                mm.then_inc(proj_done, 1)

            def h_transpose(t):
                pe.wait_ge(h_normed, t + 1)
                for i in range(2):
                    if is_(t, 0):
                        pe.wait_ge((css_sum, attn_sum_out)[i], (1, NT)[i])
                    else:
                        pe.wait_ge(h2_lo, 2 * t - 1 + i)
                    for k in range(4):
                        mm = pe.transpose(TR[i][:, k * P:(k + 1) * P], xn[:, (4 * i + k) * P:(4 * i + k + 1) * P],
                                          ident[:, :])
                    mm.then_inc(h_turned, 1)

            def d_step(t, par):
                pe.wait_ge(mix_lo_out, 1 if is_(t, 0) else t + 2)
                project(t, par, 0)
                if is_(t, 0):
                    conv_sums()
                    pe.wait_ge(mix_lo_out, 2)
                else:
                    h_transpose(t - 1)
                project(t, par, 1)

            pe.wait_ge(stage_lo, N_F0)
            d_step(0, 0)
            d_step(1, 1)
            d_step(2, 0)
            with pe.Fori(0, 2) as tt:
                d_step(2 * tt + 3, 1)
                d_step(2 * tt + 4, 0)
            d_step(LAST, 1)

            def up_unit(i, s):
                if is_(i, 0):
                    pe.wait_ge(stage_lo, up0_load(s).n + 1)
                else:
                    pe.wait_ge(stage_lo, up_load(i - 1, s).n + 1)
                pe.wait_ge(z_out, 8 * i + 2 * s - 2)
                unit((Q, A[0:2])[s % 2], wu_hi[s], wu_lo[s]).then_inc(up_done, 1)

            def up_units(i):
                for s in range(4):
                    up_unit(i, s)

            def down(i):
                ring = (TR[0], TR[1], A[2], A[3])
                a_hi, a_lo, w_hi, w_lo = down_operands(i)
                pe.wait_ge(act_lo_out, 2 * i + 2)
                pe.wait_ge(stage_lo, down_load(i, 1).n + 1)
                for g in range(2 * NT):
                    t, n = g // 2, g % 2
                    if not (is_(i, 0) and g < 4):
                        pe.wait_ge(down_added, 2 * NT * i + g - 3)
                    for k in range(2):
                        for m, (a, w) in enumerate(((a_hi, w_hi), (a_hi, w_lo), (a_lo, w_hi))):
                            mm = pe.matmul(ring[g % 4][:, :], a[k][:, t * P:(t + 1) * P],
                                           w[k][:, n * HALF:(n + 1) * HALF],
                                           start=k == 0 and m == 0, stop=k == 1 and m == 2)
                    mm.then_inc(down_filled, 1)

            pe.wait_ge(h2_lo, NT)
            pe.wait_ge(c_out, NH * NC)
            pe.wait_ge(X_added, 4 * NT - 2)
            for s in range(2):
                pe.wait_ge(stage_lo, up0_load(s).n + 1)
                unit((Q, A[0:2])[s], wu_hi[s], wu_lo[s], (0,))
                if s == 0:
                    h_transpose(LAST)
            pe.wait_ge(h2_lo, 2 * NT)
            for s in range(2):
                unit((Q, A[0:2])[s], wu_hi[s], wu_lo[s], (1,)).then_inc(up_done, 1)
            for s in range(2, 4):
                up_unit(0, s)
            pe.wait_ge(X_added, 4 * NT)
            up_units(1)
            down(0)
            with pe.Fori(2, NG - 1) as i:
                up_units(i)
                down(i - 1)
            up_units(NG - 1)
            down(NG - 2)
            down(NG - 1)

        @block.vector
        def _(dve):
            def x_norm(t, par):
                dve.wait_ge(x_rms, 2 * t + 2)
                dve.scalar_tensor_tensor(xin[par][:, :], xin[par][:, :], x_r[:, par:par + 1], gain[:, :],
                                         ALU.mult, ALU.mult).then_inc(x_normed, 1)

            def h_split_lo(t, par):
                for i in range(2):
                    dve.wait_ge(h_hi, 2 * t + i + 1)
                    dve.tensor_tensor(hb_lo[par][:, 4 * i:4 * i + 4, :],
                                      TR[i][:, :].rearrange("p (k t) -> p k t", t=P),
                                      hb_hi[par][:, 4 * i:4 * i + 4, :].bitcast(FP32), ALU.subtract).then_inc(h_lo, 1)

            def head_sums(t):
                dve.wait_ge(qk_sq, 2 * t + 2)
                dve.tensor_reduce(qk_ss[:, :], qk_sqr[:, :, :], AX.X, ALU.add).then_inc(qk_sum, 1)

            qn_heads = (qn[:, 0:GROUP, :].rearrange("p i (g d) -> p g i d", d=HD),
                        qn[:, GROUP, :].rearrange("p (g d) -> p g d", d=HD))

            def qk_norm(t):
                dve.wait_ge(qk_rms, 2 * t + 2)
                dve.wait_ge(qk_sq, 2 * t + 2)
                dve.wait_ge(v_read, t + 1)
                if not is_(t, 0):
                    dve.wait_ge(qk_turned, 2 * t)
                q_r = qk_r[:, 0:NQ].rearrange("p (g i) -> p g i", i=GROUP)
                q_bank, kv_bank = qkv_banks(t)
                dve.tensor_tensor(qn_heads[0], q_bank[:, :].rearrange("p (g i d) -> p g i d", i=GROUP, d=HD),
                                  q_r.unsqueeze(3).to_broadcast([P, NKV, GROUP, HD]), ALU.mult).then_inc(qk_normed, 1)
                dve.tensor_tensor(qn_heads[1], kv_bank[:, 0:NKV * HD].rearrange("p (h d) -> p h d", d=HD),
                                  qk_r[:, NQ:].unsqueeze(2).to_broadcast([P, NKV, HD]), ALU.mult).then_inc(qk_normed, 1)
                for n, (lo, hi) in enumerate(((0, GROUP), (GROUP, GROUP + 1))):
                    dve.wait_ge(qk_normed, 4 * t + n + 1)
                    tile = qn[:, lo:hi, :].rearrange("p i (g d) -> p (i g) d", d=HD)
                    dve.tensor_tensor(tile, tile, qk_gain[:, n:n + 1, :].to_broadcast([P, 2 * (hi - lo), HD]),
                                      ALU.mult).then_inc(qk_normed, 1)

            def qkT_lo(t, par):
                for i, (lo, hi, width) in enumerate(((qT_lo[:, :, :], qT_hi[:, :, :], AW),
                                                     (kT_lo[:, par, :], kT_hi[:, par, :], P))):
                    dve.wait_ge(qkT_hi_out, 2 * t + i + 1)
                    src = qk_banks(t)[i][:, 0:width]
                    dve.tensor_tensor(lo, src.rearrange("p (h t) -> p h t", t=P) if i == 0 else src,
                                      hi.bitcast(FP32), ALU.subtract).then_inc(qkT_lo_out, 1)

            def prob_divide(b, g, keys):
                cols = slice(4 * g, 4 * g + 4)
                dve.wait_ge(exps, 2 * b + g + 1)
                dve.tensor_tensor(dsum[:, cols], den[:, cols], es[:, cols], ALU.add).then_inc(denom, 1)
                dve.wait_ge(denom, 4 * b + 2 * g + 1)
                dve.reciprocal(rden[:, cols], dsum[:, cols]).then_inc(denom, 1)
                dve.wait_ge(denom, 4 * b + 2 * g + 2)
                dve.tensor_tensor(prob[:, cols, 0:keys], prob[:, cols, 0:keys],
                                  rden[:, cols].unsqueeze(2).to_broadcast([P, GROUP, keys]),
                                  ALU.mult).then_inc(prob_divided, 1)

            def copy_attn_sums(b, src):
                dve.wait_ge(attn_sums_done, b + 1)
                dve.tensor_copy(attn_ss[:, ds(b, 1)], src).then_inc(attn_sum_out, 1)

            def fold_attn_squares(b):
                dve.wait_ge(attn_sq, b + 1)
                if not is_(b, 0):
                    dve.wait_ge(attn_sums_done, b)
                dve.tensor_reduce(attn_sqf[:, :], attn_sqr[:, :, :].rearrange("p h t -> p t h"), AX.X,
                                  ALU.add).then_inc(attn_folded, 1)

            def mask_max(b, g, par, keys):
                window = mask[:, par * P:par * P + keys]
                cols = slice(4 * g, 4 * g + 4)
                dve.wait_ge(scores_done, 2 * b + g + 1)
                if not is_(b, 0):
                    dve.wait_ge(exps, 2 * b + g - 1)
                dve.sem_inc(scores_seen, 1)
                for h in range(4 * g, 4 * g + 4):
                    mm = dve.tensor_tensor_reduce(out=prob[:, h, 0:keys],
                                                  in0=A[h // 2][:, (h % 2) * 2 * P:(h % 2) * 2 * P + keys],
                                                  in1=window, scale=1.0, scalar=-3e38, op0=ALU.add, op1=ALU.max,
                                                  accum_out=mx[:, h:h + 1])
                mm.then_inc(masked, 1)
                dve.wait_ge(masked, 2 * b + g + 1)
                dve.tensor_tensor(top_score[:, cols], mx[:, cols], sink[:, cols], ALU.max).then_inc(shift, 1)
                dve.wait_ge(shift, 6 * b + 3 * g + 1)
                dve.tensor_scalar(negm[:, cols], top_score[:, cols], -1.0, None, ALU.mult).then_inc(shift, 1)
                dve.tensor_tensor(sd[:, cols], sink[:, cols], top_score[:, cols], ALU.subtract).then_inc(shift, 1)

            def step(t, par):
                if is_(t, LAST):
                    split_lo(dve, unit0_load(0), wc_hi[0][:, :, :], wc_lo[0][:, :, :])
                else:
                    x_norm(t + 1, 1 - par)
                if from_(t, 3):
                    copy_attn_sums(t - 3, A[3][:, 0:1])
                head_sums(t)
                mask_max(t - 1, 0, 1 - par, 2 * P)
                qk_norm(t)
                if is_(t, LAST):
                    split_lo(dve, unit0_load(1), wc_hi[1][:, :, :], wc_lo[1][:, :, :])
                else:
                    h_split_lo(t + 1, 1 - par)
                mask_max(t - 1, 1, 1 - par, 2 * P)
                for g in range(2):
                    prob_divide(t - 1, g, 2 * P)
                qkT_lo(t, par)
                fold_attn_squares(t - 2)

            dve.wait_ge(gain_in, 16)
            x_norm(0, 0)
            h_split_lo(0, 0)
            def wq_split_lo(k):
                dve.wait_ge(wq_in[k // 2], 16)
                dve.wait_ge(wq_hi_out, k + 1)
                dve.tensor_tensor(wq_lo[:, k, :], wq_raw[:, k, :], wq_hi[:, k, :].bitcast(FP32),
                                  ALU.subtract).then_inc(wq_lo_out, 1)

            for k in range(KT):
                wq_split_lo(k)
            x_norm(1, 1)
            h_split_lo(1, 1)
            dve.wait_ge(const_in, 8 * 16)
            dve.tensor_scalar(qk_gain[:, 0, :], qk_gain[:, 0, :], float(HD) ** -0.5, None, ALU.mult).then_inc(coef_set, 1)
            for i in range(2):
                dve.wait_ge(coef_turned, i + 1)
                dve.tensor_copy(coef[:, i * P:(i + 1) * P], A[i][:, 0:P]).then_inc(coef_out, 1)
            dve.wait_ge(coef_set, 1)
            head_sums(0)
            qk_norm(0)
            x_norm(2, 0)
            head_sums(1)
            qkT_lo(0, 0)
            h_split_lo(2, 0)
            dve.wait_ge(const_set, 10)
            mask_max(0, 0, 0, P)
            qk_norm(1)
            mask_max(0, 1, 0, P)
            qkT_lo(1, 1)
            for g in range(2):
                prob_divide(0, g, P)
            step(2, 0)
            with dve.Fori(0, 2) as tt:
                step(2 * tt + 3, 1)
                step(2 * tt + 4, 0)
            step(LAST, 1)
            split_lo(dve, unit0_load(2), b0_hi[:, :, :], b0_lo[:, :, :])
            copy_attn_sums(LAST - 2, A[3][:, 0:1])
            for g in range(2):
                mask_max(LAST, g, 1, 2 * P)
            fold_attn_squares(LAST - 1)
            for g in range(2):
                prob_divide(LAST, g, 2 * P)
            copy_attn_sums(LAST - 1, A[1][:, 0:1])
            fold_attn_squares(LAST)

            def causal_conv(acc, src, taps, chain, count, before=(), between=None):
                for sem_, value in before:
                    dve.wait_ge(sem_, value)
                dve.tensor_scalar(acc[:, :], src[:, 2:2 + SEQ], coef[:, taps[2]], None, ALU.mult).then_inc(chain, 1)
                for n in (1, 2):
                    if between:
                        between(n - 1)
                    dve.wait_ge(chain, count + n)
                    dve.scalar_tensor_tensor(acc[:, :], src[:, 2 - n:2 - n + SEQ], coef[:, taps[2 - n]], acc[:, :],
                                             ALU.mult, ALU.add).then_inc(chain, 1)

            def conv_iteration(j, last):
                if not last:
                    split_lo(dve, unit_load(j, 0), wc_hi[0][:, :, :], wc_lo[0][:, :, :])
                u_banks, b_banks = (A[2:4], A[0:2]) if is_(j, 0) else (A[0:2], A[2:4])
                dve.wait_ge(unit_done, 3 * j + 2)
                if not is_(j, 0):
                    dve.wait_ge(y_chain, 5 * j)
                for hf in range(NH):
                    dve.wait_ge(c_out, NH * j + hf + 1)
                    dve.tensor_tensor(cu[:, TAPS - 1 + hf * HALF:TAPS - 1 + (hf + 1) * HALF], u_banks[hf][:, :],
                                      c_sb[:, hf * HALF:(hf + 1) * HALF], ALU.mult).then_inc(cu_out, 1)
                dve.wait_ge(cu_out, NH * j + NH)
                before = () if is_(j, 0) else ((y_stored, 16 * j), (ysq_out, j))
                causal_conv(y, cu, [mix_tap(n, j) for n in range(TAPS)], y_chain, 5 * j, before)
                if not last:
                    split_lo(dve, unit_load(j, 1), wc_hi[1][:, :, :], wc_lo[1][:, :, :])
                else:
                    dve.wait_ge(mix_hi_out, 1)
                    dve.tensor_tensor(mix_lo[0][:, 0:KT - 1, :], mixb[:, 0:KT - 1, :],
                                      mix_hi[0][:, 0:KT - 1, :].bitcast(FP32), ALU.subtract).then_inc(mix_lo_out, 1)
                dve.wait_ge(unit_done, 3 * j + 3)
                dve.wait_ge(y_chain, 5 * j + 3)
                for hf in range(NH):
                    half = slice(hf * HALF, (hf + 1) * HALF)
                    dve.tensor_tensor(y[:, half], b_banks[hf][:, :], y[:, half], ALU.mult).then_inc(y_chain, 1)
                if not last:
                    split_lo(dve, unit_load(j, 2), wc_hi[2][:, :, :], wc_lo[2][:, :, :])
                    for m in range(wo_tiles(j)):
                        k = WO_STEP * j + m
                        split_lo(dve, wo_load(j, m), wo_hi[:, ds(k, 1), :].rearrange("p a e -> p (a e)"),
                                 wo_lo[:, ds(k, 1), :].rearrange("p a e -> p (a e)"), coef[:, ds(OUT0 + k, 1)])

            def add_squares(j):
                dve.wait_ge(ysq_out, j + 1)
                if not is_(j, 1):
                    dve.wait_ge(ysum_out, j - 1)
                dve.tensor_tensor(ysum[:, :], ysq[:, :], ysum[:, :], ALU.add).then_inc(ysum_out, 1)

            dve.wait_ge(mix_stored, 32 * NT)
            dve.memset(cu[:, 0:TAPS - 1], 0.0).then_inc(cu_pad, 1)
            dve.wait_ge(cu_pad, 1)
            conv_iteration(0, False)
            copy_attn_sums(LAST, TR[1][:, 0:1])
            conv_iteration(1, False)
            add_squares(1)
            conv_iteration(2, False)
            add_squares(2)
            conv_iteration(3, True)

            def mix_split_lo(t, par):
                dve.wait_ge(mix_hi_out, t + 2)
                dve.tensor_tensor(mix_lo[par][:, :, :], mixb[:, :, :], mix_hi[par][:, :, :].bitcast(FP32),
                                  ALU.subtract).then_inc(mix_lo_out, 1)

            def add_part(t, part):
                dve.wait_ge(proj_done, 2 * t + part + 1)
                r = (attn_r, conv_r)[part]
                if part == 0:
                    dve.wait_ge(X_in, 16 * 4)
                    if not is_(t, 0):
                        dve.wait_ge(X_late_in, 16 * 4)
                    dve.wait_ge(attn_rms, 3)
                else:
                    dve.wait_ge(conv_rms, 3)
                    dve.wait_ge(X_added, 4 * t + 2)
                for n in range(2):
                    x_half = X[:, ds(t, 1), n * HALF:(n + 1) * HALF].rearrange("p a d -> p (a d)")
                    dve.scalar_tensor_tensor(x_half, A[2 * part + n][:, :], r[:, ds(t, 1)], x_half,
                                             ALU.mult, ALU.add).then_inc(X_added, 1)

            def h_norm(t, par):
                dve.wait_ge(h_rms, 2 * t + 2)
                if not is_(t, 0):
                    dve.wait_ge(h_turned, 2 * t)
                dve.scalar_tensor_tensor(xn[:, :], X[:, ds(t, 1), :].rearrange("p a d -> p (a d)"),
                                         h_r[:, par:par + 1], gain[:, :], ALU.mult, ALU.mult).then_inc(h_normed, 1)

            def h2_split_lo(t):
                for i in range(2):
                    dve.wait_ge(h2_hi, 2 * t + i + 1)
                    dve.tensor_tensor(hT_lo[:, 4 * i:4 * i + 4, ds(P * t, P)],
                                      TR[i][:, :].rearrange("p (k t) -> p k t", t=P),
                                      hT_hi[:, 4 * i:4 * i + 4, ds(P * t, P)].bitcast(FP32),
                                      ALU.subtract).then_inc(h2_lo, 1)

            def d_step(t, par):
                h_norm(t - 1, 1 - par)
                if not is_(t, LAST):
                    mix_split_lo(t + 1, 1 - par)
                add_part(t, 0)
                h2_split_lo(t - 1)
                if is_(t, LAST):
                    for s in range(2):
                        split_lo(dve, up0_load(s), wu_hi[s][:, :, :], wu_lo[s][:, :, :])
                add_part(t, 1)

            dve.wait_ge(mix_hi_out, 2)
            dve.tensor_tensor(mix_lo[0][:, KT - 1, :], y[:, 0:P], mix_hi[0][:, KT - 1, :].bitcast(FP32),
                              ALU.subtract).then_inc(mix_lo_out, 1)
            dve.wait_ge(gain_in, 32)
            add_squares(NC - 1)
            dve.wait_ge(css_done, 1)
            dve.tensor_copy(conv_ss[:, :], TR[0][:, 0:NT]).then_inc(css_sum, 1)
            add_part(0, 0)
            mix_split_lo(1, 1)
            add_part(0, 1)
            d_step(1, 1)
            d_step(2, 0)
            with dve.Fori(0, 2) as tt:
                d_step(2 * tt + 3, 1)
                d_step(2 * tt + 4, 0)
            d_step(LAST, 1)
            h_norm(LAST, 1)
            h2_split_lo(LAST)
            for s in range(2, 4):
                split_lo(dve, up0_load(s), wu_hi[s][:, :, :], wu_lo[s][:, :, :])

            def act_split_lo(i, k):
                a_hi, a_lo, _, _ = down_operands(i)
                dve.wait_ge(act_hi_out, 2 * i + k + 1)
                dve.tensor_tensor(a_lo[k], gated[:, k, :], a_hi[k].bitcast(FP32), ALU.subtract).then_inc(act_lo_out, 1)

            def down_weights_lo(i, k):
                _, _, w_hi, w_lo = down_operands(i)
                split_lo(dve, down_load(i, k), w_hi[k], w_lo[k])

            def up_weights_lo(i, s):
                split_lo(dve, up_load(i, s), wu_hi[s][:, :, :], wu_lo[s][:, :, :])

            def add_down(i, g):
                ring = (TR[0], TR[1], A[2], A[3])
                t, n = g // 2, g % 2
                x_half = X[:, t, n * HALF:(n + 1) * HALF]
                dve.wait_ge(down_filled, 2 * NT * i + g + 1)
                dve.tensor_tensor(x_half, ring[g % 4][:, :], x_half, ALU.add).then_inc(down_added, 1)

            def convolve(i, s, first, between=None):
                dve.wait_ge(z_out, 8 * i + 2 * s + 2)
                before = () if first and s < 2 else ((gated_out, 2 * i + s // 2),)
                f = 2 * i + s // 2 + (s % 2) * NF
                causal_conv((acc_g, acc_u)[s % 2], z, [ffn_tap(n, f) for n in range(TAPS)], conv_chain,
                            12 * i + 3 * s, before, between)

            def gate(i, k, first):
                dve.wait_ge(silu_out, 2 * i + k + 1)
                dve.wait_ge(conv_chain, 12 * i + 6 * k + 6)
                if not first:
                    dve.wait_ge(act_lo_out, 2 * i)
                dve.tensor_tensor(gated[:, k, :], acc_g[:, :], acc_u[:, :], ALU.mult).then_inc(gated_out, 1)

            def ffn_iteration(i, first, last):
                def add(g):
                    if not first:
                        add_down(i - 1, g)

                convolve(i, 0, first)
                if not first:
                    for k in range(2):
                        act_split_lo(i - 1, k)
                    for k in range(2):
                        down_weights_lo(i - 1, k)
                convolve(i, 1, first)
                gate(i, 0, first)
                if not last:
                    up_weights_lo(i, 0)
                convolve(i, 2, first)
                if not last:
                    up_weights_lo(i, 1)
                convolve(i, 3, first, between=add)
                add(2)
                gate(i, 1, first)
                add(3)
                if last:
                    act_split_lo(i, 0)
                else:
                    up_weights_lo(i, 2)
                add(4)
                add(5)
                if last:
                    act_split_lo(i, 1)
                else:
                    up_weights_lo(i, 3)
                for g in range(6, 2 * NT):
                    add(g)
                    if last and g in (7, 9):
                        down_weights_lo(i, (g - 7) // 2)

            dve.wait_ge(h_turned, 2 * NT)
            dve.memset(z[:, 0:TAPS - 1], 0.0).then_inc(z_pad, 1)
            dve.wait_ge(z_pad, 1)
            ffn_iteration(0, True, False)
            ffn_iteration(1, False, False)
            with dve.Fori(2, NG - 1) as i:
                ffn_iteration(i, False, False)
            ffn_iteration(NG - 1, False, True)
            for g in range(2 * NT):
                add_down(NG - 1, g)


_INS = ["x", "attn_norm_w", "w_in", "q_norm_w", "k_norm_w", "sinks", "conv_mix_w", "attn_out_norm_w",
        "conv_out_norm_w", "w_out", "ffn_norm_w", "w_up", "ffn_conv_w", "w_down"]


def kernel(**inputs):
    import numpy as _np
    import concourse.bacc as _bacc
    from concourse import mybir as _mybir
    from concourse.bass_utils import run_bass_kernel_spmd as _run

    nc = _bacc.Bacc("TRN2", target_bir_lowering=False, num_devices=1)
    arrays, args = {}, []
    for name in _INS:
        a = _np.ascontiguousarray(inputs[name])
        arrays[f"in_{name}_dram"] = a
        args.append(nc.dram_tensor(f"in_{name}_dram", a.shape, _mybir.dt.from_np(a.dtype), kind="ExternalInput").ap())
    shape = tuple(inputs["x"].shape)
    args.append(nc.dram_tensor("out_0_dram", shape, _mybir.dt.float32, kind="ExternalOutput").ap())
    build_layer(nc, *args)
    r = _run(nc, [arrays], core_ids=[0])
    return r.results[0]["out_0_dram"]
```
